# Optimizing a Trainium2 kernel written in Bass

```python
import jax, jax.numpy as jnp
from jax import lax
import numpy as np

D_MODEL = 1024
BATCH = 1
SEQ = 256
DEPTH = 2

CHUNK = 64
Q_BLOCK = 128
N_A_LAYERS = DEPTH // 2
MLA_HEADS = 8
QK_NOPE = 128
QK_ROPE = 64
V_HEAD = 128
Q_LORA = 384
KV_LORA = 256
ROPE_BASE = 10000.0
SB_HEADS = 8
SB_HEAD = 128
D_FF = 2816
N_EXPERTS = 8
TOP_K = 2
D_FF_EXPERT = 2816
EPS = 1e-6

kernel_name = "yoco_mla_stickbreaking_moe_trunk"

def rms_norm(x, g):
    xf = x.astype(jnp.float32)
    y = xf * lax.rsqrt(jnp.mean(xf * xf, axis=-1, keepdims=True) + EPS)
    return (y * g.astype(jnp.float32)).astype(x.dtype)

def rope_cos_sin(positions):
    inv_freq = 1.0 / (ROPE_BASE ** (jnp.arange(0, QK_ROPE, 2, dtype=jnp.float32) / QK_ROPE))
    ang = positions.astype(jnp.float32)[..., None] * inv_freq
    return jnp.cos(ang), jnp.sin(ang)

def apply_rope(x, cos, sin):
    xf = x.astype(jnp.float32)
    x1, x2 = jnp.split(xf, 2, axis=-1)
    return jnp.concatenate([x1 * cos - x2 * sin, x1 * sin + x2 * cos], axis=-1).astype(x.dtype)

def swiglu(h, w_gate_up, w_down):
    g, u = jnp.split(h @ w_gate_up, 2, axis=-1)
    return (jax.nn.silu(g) * u) @ w_down

def mla(h, cos, sin, w_down, q_norm, w_uq, kv_norm, w_ukv, w_o):
    B, S, _ = h.shape
    c_q, c_kv, k_rope = jnp.split(h @ w_down, [Q_LORA, Q_LORA + KV_LORA], axis=-1)
    q = (rms_norm(c_q, q_norm) @ w_uq).reshape(B, S, MLA_HEADS, QK_NOPE + QK_ROPE)
    q_nope = q[..., :QK_NOPE]
    q_rope = apply_rope(q[..., QK_NOPE:], cos[:, :, None, :], sin[:, :, None, :])
    k_rope = apply_rope(k_rope, cos, sin)
    kv = (rms_norm(c_kv, kv_norm) @ w_ukv).reshape(B, S, MLA_HEADS, QK_NOPE + V_HEAD)
    k_nope, v = kv[..., :QK_NOPE], kv[..., QK_NOPE:]
    scale = (QK_NOPE + QK_ROPE) ** -0.5
    outs = []
    for start in range(0, S, Q_BLOCK):
        end = start + Q_BLOCK
        s = (jnp.einsum('bqhd,bkhd->bhqk', q_nope[:, start:end], k_nope[:, :end])
             + jnp.einsum('bqhr,bkr->bhqk', q_rope[:, start:end], k_rope[:, :end]))
        s = s.astype(jnp.float32) * scale
        q_chunk = (start + jnp.arange(Q_BLOCK)) // CHUNK
        k_chunk = jnp.arange(end) // CHUNK
        mask = k_chunk[None, :] <= q_chunk[:, None]
        p = jax.nn.softmax(jnp.where(mask, s, -jnp.inf), axis=-1).astype(v.dtype)
        outs.append(jnp.einsum('bhqk,bkhd->bqhd', p, v[:, :end]))
    o = jnp.concatenate(outs, axis=1).reshape(B, S, MLA_HEADS * V_HEAD)
    return o @ w_o

def stick_breaking(h, w_q, w_o, k, v):
    B, S, _ = h.shape
    q = (h @ w_q).reshape(B, S, SB_HEADS, SB_HEAD)
    scale = SB_HEAD ** -0.5
    outs = []
    for start in range(0, S, Q_BLOCK):
        end = start + Q_BLOCK
        z = jnp.einsum('bqhd,bkhd->bhqk', q[:, start:end], k[:, :end]).astype(jnp.float32) * scale
        t = start + jnp.arange(Q_BLOCK)
        s = jnp.arange(end)
        mask = s[None, :] < t[:, None]
        log_1m_beta = jnp.where(mask, jax.nn.log_sigmoid(-z), 0.0)
        between = lax.cumsum(log_1m_beta, axis=3, reverse=True) - log_1m_beta
        log_a = jnp.where(mask, jax.nn.log_sigmoid(z) + between, -jnp.inf)
        a = jnp.exp(log_a).astype(v.dtype)
        outs.append(jnp.einsum('bhqk,bkhd->bqhd', a, v[:, :end]))
    o = jnp.concatenate(outs, axis=1).reshape(B, S, SB_HEADS * SB_HEAD)
    return o @ w_o

def moe(h, router, w_gate_up, w_down):
    B, S, D = h.shape
    xt = h.reshape(B * S, D)
    probs = jax.nn.softmax((xt @ router).astype(jnp.float32), axis=-1)
    top_p, top_i = lax.top_k(probs, TOP_K)
    top_p = top_p / jnp.sum(top_p, axis=-1, keepdims=True)
    gates = jnp.sum(jax.nn.one_hot(top_i, N_EXPERTS, dtype=jnp.float32) * top_p[..., None], axis=1)
    gates = gates.astype(xt.dtype)
    y = jnp.zeros_like(xt)
    for e in range(N_EXPERTS):
        y = y + gates[:, e:e + 1] * swiglu(xt, w_gate_up[e], w_down[e])
    return y.reshape(B, S, D)

def setup_inputs(seed: int = 0) -> dict:
    key = jax.random.key(seed)
    keys = iter(jax.random.split(key, 64))
    f32 = jnp.float32

    def w(shape, fan_in):
        return jax.random.normal(next(keys), shape, f32) * (fan_in ** -0.5)

    def g(n):
        return 1.0 + 0.01 * jax.random.normal(next(keys), (n,), f32)

    d = {}
    d["x"] = jax.random.normal(next(keys), (BATCH, SEQ, D_MODEL), f32)
    offsets = jax.random.randint(next(keys), (BATCH, 1), 0, 4096, dtype=jnp.int32)
    d["positions"] = offsets + jnp.arange(SEQ, dtype=jnp.int32)[None, :]

    def add_mla(i):
        d[f"attn_norm_{i}"] = g(D_MODEL)
        d[f"mla_w_down_{i}"] = w((D_MODEL, Q_LORA + KV_LORA + QK_ROPE), D_MODEL)
        d[f"mla_q_norm_{i}"] = g(Q_LORA)
        d[f"mla_w_uq_{i}"] = w((Q_LORA, MLA_HEADS * (QK_NOPE + QK_ROPE)), Q_LORA)
        d[f"mla_kv_norm_{i}"] = g(KV_LORA)
        d[f"mla_w_ukv_{i}"] = w((KV_LORA, MLA_HEADS * (QK_NOPE + V_HEAD)), KV_LORA)
        d[f"mla_w_o_{i}"] = w((MLA_HEADS * V_HEAD, D_MODEL), MLA_HEADS * V_HEAD)

    def add_sb(i):
        d[f"attn_norm_{i}"] = g(D_MODEL)
        d[f"sb_w_q_{i}"] = w((D_MODEL, SB_HEADS * SB_HEAD), D_MODEL)
        d[f"sb_w_o_{i}"] = w((SB_HEADS * SB_HEAD, D_MODEL), SB_HEADS * SB_HEAD)

    def add_dense(i):
        d[f"ffn_norm_{i}"] = g(D_MODEL)
        d[f"ffn_w_gate_up_{i}"] = w((D_MODEL, 2 * D_FF), D_MODEL)
        d[f"ffn_w_down_{i}"] = w((D_FF, D_MODEL), D_FF)

    def add_moe(i):
        d[f"ffn_norm_{i}"] = g(D_MODEL)
        d[f"moe_router_{i}"] = w((D_MODEL, N_EXPERTS), D_MODEL)
        d[f"moe_w_gate_up_{i}"] = w((N_EXPERTS, D_MODEL, 2 * D_FF_EXPERT), D_MODEL)
        d[f"moe_w_down_{i}"] = w((N_EXPERTS, D_FF_EXPERT, D_MODEL), D_FF_EXPERT)

    add_mla(0); add_dense(0)
    add_mla(1); add_moe(1)
    d["kv_shared_norm"] = g(D_MODEL)
    d["kv_shared_w"] = w((D_MODEL, 2 * SB_HEADS * SB_HEAD), D_MODEL)
    add_sb(2); add_dense(2)
    add_sb(3); add_moe(3)
    d["final_norm"] = g(D_MODEL)
    return d

def reference(x, positions,
              attn_norm_0, mla_w_down_0, mla_q_norm_0, mla_w_uq_0, mla_kv_norm_0, mla_w_ukv_0, mla_w_o_0,
              ffn_norm_0, ffn_w_gate_up_0, ffn_w_down_0,
              attn_norm_1, mla_w_down_1, mla_q_norm_1, mla_w_uq_1, mla_kv_norm_1, mla_w_ukv_1, mla_w_o_1,
              ffn_norm_1, moe_router_1, moe_w_gate_up_1, moe_w_down_1,
              kv_shared_norm, kv_shared_w,
              attn_norm_2, sb_w_q_2, sb_w_o_2,
              ffn_norm_2, ffn_w_gate_up_2, ffn_w_down_2,
              attn_norm_3, sb_w_q_3, sb_w_o_3,
              ffn_norm_3, moe_router_3, moe_w_gate_up_3, moe_w_down_3,
              final_norm):
    B, S, _ = x.shape
    attn_norms = [attn_norm_0, attn_norm_1, attn_norm_2, attn_norm_3]
    ffn_norms = [ffn_norm_0, ffn_norm_1, ffn_norm_2, ffn_norm_3]
    mla_params = [
        (mla_w_down_0, mla_q_norm_0, mla_w_uq_0, mla_kv_norm_0, mla_w_ukv_0, mla_w_o_0),
        (mla_w_down_1, mla_q_norm_1, mla_w_uq_1, mla_kv_norm_1, mla_w_ukv_1, mla_w_o_1),
    ]
    sb_params = [(sb_w_q_2, sb_w_o_2), (sb_w_q_3, sb_w_o_3)]
    dense_params = [(ffn_w_gate_up_0, ffn_w_down_0), (ffn_w_gate_up_2, ffn_w_down_2)]
    moe_params = [(moe_router_1, moe_w_gate_up_1, moe_w_down_1),
                  (moe_router_3, moe_w_gate_up_3, moe_w_down_3)]

    cos, sin = rope_cos_sin(positions)
    h = x
    k_sh = v_sh = None
    for layer in range(DEPTH):
        if layer < N_A_LAYERS:
            h = h + mla(rms_norm(h, attn_norms[layer]), cos, sin, *mla_params[layer])
        else:
            if layer == N_A_LAYERS:
                kv = (rms_norm(h, kv_shared_norm) @ kv_shared_w).reshape(B, S, 2, SB_HEADS, SB_HEAD)
                k_sh, v_sh = kv[:, :, 0], kv[:, :, 1]
            h = h + stick_breaking(rms_norm(h, attn_norms[layer]), *sb_params[layer - N_A_LAYERS], k_sh, v_sh)
        f_in = rms_norm(h, ffn_norms[layer])
        if layer % 2 == 0:
            h = h + swiglu(f_in, *dense_params[layer // 2])
        else:
            h = h + moe(f_in, *moe_params[layer // 2])
    return rms_norm(h, final_norm)


_drawn_inputs = setup_inputs


def setup_inputs(seed=0):
    import zlib

    import numpy as np

    out = dict(_drawn_inputs(seed))
    spreads = {}
    factors = {'attn_norm_0': 3.372,
     'mla_q_norm_0': 8.0,
     'mla_kv_norm_0': 8.0,
     'ffn_norm_0': 3.881,
     'attn_norm_1': 8.0,
     'ffn_norm_1': 4.006,
     'kv_shared_norm': 7.728,
     'final_norm': 5.741}
    for name, (base, spread) in spreads.items():
        noise = np.random.default_rng([zlib.crc32(name.encode()), seed]).standard_normal(out[name].shape)
        drawn = base * np.exp(spread * noise) if base else spread * noise
        out[name] = __import__('jax').numpy.asarray(drawn.astype(out[name].dtype))
    for name, factor in factors.items():
        out[name] = (out[name] * factor).astype(out[name].dtype)
    return out
```

```python
import numpy as np
from contextlib import ExitStack

import concourse.bass as bass
from concourse import mybir

F32 = mybir.dt.float32
F32R = mybir.dt.float32r
I32 = mybir.dt.int32
ALU = mybir.AluOpType
ACT = mybir.ActivationFunctionType
AX = mybir.AxisListType.X

P = 128
SEQ, D = 256, 1024
TC = SEQ // P
KD = D // P
HEADS = 8
Q_LORA, KV_LORA, ROPE = 384, 256, 64
DOWN = Q_LORA + KV_LORA + ROPE
QH = P + ROPE
CC = (Q_LORA + KV_LORA) // P
FF = 2816
N_EXP = 8
CHUNK = 64
EPS = 1e-6
MLA_SCALE = float(QH) ** -0.5
SB_SCALE = float(P) ** -0.5
NEG = -1e30

RAW = 11
RING = 6
HALF = 1024
GW = 256
NG = FF // GW
FU = 3 * NG
FH = 2 * FU
FC = FF // P
H_DOWN, H_UQ, H_UKV, H_WO = 0, 8, 14, 18
H_FFN = 26
GA = 6
H_FFN_B = H_FFN + 6 * GA
H_SBK = H_FFN + FH
H_SBV, H_SBQ, H_SBO = H_SBK + 8, H_SBK + 16, H_SBK + 24
H_MOE = H_SBK + 32
U_MOE = H_MOE // 2
assert H_MOE % 2 == 0 and FU % RAW == 0 and FH % RING == 0
ITEMS = 12

G_ATTN0, G_Q, G_KV, G_FFN0, G_KVSH, G_ATTN1, G_FFN1, G_ALL = 0, 8, 11, 13, 21, 29, 37, 45


def half_width(h):
    return DOWN if h < H_UQ else 4 * QH if h < H_UKV else HALF


def build(nc, t, out):
    with ExitStack() as ctx:
        def sb(name, shape, dt=F32):
            return ctx.enter_context(nc.sbuf_tensor(name, shape, dt))

        def sem(name):
            return ctx.enter_context(nc.semaphore(name))

        raw = sb("raw", [P, RAW, 2 * HALF])
        whi = sb("whi", [P, RING, HALF], F32R)
        wlo = sb("wlo", [P, RING, HALF], F32R)
        h = sb("h", [P, TC, D])
        xhi = sb("xhi", [P, KD, SEQ], F32R)
        xlo = sb("xlo", [P, KD, SEQ], F32R)
        ident = sb("ident", [P, P])
        ones = sb("ones", [P, P])
        neg_ones = sb("neg_ones", [P, P])
        before = sb("before", [P, P])
        neg_from = sb("neg_from", [P, P])
        hide = sb("hide", [P, P])
        iota = sb("iota", [P, P])
        gcol = sb("gcol", [P, G_ALL])
        ss = sb("ss", [P, 5, TC])
        std = sb("std", [P, 5, TC])
        rstd = sb("rstd", [P, 5, TC])
        eps = sb("eps", [P, 1])
        one = sb("one", [P, 1])
        router = sb("router", [P, KD, N_EXP])
        router_hi = sb("router_hi", [P, KD, N_EXP], F32R)
        router_lo = sb("router_lo", [P, KD, N_EXP], F32R)
        pm_tab = sb("pm_tab", [P, ITEMS, 2, TC])
        g_tab = sb("g_tab", [P, ITEMS, TC])
        item_expert = sb("item_expert", [P, ITEMS], I32)
        n_items_i = sb("n_items_i", [P, 1], I32)
        pm = sb("pm", [P, 2, TC])
        gt = sb("gt", [P, TC])

        def over(*specs):
            with ExitStack() as e:
                return [e.enter_context(nc.sbuf_tensor(n, s, d)) for n, s, d in specs]

        kT, qT, v, qrT, krT, chi, clo = over(
            ("kT", [P, HEADS, SEQ], F32), ("qT", [P, HEADS, SEQ], F32), ("v", [P, TC, D], F32),
            ("qrT", [P, 4, SEQ], F32), ("krT", [P, SEQ], F32),
            ("chi", [P, CC, SEQ], F32R), ("clo", [P, CC, SEQ], F32R))
        xn, cn, _, rot, rt, kr, _, prob, probT = over(
            ("xn", [P, TC, D], F32), ("cn", [P, TC, Q_LORA + KV_LORA], F32), ("gap0", [P, 768], F32),
            ("rot", [P, TC, HEADS, ROPE], F32), ("rt", [P, 2, HEADS, ROPE // 2], F32),
            ("kr", [P, TC, 2 * ROPE], F32),
            ("gap1", [P, 5 * SEQ + 256], F32), ("prob", [P, 2, 384], F32), ("probT", [P, 2, 384], F32))
        _, ang, ang_k, cos, sin, invf, posi, posf, mx, nmx, rs, rr, css, cstd, crstd, grow, _ = over(
            ("gap2", [P, 6 * 1024 + 1280 + 2560], F32), ("ang", [P, TC, 32], F32), ("ang_k", [P, TC, 32], F32),
            ("cos", [P, TC, 32], F32), ("sin", [P, TC, 32], F32), ("invf", [P, 32], F32),
            ("posi", [P, TC], I32), ("posf", [P, TC], F32),
            ("mx", [P, HEADS, 2], F32), ("nmx", [P, HEADS, 2], F32), ("rs", [P, HEADS, 2], F32),
            ("rr", [P, HEADS, 2], F32), ("css", [P, 2, TC], F32), ("cstd", [P, 2, TC], F32),
            ("crstd", [P, 2, TC], F32), ("grow", [P, P], F32), ("half_mask", [P, 192], F32))
        half_mask = _
        hhi, hlo, xm, gu, sel, selT = over(
            ("hhi", [P, 2 * GA, SEQ], F32R), ("hlo", [P, 2 * GA, SEQ], F32R),
            ("xm", [P, TC, D], F32), ("gu", [P, 2, TC, GW], F32), ("sel", [P, TC, P], F32),
            ("selT", [P, SEQ], F32R))
        ehi = hhi[:, :, :].rearrange("p c t -> p (c t)").rearrange("p (c t) -> p c t", t=P)
        elo = hlo[:, :, :].rearrange("p c t -> p (c t)").rearrange("p (c t) -> p c t", t=P)
        skT, sqT, sv, xs = over(
            ("skT", [P, HEADS, SEQ], F32), ("sqT", [P, HEADS, SEQ], F32), ("sv", [P, TC, D], F32),
            ("xs", [P, TC, D], F32))
        _, sp, aT = over(("gap3", [P, 3 * 2048], F32), ("sp", [P, 4, 384], F32), ("aT", [P, 4, 384], F32))
        lg, pr, oh1, oh2, sc8, msk, gates, posn, ovf, csum, selr, prod, m1, nm1, m2, den, rank, eidx, \
            cnt, r3, tf = over(
                *[(f"rt_{n}", [P, TC, N_EXP], F32) for n in
                  ("lg", "pr", "oh1", "oh2", "sc8", "msk", "gates", "posn")],
                ("rt_ovf", [P, N_EXP], F32), ("rt_csum", [P, N_EXP], F32), ("rt_selr", [P, 3, N_EXP], F32),
                ("rt_prod", [P, 3, N_EXP], F32), ("rt_m1", [P, TC], F32), ("rt_nm1", [P, TC], F32),
                ("rt_m2", [P, TC], F32), ("rt_den", [P, TC], F32), ("rt_rank", [P, N_EXP], F32),
                ("rt_eidx", [P, N_EXP], F32), ("rt_cnt", [P, N_EXP], F32), ("rt_r3", [P, 3, 3], F32),
                ("rt_tf", [P, ITEMS], F32))
        yout, gbc = over(("yout", [P, TC, D], F32), ("gbc", [P, D], F32))

        ps = ctx.enter_context(nc.psum_tensor("ps", [P, 8, 512], F32))

        landed = [sem(f"landed{i}") for i in range(RAW)]
        hi_made = sem("hi_made")
        lo_made = sem("lo_made")
        used = sem("used")
        small_in = sem("small_in")
        pos_in = sem("pos_in")
        h_ready = [sem(f"h_ready{n}") for n in range(5)]
        consts = sem("consts")
        pool_step = sem("pool_step")
        dve_step = sem("dve_step")
        act_step = sem("act_step")
        NORMS = 5
        ss_ready = [sem(f"ss_ready{n}") for n in range(NORMS)]
        std_ready = [sem(f"std_ready{n}") for n in range(NORMS)]
        rstd_ready = [sem(f"rstd_ready{n}") for n in range(NORMS)]
        xn_ready = [sem(f"xn_ready{n}") for n in range(4)]
        TRS = 5
        x_tr = [sem(f"x_tr{n}") for n in range(TRS)]
        xhi_ready = [sem(f"xhi_ready{n}") for n in range(TRS)]
        xlo_ready = [sem(f"xlo_ready{n}") for n in range(TRS)]
        g_tr, g_ready = sem("g_tr"), sem("g_ready")
        ang_ready, rc_ready, sin_ready = sem("ang_ready"), sem("rc_ready"), sem("sin_ready")
        c_ss, c_std, c_rstd, cn_ready, kr_ready = (sem(n) for n in ("c_ss", "c_std", "c_rstd", "cn_ready", "kr_ready"))
        c_tr, chi_ready, clo_ready = sem("c_tr"), sem("chi_ready"), sem("clo_ready")
        qn_done, qT_ready, kn_done, kT_ready = sem("qn_done"), sem("qT_ready"), sem("kn_done"), sem("kT_ready")
        rot_ready, v_ready, rot_tr, qrT_ready = sem("rot_ready"), sem("v_ready"), sem("rot_tr"), sem("qrT_ready")
        s_done, max_done, exp_done, pn_ready = sem("s_done"), sem("max_done"), sem("exp_done"), sem("pn_ready")
        pt_done, probT_ready, o_done, o_hi, o_lo = (sem(n) for n in ("pt_done", "probT_ready", "o_done", "o_hi", "o_lo"))
        skT_ready, sv_ready, sqT_ready = sem("skT_ready"), sem("sv_ready"), sem("sqT_ready")
        z_done, ln_done, sp_ready, c_done, a_ready = (sem(n) for n in ("z_done", "ln_done", "sp_ready", "c_done", "a_ready"))
        so_done, so_hi, so_lo = sem("so_done"), sem("so_hi"), sem("so_lo")
        silu_done = [sem(f"silu_done{n}") for n in range(3)]
        gated = [sem(f"gated{n}") for n in range(3)]
        gu_tr = [sem(f"gu_tr{n}") for n in range(3)]
        h_hi = [sem(f"h_hi{n}") for n in range(3)]
        h_lo = [sem(f"h_lo{n}") for n in range(3)]
        router_ready, lg_done, sm_nmax, sm_exp = sem("router_ready"), sem("lg_done"), sem("sm_nmax"), sem("sm_exp")
        msk_ready, pos_done, items_ready = sem("msk_ready"), sem("pos_done"), sem("items_ready")
        pm_ready, sel_ready, gathered, xe_hi, xe_lo = (sem(n) for n in ("pm_ready", "sel_ready", "gathered", "xe_hi", "xe_lo"))
        sel_tr, selT_ready, y_hi, y_lo, scattered, gt_ready = (sem(n) for n in ("sel_tr", "selT_ready", "y_hi", "y_lo", "scattered", "gt_ready"))
        gbc_in, y_ready, stored = sem("gbc_in"), sem("y_ready"), sem("stored")

        block = ctx.enter_context(nc.Block())

        def raw_half(hh):
            return raw[:, (hh // 2) % RAW, (hh % 2) * HALF:(hh % 2) * HALF + half_width(hh)]

        def w_hi(hh):
            return whi[:, hh % RING, :]

        def w_lo(hh):
            return wlo[:, hh % RING, :]

        def bank_gu(x, c, par):
            return par if x == 2 else 2 * par + c

        def bank_tr(x, par):
            return 2 + par if x == 2 else 4 + par

        def bank_out(x, c, n):
            return 4 + n if x == 2 else (6 + n if c == 0 else n)

        def parity(x, j):
            return (j + 1) % 2 if x == 1 else j % 2

        FFN = [(GA, 2, H_FFN), (NG - GA, 2, H_FFN_B), (NG, 1, H_MOE)]

        @block.sync
        def _(sp_eng):
            def slot_free(u, i=0):
                if u >= RAW:
                    sp_eng.wait_ge(lo_made, i * FH + 2 * (u - RAW) + 2)

            def load(u, halves, i=0):
                slot_free(u, i)
                for dst, src in halves:
                    sp_eng.dma_start(dst, src).then_inc(landed[u % RAW], 16)

            def rows(u, w, r, width=HALF):
                return [(raw[:, u % RAW, n * HALF:n * HALF + width], w[r + n * P:r + (n + 1) * P, :]) for n in range(2)]

            def square(u0, w):
                for n in range(4):
                    load(u0 + n, rows(u0 + n, w, 256 * n))

            def swiglu_unit(u, x_unit, w_gu, w_dn, i=0):
                if x_unit < 2 * NG:
                    j, q = x_unit // 2, x_unit % 2
                    src = w_gu.rearrange("(k p) f -> p k f", p=P)[:, 4 * q:4 * q + 4, :]
                    dst = raw[:, u % RAW, :].rearrange("p (k f) -> p k f", k=4)
                    load(u, [(dst[:, :, g * GW:(g + 1) * GW], src[:, :, g * FF + j * GW:g * FF + (j + 1) * GW])
                             for g in range(2)], i)
                else:
                    load(u, rows(u, w_dn, (x_unit - 2 * NG) * 256), i)

            sp_eng.dma_start(h[:, :, :], t["x"].rearrange("a (c p) d -> p (a c) d", p=P)).then_inc(h_ready[0], 16)
            for u in range(4):
                load(u, rows(u, t["mla_w_down_0"], u * 256, DOWN))
            for k in range(3):
                u, w = H_UQ // 2 + k, t["mla_w_uq_0"][k * P:(k + 1) * P, :]
                load(u, [(raw[:, u, g * HALF:g * HALF + 4 * QH], w[:, g * 4 * QH:(g + 1) * 4 * QH]) for g in range(2)])
            for k in range(2):
                u, w = H_UKV // 2 + k, t["mla_w_ukv_0"][k * P:(k + 1) * P, :]
                load(u, [(raw[:, u, g * HALF:(g + 1) * HALF], w[:, g * HALF:(g + 1) * HALF]) for g in range(2)])
            square(H_WO // 2, t["mla_w_o_0"])
            order = list(range(2 * GA)) + [2 * NG + n for n in range(GA)] + \
                list(range(2 * GA, 2 * NG)) + [2 * NG + n for n in range(GA, NG)]
            for n, x_unit in enumerate(order):
                swiglu_unit(H_FFN // 2 + n, x_unit, t["ffn_w_gate_up_0"], t["ffn_w_down_0"])
            square(H_SBK // 2, t["kv_shared_w"][:, 0:D])
            square(H_SBV // 2, t["kv_shared_w"][:, D:2 * D])
            square(H_SBQ // 2, t["sb_w_q_2"])
            square(H_SBO // 2, t["sb_w_o_2"])

            def expert(e):
                return (t["moe_w_gate_up_1"][bass.ds(e, 1), :, :].rearrange("a k f -> (a k) f"),
                        t["moe_w_down_1"][bass.ds(e, 1), :, :].rearrange("a k f -> (a k) f"))

            def item_loads(i, now, following):
                for n in range(3, FU):
                    swiglu_unit(U_MOE + n, n, *now, i=i)
                for n in range(3):
                    swiglu_unit(U_MOE + FU + n, n, *following, i=i)

            first = (t["moe_w_gate_up_1"][0], t["moe_w_down_1"][0])
            for n in range(3):
                swiglu_unit(U_MOE + n, n, *first)
            with sp_eng.Fori(0, N_EXP - 1) as i:
                item_loads(i, expert(i), expert(i + 1))
            sp_eng.wait_ge(items_ready, 2)
            n_items = sp_eng.value_load(n_items_i[0:1, 0:1], min_val=N_EXP, max_val=ITEMS - 1)
            with sp_eng.Fori(N_EXP - 1, n_items) as i:
                e = sp_eng.value_load(item_expert[0:1, bass.ds(i, 1)], min_val=0, max_val=N_EXP - 1)
                e_next = sp_eng.value_load(item_expert[0:1, bass.ds(i + 1, 1)], min_val=0, max_val=N_EXP - 1)
                item_loads(i, expert(e), expert(e_next))
            for n in range(3):
                u = U_MOE + n
                sp_eng.wait_ge(landed[u % RAW], n_items * (32 * FU // RAW) + 32 * (u // RAW + 1))
            for c in range(TC):
                sp_eng.wait_ge(y_ready, c + 1)
                sp_eng.dma_start(out[0, c * P:(c + 1) * P, :], yout[:, c, :]).then_inc(stored, 16)
            sp_eng.wait_ge(stored, 16 * TC)

        @block.gpsimd
        def _(pool):
            n = [0]

            def step(ins):
                n[0] += 1
                ins.then_inc(pool_step, 1)
                pool.wait_ge(pool_step, n[0])

            inv = 1.0 / (10000.0 ** (np.arange(0, ROPE, 2, dtype=np.float64) / ROPE))
            for c in range(ROPE // 2):
                nc.gpsimd.memset(invf[:, c:c + 1], float(np.float32(inv[c])))
            nc.gpsimd.memset(eps[:, :], EPS)
            nc.gpsimd.memset(one[:, :], 1.0)
            nc.gpsimd.memset(ones[:, :], 1.0)
            nc.gpsimd.memset(neg_ones[:, :], -1.0)
            nc.gpsimd.memset(half_mask[0:1, 0:64], 1.0)
            nc.gpsimd.memset(half_mask[0:1, 64:128], 0.0)
            nc.gpsimd.memset(half_mask[0:1, 128:192], NEG)
            nc.gpsimd.memset(ident[:, :], 0.0)
            nc.gpsimd.memset(hide[:, :], 0.0)
            step(nc.gpsimd.memset(before[:, :], 0.0))
            nc.gpsimd.affine_select(out=ident[:, :], in_=ident[:, :], compare_op=ALU.not_equal, fill=1.0,
                                    base=0, pattern=[[-1, P]], channel_multiplier=1)
            nc.gpsimd.affine_select(out=before[:, :], in_=before[:, :], compare_op=ALU.is_ge, fill=1.0,
                                    base=0, pattern=[[-1, P]], channel_multiplier=1)
            nc.gpsimd.affine_select(out=hide[:, :], in_=hide[:, :], compare_op=ALU.is_gt, fill=NEG,
                                    base=0, pattern=[[1, P]], channel_multiplier=-1)
            nc.gpsimd.affine_select(out=neg_from[:, :], in_=neg_ones[:, :], compare_op=ALU.is_ge, fill=0.0,
                                    base=0, pattern=[[-1, P]], channel_multiplier=1)
            nc.gpsimd.iota(iota[:, :], [[1, P]], base=0, channel_multiplier=0,
                           allow_small_or_imprecise_dtypes=True).then_inc(consts, 1)

        @block.scalar
        def _(act):
            steps = [0]

            def step(ins):
                steps[0] += 1
                ins.then_inc(act_step, 1)
                act.wait_ge(act_step, steps[0])

            def copy(o, i, scale=1.0):
                return nc.scalar.activation(o, i, ACT.Copy, scale=scale)

            def split_high(hh, i=0):
                u = hh // 2
                act.wait_ge(landed[u % RAW], i * (32 * FU // RAW) + 32 * (u // RAW + 1))
                if hh >= RING:
                    act.wait_ge(used, i * FH + hh - RING + 1)
                copy(w_hi(hh)[:, 0:half_width(hh)], raw_half(hh)).then_inc(hi_made, 1)

            def norm_tokens(n, dst):
                nc.scalar.activation(dst[:, 0, :], h[:, 0, :], ACT.Square, accum_out=ss[:, n, 0:1]).then_inc(ss_ready[n], 1)
                act.wait_ge(ss_ready[n], 2)
                nc.scalar.activation(std[:, n, :], ss[:, n, :], ACT.Sqrt, scale=1.0 / D, bias=eps[:, 0:1]).then_inc(std_ready[n], 1)
                act.wait_ge(rstd_ready[n], 1)
                copy(dst[:, 1, :], h[:, 1, :], scale=rstd[:, n, 1:2]).then_inc(xn_ready[n], 1)

            def x_high(n, gain, bank0):
                for b in range(4):
                    act.wait_ge(x_tr[n], b + 1)
                    for k in (2 * b, 2 * b + 1):
                        copy(xhi[:, k, :], ps[:, bank0 + b, (k % 2) * SEQ:(k % 2 + 1) * SEQ],
                             scale=gcol[:, gain + k:gain + k + 1]).then_inc(xhi_ready[n], 1)

            row = 0
            for name, rows in (("attn_norm_0", 8), ("mla_q_norm_0", 3), ("mla_kv_norm_0", 2), ("ffn_norm_0", 8),
                               ("kv_shared_norm", 8), ("attn_norm_1", 8), ("ffn_norm_1", 8)):
                act.dma_start(grow[row:row + rows, :], t[name].rearrange("(k c) -> k c", c=P)).then_inc(small_in, 16)
                row += rows
            act.dma_start(posi[:, :], t["positions"].rearrange("a (c p) -> p (a c)", p=P),
                          allow_slow_non_contiguous=True).then_inc(pos_in, 16)
            act.dma_start(router[:, :, :], t["moe_router_1"].rearrange("(k p) e -> p k e", p=P)).then_inc(pos_in, 16)

            act.wait_ge(consts, 1)
            act.wait_ge(h_ready[0], 16)
            norm_tokens(0, xn)
            act.wait_ge(g_tr, 1)
            copy(gcol[:, :], ps[:, 7, 0:G_ALL]).then_inc(g_ready, 1)
            act.wait_ge(g_ready, 1)
            split_high(0)
            split_high(1)
            x_high(0, G_ATTN0, 0)
            for hh in range(2, 6):
                split_high(hh)
            act.wait_ge(ang_ready, 1)
            nc.scalar.activation(sin[:, :, :], ang[:, :, :], ACT.Sin).then_inc(sin_ready, 1)
            act.wait_ge(rc_ready, 1)
            nc.scalar.activation(cos[:, :, :], ang_k[:, :, :], ACT.Sin).then_inc(sin_ready, 1)
            act.wait_ge(pos_in, 32)
            copy(router_hi[:, :, :], router[:, :, :]).then_inc(router_ready, 1)
            for hh in range(6, 14):
                split_high(hh)

            act.wait_ge(used, H_UQ)
            for c in range(TC):
                nc.scalar.activation(cn[:, c, 0:Q_LORA], ps[:, 4 + 2 * c, 0:Q_LORA], ACT.Square,
                                     accum_out=css[:, 0, c:c + 1]).then_inc(c_ss, 1)
                nc.scalar.activation(cn[:, c, Q_LORA:], ps[:, 5 + 2 * c, 0:KV_LORA], ACT.Square,
                                     accum_out=css[:, 1, c:c + 1]).then_inc(c_ss, 1)
            act.wait_ge(c_ss, 4)
            nc.scalar.activation(cstd[:, 0, :], css[:, 0, :], ACT.Sqrt, scale=1.0 / Q_LORA, bias=eps[:, 0:1]).then_inc(c_std, 1)
            nc.scalar.activation(cstd[:, 1, :], css[:, 1, :], ACT.Sqrt, scale=1.0 / KV_LORA, bias=eps[:, 0:1]).then_inc(c_std, 1)
            for b in range(3):
                act.wait_ge(c_tr, b + 1)
                for j in (2 * b, 2 * b + 1):
                    src = ps[:, b, (j % 2) * SEQ:(j % 2 + 1) * SEQ]
                    if j < CC:
                        copy(chi[:, j, :], src, scale=gcol[:, G_Q + j:G_Q + j + 1]).then_inc(chi_ready, 1)
                    else:
                        copy(krT[:, :], src).then_inc(chi_ready, 1)
            for b in range(4):
                act.wait_ge(qn_done, b + 1)
                copy(qT[:, 2 * b:2 * b + 2, :].rearrange("p a s -> p (a s)"), ps[:, 4 + b, :]).then_inc(qT_ready, 1)
            for hh in range(14, 20):
                split_high(hh)
            for b in range(4):
                act.wait_ge(kn_done, b + 1)
                copy(kT[:, 2 * b:2 * b + 2, :].rearrange("p a s -> p (a s)"), ps[:, 4 + b, :]).then_inc(kT_ready, 1)
            for b in range(2):
                act.wait_ge(rot_tr, b + 1)
                copy(qrT[:, 2 * b:2 * b + 2, :].rearrange("p a s -> p (a s)"), ps[:, 4 + b, :]).then_inc(qrT_ready, 1)
            for hh in range(20, 24):
                split_high(hh)

            def mla_exp(hd):
                act.wait_ge(max_done, hd + 1)
                if hd >= 2:
                    act.wait_ge(pt_done, hd - 1)
                for c, (a, b) in enumerate(((0, 128), (128, 384))):
                    nc.scalar.activation(prob[:, hd % 2, a:b], ps[:, 6 + hd % 2, a:b], ACT.Exp, bias=nmx[:, hd, c:c + 1],
                                         scale=MLA_SCALE, accum_out=rs[:, hd, c:c + 1]).then_inc(exp_done, 1)

            mla_exp(0)
            for hd in range(HEADS):
                if hd + 1 < HEADS:
                    mla_exp(hd + 1)
                act.wait_ge(pt_done, hd + 1)
                if hd >= 2:
                    act.wait_ge(o_done, hd - 1)
                copy(probT[:, hd % 2, :], ps[:, hd % 2, 0:384]).then_inc(probT_ready, 1)
                act.wait_ge(o_done, hd + 1)
                copy(xhi[:, hd, :], ps[:, 2 + hd % 2, 0:SEQ]).then_inc(o_hi, 1)
            for hh in range(24, 32):
                split_high(hh)

            def ffn(x, i=0, at_group=None):
                n, nt, base = FFN[x]

                def silu(j):
                    act.wait_ge(used, i * FH + base + 4 * (j + 1))
                    for c in range(nt):
                        if j >= 2 and c == 0:
                            act.wait_ge(gu_tr[x], i * n + j - 1)
                        nc.scalar.activation(gu[:, j % 2, c, :], ps[:, bank_gu(x, c, parity(x, j)), 0:GW],
                                             ACT.Silu).then_inc(silu_done[x], 1)

                def high(j):
                    act.wait_ge(gu_tr[x], i * n + j + 1)
                    src = ps[:, bank_tr(x, j % 2), 0:2 * nt * P]
                    dst = ehi[:, 2 * j:2 * j + 2, :] if nt == 1 else hhi[:, 2 * j:2 * j + 2, :]
                    copy(dst.rearrange("p a s -> p (a s)"), src).then_inc(h_hi[x], 1)

                for j in range(n):
                    if j >= 1:
                        silu(j - 1)
                    if j >= 2:
                        high(j - 2)
                    for m in range(4):
                        split_high(base + RING + 4 * j + m, i)
                silu(n - 1)
                high(n - 2)
                for f in range(2 * n):
                    split_high(base + RING + 4 * n + f, i)
                    if f == 1:
                        high(n - 1)
                    if f == 17 and x == 2:
                        for b in range(2):
                            act.wait_ge(gathered, i * 2 + 2 + b + 1)
                            for k in range(4 * b, 4 * b + 4):
                                copy(xhi[:, k, 0:P], ps[:, 6 + b, (k % 4) * P:(k % 4 + 1) * P],
                                     scale=gcol[:, G_FFN1 + k:G_FFN1 + k + 1]).then_inc(xe_hi, 1)

            act.wait_ge(h_ready[1], 4)
            norm_tokens(1, xm)
            x_high(1, G_FFN0, 0)
            ffn(0)
            ffn(1)

            act.wait_ge(h_ready[2], 8)
            norm_tokens(2, xs)
            x_high(2, G_KVSH, 0)
            for m in range(8):
                split_high(H_SBK + RING + m)
            act.wait_ge(used, H_SBV)
            for b in range(4):
                copy(skT[:, 2 * b:2 * b + 2, :].rearrange("p a s -> p (a s)"), ps[:, 4 + b, :]).then_inc(skT_ready, 1)
            for m in range(8):
                split_high(H_SBV + RING + m)
            act.wait_ge(used, H_SBQ)
            x_high(3, G_ATTN1, 4)
            for m in range(8):
                split_high(H_SBQ + RING + m)
            act.wait_ge(used, H_SBO)
            for b in range(4):
                copy(sqT[:, 2 * b:2 * b + 2, :].rearrange("p a s -> p (a s)"), ps[:, b, :], scale=SB_SCALE).then_inc(sqT_ready, 1)

            def log_term(hd):
                act.wait_ge(z_done, hd + 1)
                if hd >= 4:
                    act.wait_ge(c_done, hd - 3)
                buf = sp[:, hd % 4, :]
                step(nc.scalar.activation(buf, ps[:, hd % 4, 0:384], ACT.Abs))
                step(nc.scalar.activation(buf, buf, ACT.Exp, scale=-1.0))
                nc.scalar.activation(buf, buf, ACT.Ln, bias=one[:, 0:1]).then_inc(ln_done, 1)

            def sb_high(hd):
                act.wait_ge(so_done, hd + 1)
                copy(xhi[:, hd, :], ps[:, 4 + hd % 4, 0:SEQ]).then_inc(so_hi, 1)

            log_term(0)
            log_term(1)
            for hd in range(HEADS):
                if hd + 2 < HEADS:
                    log_term(hd + 2)
                act.wait_ge(c_done, hd + 1)
                if hd >= 4:
                    act.wait_ge(so_done, hd - 3)
                nc.scalar.activation(aT[:, hd % 4, :], ps[:, hd % 4, 0:384], ACT.Exp).then_inc(a_ready, 1)
                if hd >= 1:
                    sb_high(hd - 1)
            sb_high(HEADS - 1)
            for m in range(8):
                split_high(H_SBO + RING + m)

            act.wait_ge(h_ready[3], 4)
            norm_tokens(3, xm)
            x_high(4, G_FFN1, 0)
            act.wait_ge(sm_nmax, 1)
            for c in range(TC):
                nc.scalar.activation(pr[:, c, :], lg[:, c, :], ACT.Exp, bias=nm1[:, c:c + 1],
                                     accum_out=den[:, c:c + 1]).then_inc(sm_exp, 1)
            act.wait_ge(items_ready, 2)
            n_items = act.value_load(n_items_i[0:1, 0:1], min_val=N_EXP, max_val=ITEMS - 1)
            for b in range(2):
                act.wait_ge(gathered, b + 1)
                for k in range(4 * b, 4 * b + 4):
                    copy(xhi[:, k, 0:P], ps[:, 6 + b, (k % 4) * P:(k % 4 + 1) * P],
                         scale=gcol[:, G_FFN1 + k:G_FFN1 + k + 1]).then_inc(xe_hi, 1)
            act.wait_ge(sel_tr, 1)
            copy(selT[:, :], ps[:, 6, 0:SEQ]).then_inc(selT_ready, 1)
            with act.Fori(0, n_items) as i:
                ffn(2, i)
                act.wait_ge(used, i * FH + H_MOE + FH)
                for n in range(2):
                    copy(xhi[:, 4 * n:4 * n + 4, P:SEQ], ps[:, 4 + n, :].rearrange("p (a s) -> p a s", a=4)).then_inc(y_hi, 1)
                act.wait_ge(sel_tr, i + 2)
                copy(selT[:, :], ps[:, 6, 0:SEQ]).then_inc(selT_ready, 1)

            act.wait_ge(h_ready[4], n_items * 4 + 4)
            act.dma_start(gbc[:, :], t["final_norm"].partition_broadcast(P)).then_inc(gbc_in, 16)
            nc.scalar.activation(yout[:, 0, :], h[:, 0, :], ACT.Square, accum_out=ss[:, 4, 0:1]).then_inc(ss_ready[4], 1)
            act.wait_ge(ss_ready[4], 2)
            nc.scalar.activation(std[:, 4, :], ss[:, 4, :], ACT.Sqrt, scale=1.0 / D, bias=eps[:, 0:1]).then_inc(std_ready[4], 1)

        @block.vector
        def _(dve):
            V = nc.vector
            steps = [0]

            def step(ins):
                steps[0] += 1
                ins.then_inc(dve_step, 1)
                dve.wait_ge(dve_step, steps[0])

            def split_low(hh, i=0):
                dve.wait_ge(hi_made, i * FH + hh + 1)
                w = half_width(hh)
                V.tensor_tensor(w_lo(hh)[:, 0:w], raw_half(hh), w_hi(hh)[:, 0:w].bitcast(F32), ALU.subtract).then_inc(lo_made, 1)

            def norm_tokens(n, dst):
                V.tensor_tensor_reduce(out=dst[:, 1, :], in0=h[:, 1, :], in1=h[:, 1, :], scale=1.0, scalar=0.0,
                                       op0=ALU.mult, op1=ALU.add, accum_out=ss[:, n, 1:2]).then_inc(ss_ready[n], 1)
                dve.wait_ge(std_ready[n], 1)
                V.reciprocal(rstd[:, n, :], std[:, n, :]).then_inc(rstd_ready[n], 1)
                dve.wait_ge(rstd_ready[n], 1)
                V.tensor_scalar(dst[:, 0, :], h[:, 0, :], rstd[:, n, 0:1], None, ALU.mult).then_inc(xn_ready[n], 1)

            def x_low(n, gain, bank0):
                for b in range(4):
                    dve.wait_ge(xhi_ready[n], 2 * b + 2)
                    for k in (2 * b, 2 * b + 1):
                        V.scalar_tensor_tensor(out=xlo[:, k, :], in0=ps[:, bank0 + b, (k % 2) * SEQ:(k % 2 + 1) * SEQ],
                                               scalar=gcol[:, gain + k:gain + k + 1], in1=xhi[:, k, :].bitcast(F32),
                                               op0=ALU.mult, op1=ALU.subtract).then_inc(xlo_ready[n], 1)

            dve.wait_ge(h_ready[0], 16)
            norm_tokens(0, xn)
            dve.wait_ge(pos_in, 32)
            dve.wait_ge(consts, 1)
            step(V.tensor_copy(posf[:, :], posi[:, :]))
            for c in range(TC):
                last = V.tensor_scalar(ang[:, c, :], invf[:, :], posf[:, c:c + 1], None, ALU.mult)
            step(last)
            PI, MAGIC = 3.1415925, 12582912.0
            C1 = float(np.float32(6.28125))
            C2 = float(np.float32(np.float32(2 * np.pi - C1).view(np.uint32) & np.uint32(0xFFFFF000)).astype(np.uint32).view(np.float32))
            C3 = float(np.float32(2 * np.pi - C1 - C2))
            step(V.tensor_scalar(ang_k[:, :, :], ang[:, :, :], 1.0 / (2 * np.pi), MAGIC, ALU.mult, ALU.add))
            step(V.tensor_scalar(ang_k[:, :, :], ang_k[:, :, :], MAGIC, None, ALU.subtract))
            for part in (C1, C2, C3):
                step(V.scalar_tensor_tensor(out=ang[:, :, :], in0=ang_k[:, :, :], scalar=-part, in1=ang[:, :, :],
                                            op0=ALU.mult, op1=ALU.add))
            step(V.tensor_scalar(ang_k[:, :, :], ang[:, :, :], PI, -2 * np.pi, ALU.is_gt, ALU.mult))
            step(V.tensor_tensor(ang[:, :, :], ang[:, :, :], ang_k[:, :, :], ALU.add))
            step(V.tensor_scalar(ang_k[:, :, :], ang[:, :, :], -PI, 2 * np.pi, ALU.is_lt, ALU.mult))
            step(V.tensor_tensor(ang[:, :, :], ang[:, :, :], ang_k[:, :, :], ALU.add))
            step(V.tensor_scalar(ang[:, :, :], ang[:, :, :], PI, -PI, ALU.min, ALU.max))
            step(V.tensor_scalar(ang_k[:, :, :], ang[:, :, :], np.pi / 2, None, ALU.add))
            V_m = rt[:, :, 0:1, :].rearrange("p a b c -> p a (b c)")
            step(V.tensor_scalar(V_m, ang_k[:, :, :], PI, -2 * np.pi, ALU.is_gt, ALU.mult))
            step(V.tensor_tensor(ang_k[:, :, :], ang_k[:, :, :], V_m, ALU.add))
            V.tensor_scalar(ang_k[:, :, :], ang_k[:, :, :], PI, -PI, ALU.min, ALU.max).then_inc(rc_ready, 1)
            dve.wait_ge(rc_ready, 1)
            V.tensor_copy(nmx[:, 0, 0:1], posf[:, 0:1]).then_inc(ang_ready, 1)
            split_low(0)
            split_low(1)
            dve.wait_ge(g_ready, 1)
            x_low(0, G_ATTN0, 0)
            for hh in range(2, 6):
                split_low(hh)
            dve.wait_ge(router_ready, 1)
            V.tensor_tensor(router_lo[:, :, :], router[:, :, :], router_hi[:, :, :].bitcast(F32), ALU.subtract).then_inc(router_ready, 1)
            for hh in range(6, 14):
                split_low(hh)

            dve.wait_ge(c_std, 2)
            V.reciprocal(crstd[:, :, :], cstd[:, :, :]).then_inc(c_rstd, 1)
            dve.wait_ge(c_rstd, 1)
            for c in range(TC):
                V.tensor_scalar(cn[:, c, 0:Q_LORA], ps[:, 4 + 2 * c, 0:Q_LORA], crstd[:, 0, c:c + 1], None, ALU.mult).then_inc(cn_ready, 1)
                V.tensor_scalar(cn[:, c, Q_LORA:], ps[:, 5 + 2 * c, 0:KV_LORA], crstd[:, 1, c:c + 1], None, ALU.mult).then_inc(cn_ready, 1)

            def rope(x1, x2, co, si, t1, t2, o1, o2):
                step(V.tensor_tensor(t1, x1, co, ALU.mult))
                step(V.tensor_tensor(t2, x2, si, ALU.mult))
                step(V.tensor_tensor(o1, t1, t2, ALU.subtract))
                step(V.tensor_tensor(t1, x1, si, ALU.mult))
                step(V.tensor_tensor(t2, x2, co, ALU.mult))
                step(V.tensor_tensor(o2, t1, t2, ALU.add))

            dve.wait_ge(sin_ready, 2)
            R2 = ROPE // 2
            for c in range(TC):
                x = ps[:, 5 + 2 * c, KV_LORA:KV_LORA + ROPE]
                rope(x[:, 0:R2], x[:, R2:ROPE], cos[:, c, :], sin[:, c, :], rt[:, 0, 0, :], rt[:, 1, 0, :],
                     kr[:, c, 0:R2], kr[:, c, R2:ROPE])
            V.tensor_copy(kr[:, :, ROPE:2 * ROPE], kr[:, :, 0:ROPE]).then_inc(kr_ready, 1)
            for b in range(3):
                dve.wait_ge(chi_ready, 2 * b + 2)
                for j in range(2 * b, min(2 * b + 2, CC)):
                    V.scalar_tensor_tensor(out=clo[:, j, :], in0=ps[:, b, (j % 2) * SEQ:(j % 2 + 1) * SEQ],
                                           scalar=gcol[:, G_Q + j:G_Q + j + 1], in1=chi[:, j, :].bitcast(F32),
                                           op0=ALU.mult, op1=ALU.subtract).then_inc(clo_ready, 1)
            dve.wait_ge(used, H_UKV)
            for c in range(TC):
                x = ps[:, c, :].rearrange("p (a r) -> p a r", r=ROPE)
                co = cos[:, c, :].unsqueeze(1).to_broadcast([P, HEADS, R2])
                si = sin[:, c, :].unsqueeze(1).to_broadcast([P, HEADS, R2])
                rope(x[:, :, 0:R2], x[:, :, R2:ROPE], co, si, rt[:, 0, :, :], rt[:, 1, :, :],
                     rot[:, c, :, 0:R2], rot[:, c, :, R2:ROPE])
            V.tensor_copy(nmx[:, 0, 0:1], posf[:, 0:1]).then_inc(rot_ready, 1)
            for hh in range(14, 20):
                split_low(hh)
            dve.wait_ge(used, H_WO)
            dve.wait_ge(rot_tr, 2)
            for c in range(TC):
                for n in range(2):
                    V.tensor_copy(v[:, c, n * 512:(n + 1) * 512], ps[:, 2 * c + n, :]).then_inc(v_ready, 1)
            for hh in range(20, 24):
                split_low(hh)

            def mla_max(hd):
                dve.wait_ge(s_done, hd + 1)
                V.tensor_reduce(mx[:, hd, 0:1], ps[:, 6 + hd % 2, 0:128], AX, ALU.max)
                step(V.tensor_reduce(mx[:, hd, 1:2], ps[:, 6 + hd % 2, 128:384], AX, ALU.max))
                V.tensor_scalar(nmx[:, hd, :], mx[:, hd, :], -MLA_SCALE, None, ALU.mult).then_inc(max_done, 1)

            def mla_low(hd):
                dve.wait_ge(o_hi, hd + 1)
                V.tensor_tensor(xlo[:, hd, :], ps[:, 2 + hd % 2, 0:SEQ], xhi[:, hd, :].bitcast(F32), ALU.subtract).then_inc(o_lo, 1)

            mla_max(0)
            mla_max(1)
            for hd in range(HEADS):
                dve.wait_ge(exp_done, 2 * hd + 2)
                step(V.reciprocal(rr[:, hd, :], rs[:, hd, :]))
                for c, (a, b) in enumerate(((0, 128), (128, 384))):
                    V.tensor_scalar(prob[:, hd % 2, a:b], prob[:, hd % 2, a:b], rr[:, hd, c:c + 1], None, ALU.mult).then_inc(pn_ready, 1)
                if hd >= 1:
                    mla_low(hd - 1)
                if hd + 2 < HEADS:
                    mla_max(hd + 2)
            mla_low(HEADS - 1)
            for hh in range(24, 32):
                split_low(hh)
            dve.wait_ge(used, H_FFN)
            for c in range(TC):
                for n in range(2):
                    hv = h[:, c, n * 512:(n + 1) * 512]
                    V.tensor_tensor(hv, ps[:, 4 + 2 * c + n, :], hv, ALU.add).then_inc(h_ready[1], 1)

            def ffn(x, i=0):
                n, nt, base = FFN[x]

                def gate(j):
                    for c in range(nt):
                        dve.wait_ge(silu_done[x], (i * n + j) * nt + c + 1)
                        g = gu[:, j % 2, c, :]
                        V.tensor_tensor(g, ps[:, bank_gu(x, c, parity(x, j)), GW:2 * GW], g, ALU.mult).then_inc(gated[x], 1)

                def low(j):
                    dve.wait_ge(h_hi[x], i * n + j + 1)
                    src = ps[:, bank_tr(x, j % 2), 0:2 * nt * P]
                    hi = ehi[:, 2 * j:2 * j + 2, :] if nt == 1 else hhi[:, 2 * j:2 * j + 2, :]
                    lo = elo[:, 2 * j:2 * j + 2, :] if nt == 1 else hlo[:, 2 * j:2 * j + 2, :]
                    V.tensor_tensor(lo.rearrange("p a s -> p (a s)"), src, hi.bitcast(F32).rearrange("p a s -> p (a s)"),
                                    ALU.subtract).then_inc(h_lo[x], 1)

                for j in range(n):
                    if j >= 1:
                        gate(j - 1)
                    if j >= 2:
                        low(j - 2)
                    for m in range(4):
                        split_low(base + RING + 4 * j + m, i)
                    if x == 2 and j == 4:
                        V.tensor_copy(gt[:, :], g_tab[:, bass.ds(i, 1), :].rearrange("p a c -> p (a c)")).then_inc(gt_ready, 1)
                        V.tensor_copy(pm[:, :, :], pm_tab[:, bass.ds(i + 1, 1), :, :].rearrange("p a b c -> p (a b) c")).then_inc(pm_ready, 1)
                        dve.wait_ge(pm_ready, i + 2)
                        dve.wait_ge(sel_tr, i + 1)
                        for c in range(TC):
                            V.tensor_scalar(sel[:, c, :], iota[:, :], pm[:, 0, c:c + 1], pm[:, 1, c:c + 1],
                                            ALU.is_equal, ALU.mult).then_inc(sel_ready, 1)
                gate(n - 1)
                low(n - 2)
                for f in range(2 * n):
                    split_low(base + RING + 4 * n + f, i)
                    if f == 1:
                        low(n - 1)
                    if f == 17 and x == 2:
                        gathered_low(i + 1)

            def gathered_low(item):
                for b in range(2):
                    dve.wait_ge(xe_hi, item * KD + 4 * b + 4)
                    for k in range(4 * b, 4 * b + 4):
                        V.scalar_tensor_tensor(out=xlo[:, k, 0:P], in0=ps[:, 6 + b, (k % 4) * P:(k % 4 + 1) * P],
                                               scalar=gcol[:, G_FFN1 + k:G_FFN1 + k + 1], in1=xhi[:, k, 0:P].bitcast(F32),
                                               op0=ALU.mult, op1=ALU.subtract).then_inc(xe_lo, 1)

            dve.wait_ge(h_ready[1], 4)
            norm_tokens(1, xm)
            x_low(1, G_FFN0, 0)
            for x in range(2):
                ffn(x)
                dve.wait_ge(used, FFN[x][2] + 6 * FFN[x][0])
                for c in range(TC):
                    for n in range(2):
                        hv = h[:, c, n * 512:(n + 1) * 512]
                        V.tensor_tensor(hv, ps[:, bank_out(x, c, n), :], hv, ALU.add).then_inc(h_ready[2], 1)

            dve.wait_ge(h_ready[2], 8)
            norm_tokens(2, xs)
            x_low(2, G_KVSH, 0)
            for m in range(8):
                split_low(H_SBK + RING + m)
            for m in range(8):
                split_low(H_SBV + RING + m)
            dve.wait_ge(used, H_SBQ)
            for c in range(TC):
                for n in range(2):
                    V.tensor_copy(sv[:, c, n * 512:(n + 1) * 512], ps[:, 2 * c + n, :]).then_inc(sv_ready, 1)
            x_low(3, G_ATTN1, 4)
            for m in range(8):
                split_low(H_SBQ + RING + m)

            def softplus(hd):
                dve.wait_ge(ln_done, hd + 1)
                buf = sp[:, hd % 4, :]
                V.scalar_tensor_tensor(out=buf, in0=ps[:, hd % 4, 0:384], scalar=0.0, in1=buf,
                                       op0=ALU.max, op1=ALU.add).then_inc(sp_ready, 1)

            def sb_low(hd):
                dve.wait_ge(so_hi, hd + 1)
                V.tensor_tensor(xlo[:, hd, :], ps[:, 4 + hd % 4, 0:SEQ], xhi[:, hd, :].bitcast(F32), ALU.subtract).then_inc(so_lo, 1)

            softplus(0)
            softplus(1)
            for hd in range(HEADS):
                if hd + 2 < HEADS:
                    softplus(hd + 2)
                if hd >= 1:
                    sb_low(hd - 1)
            sb_low(HEADS - 1)
            for m in range(8):
                split_low(H_SBO + RING + m)
            dve.wait_ge(used, H_MOE)
            for c in range(TC):
                for n in range(2):
                    hv = h[:, c, n * 512:(n + 1) * 512]
                    V.tensor_tensor(hv, ps[:, 2 * c + n, :], hv, ALU.add).then_inc(h_ready[3], 1)

            dve.wait_ge(h_ready[3], 4)
            norm_tokens(3, xm)
            x_low(4, G_FFN1, 0)
            step(V.tensor_scalar(rank[:, :], iota[:, 0:N_EXP], -1.0, float(N_EXP), ALU.mult, ALU.add))
            dve.wait_ge(lg_done, 1)
            step(V.tensor_copy(lg[:, :, :].rearrange("p c e -> p (c e)"), ps[:, 4, 0:TC * N_EXP]))
            step(V.tensor_reduce(m1[:, :], lg[:, :, :], AX, ALU.max))
            V.tensor_scalar(nm1[:, :], m1[:, :], -1.0, None, ALU.mult).then_inc(sm_nmax, 1)
            dve.wait_ge(sm_exp, 2)
            step(V.reciprocal(m2[:, :], den[:, :]))

            def per_token(a):
                return a.unsqueeze(2).to_broadcast([P, TC, N_EXP])

            step(V.tensor_tensor(pr[:, :, :], pr[:, :, :], per_token(m2[:, :]), ALU.mult))
            rank_b = rank[:, :].unsqueeze(1).to_broadcast([P, TC, N_EXP])

            def pick(best, chosen):
                step(V.tensor_reduce(best, pr[:, :, :], AX, ALU.max))
                step(V.tensor_tensor(sc8[:, :, :], pr[:, :, :], per_token(best), ALU.is_equal))
                step(V.tensor_tensor(sc8[:, :, :], sc8[:, :, :], rank_b, ALU.mult))
                step(V.tensor_reduce(den[:, :], sc8[:, :, :], AX, ALU.max))
                step(V.tensor_tensor(chosen, sc8[:, :, :], per_token(den[:, :]), ALU.is_equal))

            pick(m1[:, :], oh1[:, :, :])
            step(V.scalar_tensor_tensor(out=pr[:, :, :], in0=oh1[:, :, :], scalar=-4.0, in1=pr[:, :, :],
                                        op0=ALU.mult, op1=ALU.add))
            pick(m2[:, :], oh2[:, :, :])
            V.tensor_tensor(msk[:, :, :], oh1[:, :, :], oh2[:, :, :], ALU.add).then_inc(msk_ready, 1)
            step(V.tensor_tensor(den[:, :], m1[:, :], m2[:, :], ALU.add))
            step(V.reciprocal(den[:, :], den[:, :]))
            step(V.tensor_tensor(m1[:, :], m1[:, :], den[:, :], ALU.mult))
            step(V.tensor_tensor(m2[:, :], m2[:, :], den[:, :], ALU.mult))
            step(V.tensor_tensor(oh1[:, :, :], oh1[:, :, :], per_token(m1[:, :]), ALU.mult))
            step(V.tensor_tensor(oh2[:, :, :], oh2[:, :, :], per_token(m2[:, :]), ALU.mult))
            step(V.tensor_tensor(gates[:, :, :], oh1[:, :, :], oh2[:, :, :], ALU.add))
            dve.wait_ge(pos_done, 1)
            step(V.tensor_copy(posn[:, :, :].rearrange("p c e -> p (c e)"), ps[:, 4, 16:32]))
            step(V.tensor_copy(cnt[:, :], ps[:, 4, 32:40]))
            step(V.tensor_scalar(ovf[:, :], cnt[:, :], float(P), None, ALU.is_gt))
            step(V.tensor_tensor_scan(csum[:, :], ones[:, 0:N_EXP], ovf[:, :], 0.0, ALU.mult, ALU.add))
            for r in range(3):
                step(V.tensor_scalar(selr[:, r, :], csum[:, :], float(r + 1), None, ALU.is_equal))
            step(V.tensor_tensor(selr[:, :, :], selr[:, :, :], ovf[:, :].unsqueeze(1).to_broadcast([P, 3, N_EXP]), ALU.mult))
            for c in range(TC):
                V.tensor_copy(pm_tab[:, 0:N_EXP, 0, c], posn[:, c, :])
                V.tensor_copy(pm_tab[:, 0:N_EXP, 1, c], msk[:, c, :])
                V.tensor_copy(g_tab[:, 0:N_EXP, c], gates[:, c, :])
            V.memset(pm_tab[:, N_EXP:ITEMS, :, :], 0.0).then_inc(h_ready[4], 4)
            step(V.memset(g_tab[:, N_EXP:ITEMS, :], 0.0))
            for c in range(TC):
                for src, dst in ((posn, pm_tab[:, N_EXP:N_EXP + 3, 0, c]), (msk, pm_tab[:, N_EXP:N_EXP + 3, 1, c]),
                                 (gates, g_tab[:, N_EXP:N_EXP + 3, c])):
                    step(V.tensor_tensor(prod[:, :, :], selr[:, :, :], src[:, c, :].unsqueeze(1).to_broadcast([P, 3, N_EXP]), ALU.mult))
                    step(V.tensor_reduce(dst, prod[:, :, :], AX, ALU.add))
                step(V.tensor_scalar(pm_tab[:, N_EXP:N_EXP + 3, 0, c], pm_tab[:, N_EXP:N_EXP + 3, 0, c], -float(P), None, ALU.add))
            step(V.tensor_copy(tf[:, :], iota[:, 0:ITEMS]))
            step(V.memset(tf[:, N_EXP:ITEMS], 0.0))
            step(V.tensor_tensor(prod[:, :, :], selr[:, :, :], iota[:, 0:N_EXP].unsqueeze(1).to_broadcast([P, 3, N_EXP]), ALU.mult))
            step(V.tensor_reduce(tf[:, N_EXP:N_EXP + 3], prod[:, :, :], AX, ALU.add))
            V.tensor_copy(item_expert[:, :], tf[:, :]).then_inc(items_ready, 1)
            V.tensor_scalar(n_items_i[:, :], csum[:, N_EXP - 1:N_EXP], float(N_EXP), None, ALU.add).then_inc(items_ready, 1)
            V.tensor_copy(pm[:, :, :], pm_tab[:, 0, :, :]).then_inc(pm_ready, 1)
            dve.wait_ge(pm_ready, 1)
            for c in range(TC):
                V.tensor_scalar(sel[:, c, :], iota[:, :], pm[:, 0, c:c + 1], pm[:, 1, c:c + 1],
                                ALU.is_equal, ALU.mult).then_inc(sel_ready, 1)
            gathered_low(0)
            dve.wait_ge(items_ready, 2)
            n_items = dve.value_load(n_items_i[0:1, 0:1], min_val=N_EXP, max_val=ITEMS - 1)
            with dve.Fori(0, n_items) as i:
                ffn(2, i)
                for n in range(2):
                    dve.wait_ge(y_hi, i * 2 + n + 1)
                    V.tensor_tensor(xlo[:, 4 * n:4 * n + 4, P:SEQ], ps[:, 4 + n, :].rearrange("p (a s) -> p a s", a=4),
                                    xhi[:, 4 * n:4 * n + 4, P:SEQ].bitcast(F32), ALU.subtract).then_inc(y_lo, 1)
                dve.wait_ge(gt_ready, i + 1)
                for c in range(TC):
                    for n in range(2):
                        dve.wait_ge(scattered, i * 4 + 2 * c + n + 1)
                        hv = h[:, c, n * 512:(n + 1) * 512]
                        V.scalar_tensor_tensor(out=hv, in0=ps[:, 2 + 2 * c + n, :], scalar=gt[:, c:c + 1], in1=hv,
                                               op0=ALU.mult, op1=ALU.add).then_inc(h_ready[4], 1)

            dve.wait_ge(h_ready[4], n_items * 4 + 4)
            V.tensor_tensor_reduce(out=yout[:, 1, :], in0=h[:, 1, :], in1=h[:, 1, :], scale=1.0, scalar=0.0,
                                   op0=ALU.mult, op1=ALU.add, accum_out=ss[:, 4, 1:2]).then_inc(ss_ready[4], 1)
            dve.wait_ge(std_ready[4], 1)
            V.reciprocal(rstd[:, 4, :], std[:, 4, :]).then_inc(rstd_ready[4], 1)
            dve.wait_ge(rstd_ready[4], 1)
            dve.wait_ge(gbc_in, 16)
            for c in range(TC):
                V.scalar_tensor_tensor(out=yout[:, c, :], in0=h[:, c, :], scalar=rstd[:, 4, c:c + 1], in1=gbc[:, :],
                                       op0=ALU.mult, op1=ALU.mult).then_inc(y_ready, 1)

        @block.tensor
        def _(pe):
            def mm3(o, a_hi, a_lo, b_hi, b_lo, start, stop):
                pe.matmul(o, a_hi, b_hi, start=start, stop=False, skip_group_check=True)
                pe.matmul(o, a_lo, b_hi, start=False, stop=False, skip_group_check=True)
                return pe.matmul(o, a_hi, b_lo, start=False, stop=stop, skip_group_check=True)

            def mm(o, a, b, start, stop):
                return pe.matmul(o, a, b, start=start, stop=stop, skip_group_check=True)

            def transpose_x(n, src, bank0):
                for b in range(4):
                    for k in (2 * b, 2 * b + 1):
                        for c in range(TC):
                            last = pe.transpose(ps[:, bank0 + b, (k % 2) * SEQ + c * P:(k % 2) * SEQ + (c + 1) * P],
                                                src[:, c, k * P:(k + 1) * P], ident[:, :])
                    last.then_inc(x_tr[n], 1)

            def tokens_out(k, hh, banks, width=512):
                for c in range(TC):
                    for n in range(2):
                        w = slice(n * 512, (n + 1) * 512)
                        last = mm3(ps[:, banks[c][n], :], xhi[:, k, c * P:(c + 1) * P], xlo[:, k, c * P:(c + 1) * P],
                                   w_hi(hh)[:, w], w_lo(hh)[:, w], k == 0, k == KD - 1)
                last.then_inc(used, 1)

            def features_out(k, hh, bank0):
                for hd in range(HEADS):
                    w = slice(hd * P, (hd + 1) * P)
                    last = mm3(ps[:, bank0 + hd // 2, (hd % 2) * SEQ:(hd % 2 + 1) * SEQ], w_hi(hh)[:, w], w_lo(hh)[:, w],
                               xhi[:, k, :], xlo[:, k, :], k == 0 and hd % 2 == 0, k == KD - 1)
                last.then_inc(used, 1)

            pe.wait_ge(consts, 1)
            pe.wait_ge(small_in, 16 * 7)
            pe.transpose(ps[:, 7, 0:G_ALL], grow[0:G_ALL, :], ident[0:G_ALL, 0:G_ALL]).then_inc(g_tr, 1)
            pe.wait_ge(xn_ready[0], 2)
            transpose_x(0, xn, 0)
            pe.wait_ge(g_ready, 1)
            for k in range(KD):
                pe.wait_ge(xlo_ready[0], k + 1)
                pe.wait_ge(lo_made, H_DOWN + k + 1)
                for c in range(TC):
                    for n, (a, b) in enumerate(((0, Q_LORA), (Q_LORA, DOWN))):
                        last = mm3(ps[:, 4 + 2 * c + n, 0:b - a], xhi[:, k, c * P:(c + 1) * P], xlo[:, k, c * P:(c + 1) * P],
                                   w_hi(H_DOWN + k)[:, a:b], w_lo(H_DOWN + k)[:, a:b], k == 0, k == KD - 1)
                last.then_inc(used, 1)
            pe.wait_ge(cn_ready, 4)
            pe.wait_ge(kr_ready, 1)
            for b in range(3):
                for j in (2 * b, 2 * b + 1):
                    for c in range(TC):
                        src = cn[:, c, j * P:(j + 1) * P] if j < CC else kr[:, c, :]
                        last = pe.transpose(ps[:, b, (j % 2) * SEQ + c * P:(j % 2) * SEQ + (c + 1) * P], src, ident[:, :])
                last.then_inc(c_tr, 1)
            pe.wait_ge(clo_ready, CC)
            pe.wait_ge(chi_ready, CC + 1)
            pe.wait_ge(lo_made, H_UKV)
            for hd in range(HEADS):
                for k in range(3):
                    hh = H_UQ + 2 * k + hd // 4
                    w = slice((hd % 4) * QH, (hd % 4) * QH + P)
                    last = mm3(ps[:, 4 + hd // 2, (hd % 2) * SEQ:(hd % 2 + 1) * SEQ], w_hi(hh)[:, w], w_lo(hh)[:, w],
                               chi[:, k, :], clo[:, k, :], k == 0 and hd % 2 == 0, k == 2)
                if hd % 2:
                    last.then_inc(qn_done, 1)
            for c in range(TC):
                for g in range(2):
                    for k in range(3):
                        hh = H_UQ + 2 * k + g
                        r_hi, r_lo = (f(hh)[:, 0:4 * QH].rearrange("p (a r) -> p a r", r=QH)[:, :, P:QH] for f in (w_hi, w_lo))
                        last = mm3(ps[:, c, g * 256:(g + 1) * 256].rearrange("p (a r) -> p a r", r=ROPE),
                                   chi[:, k, c * P:(c + 1) * P], clo[:, k, c * P:(c + 1) * P], r_hi, r_lo,
                                   k == 0 and g == 0, k == 2)
            last.then_inc(used, 6)
            pe.wait_ge(lo_made, H_WO)
            for hd in range(HEADS):
                if hd % 2 == 0:
                    pe.wait_ge(qT_ready, hd // 2 + 1)
                for k in range(2):
                    hh = H_UKV + 2 * k + hd // 4
                    w = slice((hd % 4) * 2 * P, (hd % 4) * 2 * P + P)
                    last = mm3(ps[:, 4 + hd // 2, (hd % 2) * SEQ:(hd % 2 + 1) * SEQ], w_hi(hh)[:, w], w_lo(hh)[:, w],
                               chi[:, 3 + k, :], clo[:, 3 + k, :], k == 0 and hd % 2 == 0, k == 1)
                if hd % 2:
                    last.then_inc(kn_done, 1)
            pe.wait_ge(rot_ready, 1)
            for c in range(TC):
                for g in range(2):
                    for k in range(2):
                        hh = H_UKV + 2 * k + g
                        v_hi, v_lo = (f(hh).rearrange("p (a r) -> p a r", r=2 * P)[:, :, P:2 * P] for f in (w_hi, w_lo))
                        last = mm3(ps[:, 2 * c + g, :].rearrange("p (a r) -> p a r", r=P),
                                   chi[:, 3 + k, c * P:(c + 1) * P], clo[:, 3 + k, c * P:(c + 1) * P], v_hi, v_lo,
                                   k == 0, k == 1)
            last.then_inc(used, 4)
            for b in range(2):
                pe.wait_ge(kT_ready, b + 1)
                for pair in (2 * b, 2 * b + 1):
                    for c in range(TC):
                        last = pe.transpose(ps[:, 4 + b, (pair % 2) * SEQ + c * P:(pair % 2) * SEQ + (c + 1) * P],
                                            rot[:, c, 2 * pair:2 * pair + 2, :].rearrange("p a r -> p (a r)"), ident[:, :])
                last.then_inc(rot_tr, 1)

            def scores(hd):
                b = 6 + hd % 2
                lo = (hd % 2) * ROPE
                for c, (a, e) in enumerate(((0, 128), (128, 384))):
                    mm(ps[:, b, a:e], qT[:, hd, c * P:(c + 1) * P], kT[:, hd, 0:e - a], c == 0, False)
                for c, (a, e) in enumerate(((0, 128), (128, 384))):
                    mm(ps[:, b, a:e], qrT[lo:lo + ROPE, hd // 2, c * P:(c + 1) * P], krT[lo:lo + ROPE, 0:e - a], False, False)
                for a in (CHUNK, 128 + 192):
                    last = mm(ps[:, b, a:a + CHUNK], half_mask[0:1, 0:P], half_mask[0:1, P:P + CHUNK], False, True)
                last.then_inc(s_done, 1)

            def outputs(hd):
                pe.wait_ge(probT_ready, hd + 1)
                if hd >= 2:
                    pe.wait_ge(o_lo, hd - 1)
                o = ps[:, 2 + hd % 2, :]
                mm(o[:, 0:SEQ], v[:, 0, hd * P:(hd + 1) * P], probT[:, hd % 2, 0:SEQ], True, False)
                mm(o[:, P:SEQ], v[:, 1, hd * P:(hd + 1) * P], probT[:, hd % 2, SEQ:384], False, True).then_inc(o_done, 1)

            pe.wait_ge(qrT_ready, 2)
            pe.wait_ge(kT_ready, 4)
            scores(0)
            scores(1)
            pe.wait_ge(v_ready, 4)
            for hd in range(HEADS):
                pe.wait_ge(pn_ready, 2 * hd + 2)
                if hd >= 2:
                    pe.wait_ge(probT_ready, hd - 1)
                for n in range(3):
                    last = pe.transpose(ps[:, hd % 2, n * P:(n + 1) * P], prob[:, hd % 2, n * P:(n + 1) * P], ident[:, :])
                last.then_inc(pt_done, 1)
                if hd + 2 < HEADS:
                    scores(hd + 2)
                outputs(hd)
            for k in range(HEADS):
                pe.wait_ge(o_lo, HEADS if k == 0 else k + 1)
                pe.wait_ge(lo_made, H_WO + k + 1)
                tokens_out(k, H_WO + k, ((4, 5), (6, 7)))

            def ffn(x, i=0):
                n, nt, base = FFN[x]

                def products(j):
                    if j >= 2:
                        pe.wait_ge(gated[x], (i * n + j - 1) * nt)
                    for m in range(4):
                        hh = base + 4 * j + m
                        pe.wait_ge(lo_made, i * FH + hh + 1)
                        for c in range(nt):
                            for kk in range(2):
                                k = 2 * m + kk
                                w = slice(kk * 512, (kk + 1) * 512)
                                last = mm3(ps[:, bank_gu(x, c, parity(x, j)), :],
                                           xhi[:, k, c * P:(c + 1) * P], xlo[:, k, c * P:(c + 1) * P],
                                           w_hi(hh)[:, w], w_lo(hh)[:, w], k == 0, k == KD - 1)
                        last.then_inc(used, 1)

                def transposes(j):
                    pe.wait_ge(gated[x], (i * n + j + 1) * nt)
                    if j >= 2:
                        pe.wait_ge(h_lo[x], i * n + j - 1)
                    for b in range(2):
                        for c in range(nt):
                            o = (b * nt + c) * P
                            last = pe.transpose(ps[:, bank_tr(x, j % 2), o:o + P], gu[:, j % 2, c, b * P:(b + 1) * P], ident[:, :])
                    last.then_inc(gu_tr[x], 1)

                for j in range(n):
                    if x == 1 and j == 1:
                        pe.wait_ge(h_ready[2], 4)
                    products(j)
                    if j == 1 and x == 2:
                        pe.wait_ge(h_ready[4], i * 4 + 4)
                    if j >= 1:
                        transposes(j - 1)
                hi, lo = (ehi, elo) if nt == 1 else (hhi, hlo)
                for f in range(2 * n):
                    hh = base + 4 * n + f
                    pe.wait_ge(lo_made, i * FH + hh + 1)
                    if f % 2 == 0:
                        pe.wait_ge(h_lo[x], i * n + f // 2 + 1)
                    for c in range(nt):
                        for m in range(2):
                            w = slice(m * 512, (m + 1) * 512)
                            last = mm3(ps[:, bank_out(x, c, m), :], hi[:, f, c * P:(c + 1) * P], lo[:, f, c * P:(c + 1) * P],
                                       w_hi(hh)[:, w], w_lo(hh)[:, w], f == 0, f == 2 * n - 1)
                    last.then_inc(used, 1)
                    if f == 1:
                        transposes(n - 1)
                    if f == 11 and x == 2:
                        gather(i + 1)

            def gather(item):
                pe.wait_ge(sel_ready, item * 2 + 2)
                pe.wait_ge(selT_ready, item)
                for k in range(KD):
                    o = ps[:, 6 + k // 4, (k % 4) * P:(k % 4 + 1) * P]
                    for c in range(TC):
                        last = mm(o, xm[:, c, k * P:(k + 1) * P], sel[:, c, :], c == 0 and k % 4 == 0, c == TC - 1)
                    if k % 4 == 3:
                        last.then_inc(gathered, 1)

            def transpose_sel(item):
                pe.wait_ge(xe_lo, item * KD + KD)
                for c in range(TC):
                    last = pe.transpose(ps[:, 6, c * P:(c + 1) * P], sel[:, c, :], ident[:, :])
                last.then_inc(sel_tr, 1)

            pe.wait_ge(xn_ready[1], 2)
            transpose_x(1, xm, 0)
            pe.wait_ge(xlo_ready[1], KD)
            ffn(0)
            ffn(1)

            pe.wait_ge(xn_ready[2], 2)
            transpose_x(2, xs, 0)
            pe.wait_ge(xlo_ready[2], KD)
            for k in range(KD):
                pe.wait_ge(lo_made, H_SBK + k + 1)
                features_out(k, H_SBK + k, 4)
            for k in range(KD):
                pe.wait_ge(lo_made, H_SBV + k + 1)
                tokens_out(k, H_SBV + k, ((0, 1), (2, 3)))
            pe.wait_ge(skT_ready, 4)
            transpose_x(3, xs, 4)
            pe.wait_ge(xlo_ready[3], KD)
            pe.wait_ge(sv_ready, 4)
            for k in range(KD):
                pe.wait_ge(lo_made, H_SBQ + k + 1)
                features_out(k, H_SBQ + k, 0)

            def logits(hd):
                z = ps[:, hd % 4, :]
                mm(z[:, 0:SEQ], skT[:, hd, 0:P], sqT[:, hd, :], True, False)
                mm(z[:, SEQ:384], skT[:, hd, P:SEQ], sqT[:, hd, P:SEQ], False, False)
                mm(z[:, 0:P], ident[:, :], hide[:, :], False, False)
                mm(z[:, SEQ:384], ident[:, :], hide[:, :], False, True).then_inc(z_done, 1)

            def sb_outputs(hd):
                pe.wait_ge(a_ready, hd + 1)
                if hd >= 4:
                    pe.wait_ge(so_lo, hd - 3)
                o = ps[:, 4 + hd % 4, :]
                mm(o[:, 0:SEQ], sv[:, 0, hd * P:(hd + 1) * P], aT[:, hd % 4, 0:SEQ], True, False)
                mm(o[:, P:SEQ], sv[:, 1, hd * P:(hd + 1) * P], aT[:, hd % 4, SEQ:384], False, True).then_inc(so_done, 1)

            pe.wait_ge(sqT_ready, 4)
            for hd in range(4):
                logits(hd)
            for hd in range(HEADS):
                pe.wait_ge(sp_ready, hd + 1)
                z, s = ps[:, hd % 4, :], sp[:, hd % 4, :]
                mm(z[:, 0:SEQ], neg_from[:, :], s[:, 0:SEQ], False, False)
                mm(z[:, SEQ:384], neg_from[:, :], s[:, SEQ:384], False, False)
                mm(z[:, P:SEQ], neg_ones[:, :], s[:, SEQ:384], False, True).then_inc(c_done, 1)
                if hd >= 1:
                    sb_outputs(hd - 1)
                    if hd + 3 < HEADS:
                        logits(hd + 3)
            sb_outputs(HEADS - 1)
            pe.wait_ge(so_lo, HEADS)
            for k in range(HEADS):
                pe.wait_ge(lo_made, H_SBO + k + 1)
                tokens_out(k, H_SBO + k, ((0, 1), (2, 3)))

            pe.wait_ge(xn_ready[3], 2)
            transpose_x(4, xm, 0)
            pe.wait_ge(router_ready, 2)
            pe.wait_ge(xlo_ready[4], KD)
            for c in range(TC):
                for k in range(KD):
                    a_hi, a_lo = xhi[:, k, c * P:(c + 1) * P], xlo[:, k, c * P:(c + 1) * P]
                    o = ps[:, 4, c * N_EXP:(c + 1) * N_EXP]
                    mm3(o, a_hi, a_lo, router_hi[:, k, :], router_lo[:, k, :], c == 0 and k == 0, False)
                    last = mm(o, a_lo, router_lo[:, k, :], False, k == KD - 1)
            last.then_inc(lg_done, 1)
            pe.wait_ge(msk_ready, 1)
            mm(ps[:, 4, 16:24], before[:, :], msk[:, 0, :], True, True)
            mm(ps[:, 4, 24:32], ones[:, :], msk[:, 0, :], False, False)
            mm(ps[:, 4, 24:32], before[:, :], msk[:, 1, :], False, True)
            mm(ps[:, 4, 32:40], ones[:, :], msk[:, 0, :], False, False)
            mm(ps[:, 4, 32:40], ones[:, :], msk[:, 1, :], False, True).then_inc(pos_done, 1)

            pe.wait_ge(sel_ready, 2)
            for k in range(KD):
                o = ps[:, 6 + k // 4, (k % 4) * P:(k % 4 + 1) * P]
                for c in range(TC):
                    last = mm(o, xm[:, c, k * P:(k + 1) * P], sel[:, c, :], c == 0 and k % 4 == 0, c == TC - 1)
                if k % 4 == 3:
                    last.then_inc(gathered, 1)
            transpose_sel(0)
            pe.wait_ge(items_ready, 2)
            n_items = pe.value_load(n_items_i[0:1, 0:1], min_val=N_EXP, max_val=ITEMS - 1)
            with pe.Fori(0, n_items) as i:
                pe.wait_ge(xe_lo, i * KD + KD)
                ffn(2, i)
                pe.wait_ge(y_lo, i * 2 + 2)
                pe.wait_ge(selT_ready, i + 1)
                for c in range(TC):
                    for n in range(2):
                        o = ps[:, 2 + 2 * c + n, :].rearrange("p (a s) -> p a s", a=4)
                        w = selT[:, c * P:(c + 1) * P]
                        mm(o, w, xhi[:, 4 * n:4 * n + 4, P:SEQ], True, False)
                        mm(o, w, xlo[:, 4 * n:4 * n + 4, P:SEQ], False, True).then_inc(scattered, 1)
                transpose_sel(i + 1)


INPUTS = ["x", "positions", "attn_norm_0", "mla_w_down_0", "mla_q_norm_0", "mla_w_uq_0", "mla_kv_norm_0",
          "mla_w_ukv_0", "mla_w_o_0", "ffn_norm_0", "ffn_w_gate_up_0", "ffn_w_down_0", "attn_norm_1",
          "ffn_norm_1", "moe_router_1", "moe_w_gate_up_1", "moe_w_down_1", "kv_shared_norm", "kv_shared_w",
          "sb_w_q_2", "sb_w_o_2", "final_norm"]


def kernel(**inputs):
    import concourse.bacc as bacc
    from concourse.bass_utils import run_bass_kernel_spmd as run

    nc = bacc.Bacc("TRN2", target_bir_lowering=False, num_devices=1)
    arrays, t = {}, {}
    for name in INPUTS:
        a = np.ascontiguousarray(inputs[name])
        arrays[f"{name}_dram"] = a
        t[name] = nc.dram_tensor(f"{name}_dram", a.shape, mybir.dt.from_np(a.dtype), kind="ExternalInput").ap()
    out = nc.dram_tensor("out_dram", (1, SEQ, D), F32, kind="ExternalOutput").ap()
    build(nc, t, out)
    r = run(nc, [arrays], core_ids=[0])
    return r.results[0]["out_dram"]
```

```python
import numpy as np
from contextlib import ExitStack

import concourse.bass as bass
from concourse import mybir

F32 = mybir.dt.float32
F32R = mybir.dt.float32r
I32 = mybir.dt.int32
ALU = mybir.AluOpType
ACT = mybir.ActivationFunctionType
AX = mybir.AxisListType.X

P = 128
SEQ, D = 256, 1024
TC = SEQ // P
KD = D // P
HEADS = 8
Q_LORA, KV_LORA, ROPE = 384, 256, 64
DOWN = Q_LORA + KV_LORA + ROPE
QH = P + ROPE
CC = (Q_LORA + KV_LORA) // P
FF = 2816
N_EXP = 8
CHUNK = 64
EPS = 1e-6
MLA_SCALE = float(QH) ** -0.5
SB_SCALE = float(P) ** -0.5
NEG = -1e30

RAW = 11
RING = 6
HALF = 1024
GW = 256
NG = FF // GW
FU = 3 * NG
FH = 2 * FU
FC = FF // P
H_DOWN, H_UQ, H_UKV, H_WO = 0, 8, 14, 18
H_FFN = 26
GA = 6
H_FFN_B = H_FFN + 6 * GA
H_SBK = H_FFN + FH
H_SBV, H_SBQ, H_SBO = H_SBK + 8, H_SBK + 16, H_SBK + 24
H_MOE = H_SBK + 32
U_MOE = H_MOE // 2
assert H_MOE % 2 == 0 and FU % RAW == 0 and FH % RING == 0
ITEMS = 12

G_ATTN0, G_Q, G_KV, G_FFN0, G_KVSH, G_ATTN1, G_FFN1, G_ALL = 0, 8, 11, 13, 21, 29, 37, 45


def half_width(h):
    return DOWN if h < H_UQ else 4 * QH if h < H_UKV else HALF


def build(nc, t, out):
    with ExitStack() as ctx:
        def sb(name, shape, dt=F32):
            return ctx.enter_context(nc.sbuf_tensor(name, shape, dt))

        def sem(name):
            return ctx.enter_context(nc.semaphore(name))

        raw = sb("raw", [P, RAW, 2 * HALF])
        whi = sb("whi", [P, RING, HALF], F32R)
        wlo = sb("wlo", [P, RING, HALF], F32R)
        h = sb("h", [P, TC, D])
        xhi = sb("xhi", [P, KD, SEQ], F32R)
        xlo = sb("xlo", [P, KD, SEQ], F32R)
        ident = sb("ident", [P, P])
        ones = sb("ones", [P, P])
        neg_ones = sb("neg_ones", [P, P])
        before = sb("before", [P, P])
        neg_from = sb("neg_from", [P, P])
        iota = sb("iota", [P, P])
        gcol = sb("gcol", [P, G_ALL])
        ss = sb("ss", [P, 5, TC])
        ms = sb("ms", [P, 5, TC])
        rstd = sb("rstd", [P, 5, TC])
        minus_half = sb("minus_half", [P, 4])
        rb = sb("rb", [P, SEQ])
        ident_r = sb("ident_r", [P, P], F32R)
        hide_r = sb("hide_r", [P, P], F32R)
        one = sb("one", [P, 1])
        silu_scratch = sb("silu_scratch", [P, 1])
        router = sb("router", [P, KD, N_EXP])
        pm_tab = sb("pm_tab", [P, ITEMS, 2, TC])
        g_tab = sb("g_tab", [P, ITEMS, TC])
        item_expert = sb("item_expert", [P, ITEMS], I32)
        n_items_i = sb("n_items_i", [P, 1], I32)
        pm = sb("pm", [P, 2, TC])
        gt = sb("gt", [P, TC])

        def over(*specs):
            with ExitStack() as e:
                return [e.enter_context(nc.sbuf_tensor(n, s, d)) for n, s, d in specs]

        kT, qT, v, qrT, krT, chi, clo = over(
            ("kT", [P, HEADS, SEQ], F32), ("qT", [P, HEADS, SEQ], F32), ("v", [P, TC, D], F32),
            ("qrT", [P, 4, SEQ], F32), ("krT", [P, SEQ], F32),
            ("chi", [P, CC, SEQ], F32R), ("clo", [P, CC, SEQ], F32R))
        xn, cn, _, rot, rt, kr, _, prob, probT, hide, grow = over(
            ("xn", [P, TC, D], F32), ("cn", [P, TC, Q_LORA + KV_LORA], F32), ("gap0", [P, 768], F32),
            ("rot", [P, TC, HEADS, ROPE], F32), ("rt", [P, 2, HEADS, ROPE // 2], F32),
            ("kr", [P, TC, 2 * ROPE], F32),
            ("gap1", [P, 5 * SEQ + 256], F32), ("prob", [P, 2, 384], F32), ("probT", [P, 2, 384], F32),
            ("hide", [P, P], F32), ("grow", [P, P], F32))
        diag, = over(("diag", [P, TC, P], F32))
        _, ang, ang_k, cos, sin, invf, posi, posf, mx, nmx, rs, rr, css, cfac, qscale, half_mask = over(
            ("gap2", [P, 6 * 1024 + 1280 + 2560], F32), ("ang", [P, TC, 32], F32), ("ang_k", [P, TC, 32], F32),
            ("cos", [P, TC, 32], F32), ("sin", [P, TC, 32], F32), ("invf", [P, 32], F32),
            ("posi", [P, TC], I32), ("posf", [P, TC], F32),
            ("mx", [P, HEADS, 2], F32), ("nmx", [P, HEADS, 2], F32), ("rs", [P, HEADS, 2], F32),
            ("rr", [P, HEADS, 2], F32), ("css", [P, 2, TC], F32), ("cfac", [P, 2, TC], F32),
            ("qscale", [P, 2, TC], F32), ("half_mask", [P, 192], F32))
        hhi, hlo, xm, gu, sel, selT = over(
            ("hhi", [P, 2 * GA, SEQ], F32R), ("hlo", [P, 2 * GA, SEQ], F32R),
            ("xm", [P, TC, D], F32), ("gu", [P, 2, TC, GW], F32), ("sel", [P, TC, P], F32),
            ("selT", [P, SEQ], F32R))
        gbc = gu[:, :, :, :].rearrange("p a c g -> p (a c g)")
        ehi = hhi[:, :, :].rearrange("p c t -> p (c t)").rearrange("p (c t) -> p c t", t=P)
        elo = hlo[:, :, :].rearrange("p c t -> p (c t)").rearrange("p (c t) -> p c t", t=P)
        skT, sqT, sv, sp = over(
            ("skT", [P, HEADS, SEQ], F32), ("sqT", [P, HEADS, SEQ], F32), ("sv", [P, TC, D], F32),
            ("sp", [P, HEADS, 384], F32))
        router_hl, lgT, fold, lg, lg2, oh1, oh2, sc8, msk, gates, posn, ovf, csum, selr, prod, m1, m2, den, best, \
            rank, cnt, tf = over(
                ("router_hl", [P, KD, P], F32R), ("lgT", [P, SEQ], F32), ("fold", [P, N_EXP], F32),
                *[(f"rt_{n}", [P, TC, N_EXP], F32) for n in
                  ("lg", "lg2", "oh1", "oh2", "sc8", "msk", "gates", "posn")],
                ("rt_ovf", [P, N_EXP], F32), ("rt_csum", [P, N_EXP], F32), ("rt_selr", [P, 3, N_EXP], F32),
                ("rt_prod", [P, 3, N_EXP], F32), ("rt_m1", [P, TC], F32), ("rt_m2", [P, TC], F32),
                ("rt_den", [P, TC], F32), ("rt_best", [P, TC], F32), ("rt_rank", [P, N_EXP], F32),
                ("rt_cnt", [P, N_EXP], F32), ("rt_tf", [P, ITEMS], F32))
        yout, = over(("yout", [P, TC, D], F32))

        ps = ctx.enter_context(nc.psum_tensor("ps", [P, 8, 512], F32))

        landed = [sem(f"landed{i}") for i in range(RAW)]
        hi_made = sem("hi_made")
        lo_made = sem("lo_made")
        used = sem("used")
        small_in = sem("small_in")
        pos_in = sem("pos_in")
        x_in = [sem(f"x_in{n}") for n in range(2)]
        h_ready = [None] + [sem(f"h_ready{n}") for n in range(1, 5)]
        consts = sem("consts")
        pool_step = sem("pool_step")
        dve_step = sem("dve_step")
        act_step = sem("act_step")
        ss_ready = [sem(f"ss_ready{n}") for n in range(5)]
        rstd_ready = [sem(f"rstd_ready{n}") for n in range(5)]
        rb_diag, rb_mm, rb_ready = sem("rb_diag"), sem("rb_mm"), sem("rb_ready")
        xm_ready = sem("xm_ready")
        TRS = 5
        x_tr = [sem(f"x_tr{n}") for n in range(TRS)]
        xhi_ready = [sem(f"xhi_ready{n}") for n in range(TRS)]
        xlo_ready = [sem(f"xlo_ready{n}") for n in range(TRS)]
        g_tr, g_ready = sem("g_tr"), sem("g_ready")
        ang_ready, rc_ready, sin_ready = sem("ang_ready"), sem("rc_ready"), sem("sin_ready")
        c_ss, cfac_ready, cn_ready, kr_scaled, kr_ready = (
            sem(n) for n in ("c_ss", "cfac_ready", "cn_ready", "kr_scaled", "kr_ready"))
        c_tr, chi_ready, clo_ready = sem("c_tr"), sem("chi_ready"), sem("clo_ready")
        qn_done, qT_ready, kn_done, kT_ready = sem("qn_done"), sem("qT_ready"), sem("kn_done"), sem("kT_ready")
        rot_ready, v_ready, rot_tr, qrT_ready = sem("rot_ready"), sem("v_ready"), sem("rot_tr"), sem("qrT_ready")
        s_done, max_done, exp_done, pn_ready = sem("s_done"), sem("max_done"), sem("exp_done"), sem("pn_ready")
        pt_done, probT_ready, o_done, o_hi, o_lo = (sem(n) for n in ("pt_done", "probT_ready", "o_done", "o_hi", "o_lo"))
        skT_ready, sv_ready, sqT_ready = sem("skT_ready"), sem("sv_ready"), sem("sqT_ready")
        z_done, ln_done, sp_ready, c_done, a_ready = (
            sem(n) for n in ("z_done", "ln_done", "sp_ready", "c_done", "a_ready"))
        so_done, so_hi, so_lo = sem("so_done"), sem("so_hi"), sem("so_lo")
        silu_done = [sem(f"silu_done{n}") for n in range(3)]
        gated = [sem(f"gated{n}") for n in range(3)]
        gu_tr = [sem(f"gu_tr{n}") for n in range(3)]
        h_hi = [sem(f"h_hi{n}") for n in range(3)]
        h_lo = [sem(f"h_lo{n}") for n in range(3)]
        router_ready, lgT_done, lgT_ready, lg_done, gap_ready, gap_exp = (
            sem(n) for n in ("router_ready", "lgT_done", "lgT_ready", "lg_done", "gap_ready", "gap_exp"))
        msk_ready, pos_done, items_ready = sem("msk_ready"), sem("pos_done"), sem("items_ready")
        pm_ready, sel_ready, gathered, xe_hi, xe_lo = (sem(n) for n in ("pm_ready", "sel_ready", "gathered", "xe_hi", "xe_lo"))
        sel_tr, selT_ready, y_hi, y_lo, scattered, gt_ready = (sem(n) for n in ("sel_tr", "selT_ready", "y_hi", "y_lo", "scattered", "gt_ready"))
        gbc_in, y_ready, stored = sem("gbc_in"), sem("y_ready"), sem("stored")

        block = ctx.enter_context(nc.Block())

        def raw_half(hh):
            return raw[:, (hh // 2) % RAW, (hh % 2) * HALF:(hh % 2) * HALF + half_width(hh)]

        def w_hi(hh):
            return whi[:, hh % RING, :]

        def w_lo(hh):
            return wlo[:, hh % RING, :]

        def bank_gu(x, c, par):
            return par if x == 2 else 2 * par + c

        def bank_tr(x, par):
            return 2 + par if x == 2 else 4 + par

        def bank_out(x, c, n):
            return 4 + n if x == 2 else (6 + n if c == 0 else n)

        def parity(x, j):
            return (j + 1) % 2 if x == 1 else j % 2

        X_BANKS = [(0, 1, 2, 3), (4, 6, 5, 7), (0, 2, 1, 3), (4, 5, 6, 7), (0, 2, 1, 3)]

        FFN = [(GA, 2, H_FFN), (NG - GA, 2, H_FFN_B), (NG, 1, H_MOE)]

        @block.sync
        def _(sp_eng):
            def slot_free(u, i=0):
                if u >= RAW:
                    sp_eng.wait_ge(lo_made, i * FH + 2 * (u - RAW) + 2)

            def load(u, halves, i=0):
                slot_free(u, i)
                for dst, src in halves:
                    sp_eng.dma_start(dst, src).then_inc(landed[u % RAW], 16)

            def rows(u, w, r, width=HALF):
                return [(raw[:, u % RAW, n * HALF:n * HALF + width], w[r + n * P:r + (n + 1) * P, :]) for n in range(2)]

            def square(u0, w):
                for n in range(4):
                    load(u0 + n, rows(u0 + n, w, 256 * n))

            def swiglu_unit(u, x_unit, w_gu, w_dn, i=0):
                if x_unit < 2 * NG:
                    j, q = x_unit // 2, x_unit % 2
                    src = w_gu.rearrange("(k p) f -> p k f", p=P)[:, 4 * q:4 * q + 4, :]
                    dst = raw[:, u % RAW, :].rearrange("p (k f) -> p k f", k=4)
                    load(u, [(dst[:, :, g * GW:(g + 1) * GW], src[:, :, g * FF + j * GW:g * FF + (j + 1) * GW])
                             for g in range(2)], i)
                else:
                    load(u, rows(u, w_dn, (x_unit - 2 * NG) * 256), i)

            for n in range(2):
                w = slice(n * 512, (n + 1) * 512)
                sp_eng.dma_start(h[:, :, w], t["x"].rearrange("a (c p) d -> p (a c) d", p=P)[:, :, w]).then_inc(x_in[n], 16)
            for u in range(4):
                load(u, rows(u, t["mla_w_down_0"], u * 256, DOWN))
            for hh0, w, ks, cols in ((H_UQ, t["mla_w_uq_0"], 3, 4 * QH), (H_UKV, t["mla_w_ukv_0"], 2, HALF)):
                for m in range(0, 2 * ks, 2):
                    load((hh0 + m) // 2, [
                        (raw_half(hh0 + x), w[(x % ks) * P:(x % ks + 1) * P, (x // ks) * cols:(x // ks + 1) * cols])
                        for x in (m, m + 1)])
            square(H_WO // 2, t["mla_w_o_0"])
            order = list(range(2 * GA)) + [2 * NG + n for n in range(GA)] + \
                list(range(2 * GA, 2 * NG)) + [2 * NG + n for n in range(GA, NG)]
            for n, x_unit in enumerate(order):
                swiglu_unit(H_FFN // 2 + n, x_unit, t["ffn_w_gate_up_0"], t["ffn_w_down_0"])
            square(H_SBK // 2, t["kv_shared_w"][:, 0:D])
            square(H_SBV // 2, t["kv_shared_w"][:, D:2 * D])
            square(H_SBQ // 2, t["sb_w_q_2"])
            square(H_SBO // 2, t["sb_w_o_2"])

            def expert(e):
                return (t["moe_w_gate_up_1"][bass.ds(e, 1), :, :].rearrange("a k f -> (a k) f"),
                        t["moe_w_down_1"][bass.ds(e, 1), :, :].rearrange("a k f -> (a k) f"))

            def item_loads(i, now, following):
                for n in range(3, FU):
                    swiglu_unit(U_MOE + n, n, *now, i=i)
                for n in range(3):
                    swiglu_unit(U_MOE + FU + n, n, *following, i=i)

            first = (t["moe_w_gate_up_1"][0], t["moe_w_down_1"][0])
            for n in range(3):
                swiglu_unit(U_MOE + n, n, *first)
            with sp_eng.Fori(0, N_EXP - 1) as i:
                item_loads(i, expert(i), expert(i + 1))
            sp_eng.wait_ge(items_ready, 2)
            n_items = sp_eng.value_load(n_items_i[0:1, 0:1], min_val=N_EXP, max_val=ITEMS - 1)
            with sp_eng.Fori(N_EXP - 1, n_items) as i:
                e = sp_eng.value_load(item_expert[0:1, bass.ds(i, 1)], min_val=0, max_val=N_EXP - 1)
                e_next = sp_eng.value_load(item_expert[0:1, bass.ds(i + 1, 1)], min_val=0, max_val=N_EXP - 1)
                item_loads(i, expert(e), expert(e_next))
            for n in range(3):
                u = U_MOE + n
                sp_eng.wait_ge(landed[u % RAW], n_items * (32 * FU // RAW) + 32 * (u // RAW + 1))
            for c in range(TC):
                sp_eng.wait_ge(y_ready, c + 1)
                sp_eng.dma_start(out[0, c * P:(c + 1) * P, :], yout[:, c, :]).then_inc(stored, 16)
            sp_eng.wait_ge(stored, 16 * TC)

        @block.gpsimd
        def _(pool):
            n = [0]

            def step(ins):
                n[0] += 1
                ins.then_inc(pool_step, 1)
                pool.wait_ge(pool_step, n[0])

            inv = 1.0 / (10000.0 ** (np.arange(0, ROPE, 2, dtype=np.float64) / ROPE))
            for c in range(ROPE // 2):
                nc.gpsimd.memset(invf[:, c:c + 1], float(np.float32(inv[c])))
            nc.gpsimd.memset(minus_half[:, :], -0.5)
            nc.gpsimd.memset(one[:, :], 1.0)
            nc.gpsimd.memset(ones[:, :], 1.0)
            nc.gpsimd.memset(neg_ones[:, :], -1.0)
            nc.gpsimd.memset(half_mask[0:1, 0:64], 1.0)
            nc.gpsimd.memset(half_mask[0:1, 64:128], 0.0)
            nc.gpsimd.memset(half_mask[0:1, 128:192], NEG)
            nc.gpsimd.memset(ident[:, :], 0.0)
            nc.gpsimd.memset(hide[:, :], 0.0)
            step(nc.gpsimd.memset(before[:, :], 0.0))
            nc.gpsimd.affine_select(out=ident[:, :], in_=ident[:, :], compare_op=ALU.not_equal, fill=1.0,
                                    base=0, pattern=[[-1, P]], channel_multiplier=1)
            nc.gpsimd.affine_select(out=before[:, :], in_=before[:, :], compare_op=ALU.is_ge, fill=1.0,
                                    base=0, pattern=[[-1, P]], channel_multiplier=1)
            nc.gpsimd.affine_select(out=hide[:, :], in_=hide[:, :], compare_op=ALU.is_gt, fill=NEG,
                                    base=0, pattern=[[1, P]], channel_multiplier=-1)
            nc.gpsimd.affine_select(out=neg_from[:, :], in_=neg_ones[:, :], compare_op=ALU.is_ge, fill=0.0,
                                    base=0, pattern=[[-1, P]], channel_multiplier=1)
            nc.gpsimd.iota(iota[:, :], [[1, P]], base=0, channel_multiplier=0,
                           allow_small_or_imprecise_dtypes=True).then_inc(consts, 1)

            def norm(k):
                pool.wait_ge(ss_ready[k], 2)
                step(nc.gpsimd.tensor_scalar(ms[:, k, :], ss[:, k, :], 1.0 / D, EPS, ALU.mult, ALU.add))
                nc.gpsimd.tensor_tensor(rstd[:, k, :], ms[:, k, :], minus_half[:, 0:TC], ALU.pow).then_inc(rstd_ready[k], 1)

            norm(0)
            pool.wait_ge(rstd_ready[0], 1)
            pool.wait_ge(c_ss, 4)
            for m, width in ((0, Q_LORA), (1, KV_LORA)):
                step(nc.gpsimd.tensor_tensor(cfac[:, m, :], css[:, m, :], rstd[:, 0, :], ALU.mult))
                step(nc.gpsimd.tensor_tensor(cfac[:, m, :], cfac[:, m, :], rstd[:, 0, :], ALU.mult))
                step(nc.gpsimd.tensor_scalar(cfac[:, m, :], cfac[:, m, :], 1.0 / width, EPS, ALU.mult, ALU.add))
                step(nc.gpsimd.tensor_tensor(cfac[:, m, :], cfac[:, m, :], minus_half[:, 0:TC], ALU.pow))
                step(nc.gpsimd.tensor_tensor(cfac[:, m, :], cfac[:, m, :], rstd[:, 0, :], ALU.mult))
            nc.gpsimd.tensor_scalar(qscale[:, 1, :], cfac[:, 0, :], -MLA_SCALE, None, ALU.mult)
            nc.gpsimd.tensor_scalar(qscale[:, 0, :], cfac[:, 0, :], MLA_SCALE, None, ALU.mult).then_inc(cfac_ready, 1)
            for k in range(1, 5):
                norm(k)

        @block.scalar
        def _(act):
            steps = [0]

            def step(ins):
                steps[0] += 1
                ins.then_inc(act_step, 1)
                act.wait_ge(act_step, steps[0])

            def copy(o, i, scale=1.0):
                return nc.scalar.activation(o, i, ACT.Copy, scale=scale)

            def split_high(hh, i=0):
                u = hh // 2
                act.wait_ge(landed[u % RAW], i * (32 * FU // RAW) + 32 * (u // RAW + 1))
                if hh >= RING:
                    act.wait_ge(used, i * FH + hh - RING + 1)
                copy(w_hi(hh)[:, 0:half_width(hh)], raw_half(hh)).then_inc(hi_made, 1)

            def squares(n, c, junk):
                nc.scalar.activation(junk, h[:, c, :], ACT.Square, accum_out=ss[:, n, c:c + 1]).then_inc(ss_ready[n], 1)

            def x_high(n, gain):
                for b in range(4):
                    act.wait_ge(x_tr[n], b + 1)
                    for k in (2 * b, 2 * b + 1):
                        copy(xhi[:, k, :], ps[:, X_BANKS[n][b], (k % 2) * SEQ:(k % 2 + 1) * SEQ],
                             scale=gcol[:, gain + k:gain + k + 1]).then_inc(xhi_ready[n], 1)

            row = 0
            for name, rows in (("attn_norm_0", 8), ("mla_q_norm_0", 3), ("mla_kv_norm_0", 2), ("ffn_norm_0", 8),
                               ("kv_shared_norm", 8), ("attn_norm_1", 8), ("ffn_norm_1", 8)):
                act.dma_start(grow[row:row + rows, :], t[name].rearrange("(k c) -> k c", c=P)).then_inc(small_in, 16)
                row += rows
            act.dma_start(posi[:, :], t["positions"].rearrange("a (c p) -> p (a c)", p=P),
                          allow_slow_non_contiguous=True).then_inc(pos_in, 16)
            act.dma_start(router[:, :, :], t["moe_router_1"].rearrange("(k p) e -> p k e", p=P)).then_inc(pos_in, 16)

            act.wait_ge(g_tr, 1)
            copy(gcol[:, :], ps[:, 7, 0:G_ALL]).then_inc(g_ready, 1)
            act.wait_ge(g_ready, 1)
            x_high(0, G_ATTN0)
            split_high(0)
            split_high(1)
            squares(0, 0, xn[:, 0, :])
            for hh in range(2, 6):
                split_high(hh)
            act.wait_ge(rc_ready, 2)
            nc.scalar.activation(sin[:, :, :], ang[:, :, :], ACT.Sin).then_inc(sin_ready, 1)
            nc.scalar.activation(cos[:, :, :], ang_k[:, :, :], ACT.Sin).then_inc(sin_ready, 1)
            for hh in range(6, 14):
                split_high(hh)

            act.wait_ge(used, H_UQ)
            for c in range(TC):
                copy(cn[:, c, 0:Q_LORA], ps[:, 4 + 2 * c, 0:Q_LORA]).then_inc(cn_ready, 1)
                copy(cn[:, c, Q_LORA:], ps[:, 5 + 2 * c, 0:KV_LORA]).then_inc(cn_ready, 1)
            for b in range(3):
                act.wait_ge(c_tr, b + 1)
                for j in (2 * b, 2 * b + 1):
                    src = ps[:, b, (j % 2) * SEQ:(j % 2 + 1) * SEQ]
                    if j < CC:
                        copy(chi[:, j, :], src, scale=gcol[:, G_Q + j:G_Q + j + 1]).then_inc(chi_ready, 1)
                    else:
                        copy(krT[:, :], src).then_inc(chi_ready, 1)
            act.wait_ge(cn_ready, 4)
            nc.scalar.activation(rot[:, 0, :, 0:48], cn[:, 0, 0:Q_LORA].rearrange("p (a b) -> p a b", a=HEADS), ACT.Square,
                                 accum_out=css[:, 0, 0:1]).then_inc(c_ss, 1)
            nc.scalar.activation(rot[:, 1, :, 0:32], cn[:, 0, Q_LORA:].rearrange("p (a b) -> p a b", a=HEADS), ACT.Square,
                                 accum_out=css[:, 1, 0:1]).then_inc(c_ss, 1)
            act.wait_ge(c_ss, 4)
            for b in range(4):
                if b == 2:
                    for hh in range(14, 17):
                        split_high(hh)
                act.wait_ge(qn_done, b + 1)
                copy(qT[:, 2 * b:2 * b + 2, :].rearrange("p a s -> p (a s)"), ps[:, 4 + b, :]).then_inc(qT_ready, 1)
            act.wait_ge(rb_mm, 1)
            copy(rb[:, :], ps[:, 3, 0:SEQ]).then_inc(rb_ready, 1)
            for hh in range(17, 20):
                split_high(hh)
            act.wait_ge(cfac_ready, 1)
            act.wait_ge(rot_tr, 2)
            act.wait_ge(used, H_WO)
            for c in range(TC):
                for n in range(2):
                    copy(v[:, c, n * 512:(n + 1) * 512], ps[:, 2 * c + n, :], scale=cfac[:, 1, c:c + 1]).then_inc(v_ready, 1)
            for b in range(2):
                act.wait_ge(rot_tr, b + 1)
                copy(qrT[:, 2 * b:2 * b + 2, :].rearrange("p a s -> p (a s)"), ps[:, 4 + b, :]).then_inc(qrT_ready, 1)
            for hh in range(20, 24):
                split_high(hh)

            def mla_exp(hd):
                act.wait_ge(max_done, hd + 1)
                if hd >= 2:
                    act.wait_ge(pt_done, hd - 1)
                for c, (a, b) in enumerate(((0, 128), (128, 384))):
                    nc.scalar.activation(prob[:, hd % 2, a:b], ps[:, hd % 3, a:b], ACT.Exp, bias=nmx[:, hd, c:c + 1],
                                         scale=qscale[:, 0, c:c + 1], accum_out=rs[:, hd, c:c + 1]).then_inc(exp_done, 1)

            mla_exp(0)
            for hd in range(HEADS):
                if hd + 1 < HEADS:
                    mla_exp(hd + 1)
                act.wait_ge(pt_done, hd + 1)
                if hd >= 2:
                    act.wait_ge(o_done, hd - 1)
                copy(probT[:, hd % 2, :], ps[:, 3, 0:384]).then_inc(probT_ready, 1)
                act.wait_ge(o_done, hd + 1)
                copy(xhi[:, hd, :], ps[:, hd % 3, 0:SEQ]).then_inc(o_hi, 1)
                if hd >= 2:
                    split_high(22 + hd)
            for hh in range(30, 32):
                split_high(hh)

            def ffn(x, i=0, at_group=None):
                n, nt, base = FFN[x]

                def silu(j):
                    act.wait_ge(used, i * FH + base + 4 * (j + 1))
                    for c in range(nt):
                        if j >= 2 and c == 0:
                            act.wait_ge(gu_tr[x], i * n + j - 1)
                        nc.scalar.activation(gu[:, j % 2, c, :], ps[:, bank_gu(x, c, parity(x, j)), 0:GW], ACT.Silu,
                                             scale=1.0 if x == 2 else rstd[:, 1, c:c + 1]).then_inc(silu_done[x], 1)

                def high(j):
                    act.wait_ge(gu_tr[x], i * n + j + 1)
                    src = ps[:, bank_tr(x, j % 2), 0:2 * nt * P]
                    dst = ehi[:, 2 * j:2 * j + 2, :] if nt == 1 else hhi[:, 2 * j:2 * j + 2, :]
                    copy(dst.rearrange("p a s -> p (a s)"), src).then_inc(h_hi[x], 1)

                for j in range(n):
                    if j >= 1:
                        silu(j - 1)
                    if j >= 2:
                        high(j - 2)
                    for m in range(4):
                        split_high(base + RING + 4 * j + m, i)
                silu(n - 1)
                high(n - 2)
                for f in range(2 * n):
                    if f == 2 * n - 1 and x == 2:
                        act.wait_ge(used, i * FH + H_MOE + FH)
                        for m in range(2):
                            copy(xhi[:, 4 * m:4 * m + 4, P:SEQ], ps[:, 4 + m, :].rearrange("p (a s) -> p a s", a=4)).then_inc(y_hi, 1)
                    split_high(base + RING + 4 * n + f, i)
                    if f == 1:
                        high(n - 1)
                    if f == 17 and x == 2:
                        for b in range(2):
                            act.wait_ge(gathered, i * 2 + 2 + b + 1)
                            for k in range(4 * b, 4 * b + 4):
                                copy(xhi[:, k, 0:P], ps[:, 6 + b, (k % 4) * P:(k % 4 + 1) * P],
                                     scale=gcol[:, G_FFN1 + k:G_FFN1 + k + 1]).then_inc(xe_hi, 1)

            x_high(1, G_FFN0)
            squares(1, 0, xm[:, 0, :])
            act.wait_ge(rstd_ready[1], 1)
            ffn(0)
            ffn(1)

            x_high(2, G_KVSH)
            squares(2, 0, sp[:, :, :].rearrange("p a s -> p (a s)")[:, 0:D])
            for m in range(8):
                split_high(H_SBK + RING + m)
            act.wait_ge(rb_mm, 2)
            copy(rb[:, :], ps[:, 0, 0:SEQ]).then_inc(rb_ready, 1)
            for m in range(8):
                split_high(H_SBV + RING + m)
            act.wait_ge(used, H_SBQ)
            x_high(3, G_ATTN1)
            for c in range(TC):
                for n in range(2):
                    copy(sv[:, c, n * 512:(n + 1) * 512], ps[:, 2 * c + n, :], scale=rstd[:, 2, c:c + 1]).then_inc(sv_ready, 1)
            for m in range(8):
                split_high(H_SBQ + RING + m)

            def four(g):
                return sp[:, 4 * g:4 * g + 4, :], ps[:, 4 * g:4 * g + 4, 0:384]

            for g in range(2):
                act.wait_ge(z_done, 4 * g + 4)
                step(nc.scalar.activation(four(g)[0], four(g)[1], ACT.Abs))
                step(nc.scalar.activation(four(g)[0], four(g)[0], ACT.Exp, scale=-1.0))
            for g in range(2):
                nc.scalar.activation(four(g)[0], four(g)[0], ACT.Ln, bias=one[:, 0:1]).then_inc(ln_done, 1)
            for g in range(2):
                act.wait_ge(c_done, 4 * g + 4)
                nc.scalar.activation(four(g)[0], four(g)[1], ACT.Exp).then_inc(a_ready, 1)
            for g in range(2):
                act.wait_ge(so_done, 4 * g + 4)
                copy(xhi[:, 4 * g:4 * g + 4, :], ps[:, 4 * g:4 * g + 4, 0:SEQ]).then_inc(so_hi, 1)
            for m in range(8):
                split_high(H_SBO + RING + m)

            act.wait_ge(router_ready, 1)
            copy(router_hl[:, :, 0:N_EXP], router[:, :, :]).then_inc(router_ready, 1)
            x_high(4, G_FFN1)
            squares(3, 0, xm[:, 0, :])
            act.wait_ge(lgT_done, 1)
            copy(lgT[0:2 * N_EXP, :], ps[0:2 * N_EXP, 4, 0:SEQ]).then_inc(lgT_ready, 1)
            act.wait_ge(rstd_ready[3], 1)
            act.wait_ge(ss_ready[3], 2)
            copy(xm[:, 1, :], h[:, 1, :], scale=rstd[:, 3, 1:2]).then_inc(xm_ready, 1)
            act.wait_ge(gap_ready, 1)
            nc.scalar.activation(den[:, :], best[:, :], ACT.Exp).then_inc(gap_exp, 1)
            for b in range(2):
                act.wait_ge(gathered, b + 1)
                for k in range(4 * b, 4 * b + 4):
                    copy(xhi[:, k, 0:P], ps[:, 6 + b, (k % 4) * P:(k % 4 + 1) * P],
                         scale=gcol[:, G_FFN1 + k:G_FFN1 + k + 1]).then_inc(xe_hi, 1)
            act.wait_ge(sel_tr, 1)
            copy(selT[:, :], ps[:, 6, 0:SEQ]).then_inc(selT_ready, 1)
            act.wait_ge(items_ready, 2)
            n_items = act.value_load(n_items_i[0:1, 0:1], min_val=N_EXP, max_val=ITEMS - 1)
            with act.Fori(0, n_items) as i:
                nc.scalar.activation(silu_scratch[:, :], one[:, :], ACT.Silu)
                ffn(2, i)
                act.wait_ge(sel_tr, i + 2)
                copy(selT[:, :], ps[:, 6, 0:SEQ]).then_inc(selT_ready, 1)

            act.wait_ge(gu_tr[2], n_items * NG)
            act.dma_start(gbc, t["final_norm"].partition_broadcast(P)).then_inc(gbc_in, 16)
            for c in range(TC):
                act.wait_ge(h_ready[4], n_items * 4 + 2 * c + 2)
                squares(4, c, yout[:, c, :])

        @block.vector
        def _(dve):
            V = nc.vector
            steps = [0]

            def step(ins):
                steps[0] += 1
                ins.then_inc(dve_step, 1)
                dve.wait_ge(dve_step, steps[0])

            def split_low(hh, i=0):
                dve.wait_ge(hi_made, i * FH + hh + 1)
                w = half_width(hh)
                V.tensor_tensor(w_lo(hh)[:, 0:w], raw_half(hh), w_hi(hh)[:, 0:w].bitcast(F32), ALU.subtract).then_inc(lo_made, 1)

            def squares(n, c, junk):
                V.tensor_tensor_reduce(out=junk, in0=h[:, c, :], in1=h[:, c, :], scale=1.0, scalar=0.0,
                                       op0=ALU.mult, op1=ALU.add, accum_out=ss[:, n, c:c + 1]).then_inc(ss_ready[n], 1)

            def row_factors(n, col):
                for c in range(TC):
                    V.tensor_scalar(diag[:, c, :] if n == 0 else sp[:, c, 0:P], ident[:, :], col(c), None, ALU.mult).then_inc(rb_diag, 1)

            def x_low(n, gain):
                for b in range(4):
                    dve.wait_ge(xhi_ready[n], 2 * b + 2)
                    for k in (2 * b, 2 * b + 1):
                        V.scalar_tensor_tensor(out=xlo[:, k, :], in0=ps[:, X_BANKS[n][b], (k % 2) * SEQ:(k % 2 + 1) * SEQ],
                                               scalar=gcol[:, gain + k:gain + k + 1], in1=xhi[:, k, :].bitcast(F32),
                                               op0=ALU.mult, op1=ALU.subtract).then_inc(xlo_ready[n], 1)

            dve.wait_ge(pos_in, 32)
            dve.wait_ge(consts, 1)
            step(V.tensor_copy(posf[:, :], posi[:, :]))
            for c in range(TC):
                last = V.tensor_scalar(ang[:, c, :], invf[:, :], posf[:, c:c + 1], None, ALU.mult)
            step(last)
            PI, MAGIC = 3.1415925, 12582912.0
            C1 = float(np.float32(6.28125))
            C2 = float(np.float32(np.float32(2 * np.pi - C1).view(np.uint32) & np.uint32(0xFFFFF000)).astype(np.uint32).view(np.float32))
            C3 = float(np.float32(2 * np.pi - C1 - C2))
            step(V.tensor_scalar(ang_k[:, :, :], ang[:, :, :], 1.0 / (2 * np.pi), MAGIC, ALU.mult, ALU.add))
            step(V.tensor_scalar(ang_k[:, :, :], ang_k[:, :, :], MAGIC, None, ALU.subtract))
            for part in (C1, C2, C3):
                step(V.scalar_tensor_tensor(out=ang[:, :, :], in0=ang_k[:, :, :], scalar=-part, in1=ang[:, :, :],
                                            op0=ALU.mult, op1=ALU.add))
            step(V.tensor_scalar(ang_k[:, :, :], ang[:, :, :], PI, -2 * np.pi, ALU.is_gt, ALU.mult))
            step(V.tensor_tensor(ang[:, :, :], ang[:, :, :], ang_k[:, :, :], ALU.add))
            step(V.tensor_scalar(ang_k[:, :, :], ang[:, :, :], -PI, 2 * np.pi, ALU.is_lt, ALU.mult))
            step(V.tensor_tensor(ang[:, :, :], ang[:, :, :], ang_k[:, :, :], ALU.add))
            step(V.tensor_scalar(ang_k[:, :, :], ang[:, :, :], np.pi / 2, None, ALU.add))
            over_pi = rt[:, :, 0, :]
            step(V.tensor_scalar(over_pi, ang_k[:, :, :], PI, -2 * np.pi, ALU.is_gt, ALU.mult))
            step(V.tensor_tensor(ang_k[:, :, :], ang_k[:, :, :], over_pi, ALU.add))
            V.tensor_scalar(ang[:, :, :], ang[:, :, :], PI, -PI, ALU.min, ALU.max).then_inc(rc_ready, 1)
            V.tensor_scalar(ang_k[:, :, :], ang_k[:, :, :], PI, -PI, ALU.min, ALU.max).then_inc(rc_ready, 1)
            V.tensor_copy(ident_r[:, :], ident[:, :])
            step(V.tensor_copy(hide_r[:, :], hide[:, :]))
            dve.wait_ge(g_ready, 1)
            x_low(0, G_ATTN0)
            split_low(0)
            split_low(1)
            for n in range(2):
                dve.wait_ge(x_in[n], 16)
            squares(0, 1, xn[:, 1, :])
            for hh in range(2, 14):
                split_low(hh)

            dve.wait_ge(cn_ready, 4)
            dve.wait_ge(rstd_ready[0], 1)
            for c in range(TC):
                V.tensor_scalar(kr[:, c, ROPE:2 * ROPE], ps[:, 5 + 2 * c, KV_LORA:KV_LORA + ROPE], rstd[:, 0, c:c + 1], None,
                                ALU.mult).then_inc(kr_scaled, 1)

            def rope(x1, x2, co, si, t1, t2, o1, o2, done=None):
                step(V.tensor_tensor(t1, x1, co, ALU.mult))
                step(V.tensor_tensor(t2, x2, si, ALU.mult))
                step(V.tensor_tensor(o1, t1, t2, ALU.subtract))
                step(V.tensor_tensor(t1, x1, si, ALU.mult))
                step(V.tensor_tensor(t2, x2, co, ALU.mult))
                if done is None:
                    step(V.tensor_tensor(o2, t1, t2, ALU.add))
                else:
                    V.tensor_tensor(o2, t1, t2, ALU.add).then_inc(done, 1)

            dve.wait_ge(sin_ready, 2)
            R2 = ROPE // 2
            dve.wait_ge(kr_scaled, 2)
            x = kr[:, :, ROPE:2 * ROPE]
            rope(x[:, :, 0:R2], x[:, :, R2:ROPE], cos[:, :, :], sin[:, :, :], rt[:, 0, 0:2, :], rt[:, 1, 0:2, :],
                 kr[:, :, 0:R2], kr[:, :, R2:ROPE])
            V.tensor_copy(kr[:, :, ROPE:2 * ROPE], kr[:, :, 0:ROPE]).then_inc(kr_ready, 1)
            for b in range(3):
                dve.wait_ge(chi_ready, 2 * b + 2)
                for j in range(2 * b, min(2 * b + 2, CC)):
                    V.scalar_tensor_tensor(out=clo[:, j, :], in0=ps[:, b, (j % 2) * SEQ:(j % 2 + 1) * SEQ],
                                           scalar=gcol[:, G_Q + j:G_Q + j + 1], in1=chi[:, j, :].bitcast(F32),
                                           op0=ALU.mult, op1=ALU.subtract).then_inc(clo_ready, 1)
            V.tensor_tensor_reduce(out=xn[:, 0, 0:Q_LORA], in0=cn[:, 1, 0:Q_LORA], in1=cn[:, 1, 0:Q_LORA], scale=1.0, scalar=0.0,
                                   op0=ALU.mult, op1=ALU.add, accum_out=css[:, 0, 1:2]).then_inc(c_ss, 1)
            V.tensor_tensor_reduce(out=xn[:, 0, Q_LORA:Q_LORA + KV_LORA], in0=cn[:, 1, Q_LORA:], in1=cn[:, 1, Q_LORA:], scale=1.0,
                                   scalar=0.0, op0=ALU.mult, op1=ALU.add, accum_out=css[:, 1, 1:2]).then_inc(c_ss, 1)
            for hh in range(14, 17):
                split_low(hh)
            dve.wait_ge(cfac_ready, 1)
            row_factors(0, lambda c: cfac[:, 1, c:c + 1])
            dve.wait_ge(used, H_UKV)
            for hh in range(17, 20):
                split_low(hh)
            x = ps[:, 0:2, :].rearrange("p c (a r) -> p c a r", r=ROPE)
            for c in range(TC):
                co = cos[:, c, :].unsqueeze(1).to_broadcast([P, HEADS, R2])
                si = sin[:, c, :].unsqueeze(1).to_broadcast([P, HEADS, R2])
                rope(x[:, c, :, 0:R2], x[:, c, :, R2:ROPE], co, si, rt[:, 0, :, :], rt[:, 1, :, :],
                     rot[:, c, :, 0:R2], rot[:, c, :, R2:ROPE], rot_ready)
                dve.wait_ge(rot_ready, c + 1)
            dve.wait_ge(rb_ready, 1)
            for b in range(4):
                dve.wait_ge(kn_done, b + 1)
                V.tensor_tensor(kT[:, 2 * b:2 * b + 2, :], ps[:, 4 + b, :].rearrange("p (a s) -> p a s", a=2),
                                rb[:, :].unsqueeze(1).to_broadcast([P, 2, SEQ]), ALU.mult).then_inc(kT_ready, 1)
            for hh in range(20, 24):
                split_low(hh)

            def mla_max(hd):
                dve.wait_ge(s_done, hd + 1)
                V.tensor_reduce(mx[:, hd, 0:1], ps[:, hd % 3, 0:128], AX, ALU.max)
                step(V.tensor_reduce(mx[:, hd, 1:2], ps[:, hd % 3, 128:384], AX, ALU.max))
                V.tensor_tensor(nmx[:, hd, :], mx[:, hd, :], qscale[:, 1, :], ALU.mult).then_inc(max_done, 1)

            def mla_low(hd):
                dve.wait_ge(o_hi, hd + 1)
                V.tensor_tensor(xlo[:, hd, :], ps[:, hd % 3, 0:SEQ], xhi[:, hd, :].bitcast(F32), ALU.subtract).then_inc(o_lo, 1)

            mla_max(0)
            mla_max(1)
            for hd in range(HEADS):
                dve.wait_ge(exp_done, 2 * hd + 2)
                step(V.reciprocal(rr[:, hd, :], rs[:, hd, :]))
                for c, (a, b) in enumerate(((0, 128), (128, 384))):
                    V.tensor_scalar(prob[:, hd % 2, a:b], prob[:, hd % 2, a:b], rr[:, hd, c:c + 1], None, ALU.mult).then_inc(pn_ready, 1)
                if hd >= 1:
                    mla_low(hd - 1)
                if hd + 2 < HEADS:
                    mla_max(hd + 2)
                if hd >= 2:
                    split_low(22 + hd)
            mla_low(HEADS - 1)
            split_low(30)

            def residual(ready, bank):
                for n in range(2):
                    for c in range(TC):
                        hv = h[:, c, n * 512:(n + 1) * 512]
                        V.tensor_tensor(hv, ps[:, bank(c, n), :], hv, ALU.add).then_inc(ready, 1)

            dve.wait_ge(used, H_FFN)
            residual(h_ready[1], lambda c, n: 4 + 2 * c + n)

            def ffn(x, i=0):
                n, nt, base = FFN[x]

                def gate(j):
                    for c in range(nt):
                        dve.wait_ge(silu_done[x], (i * n + j) * nt + c + 1)
                        g = gu[:, j % 2, c, :]
                        up = ps[:, bank_gu(x, c, parity(x, j)), GW:2 * GW]
                        if x == 2:
                            V.tensor_tensor(g, up, g, ALU.mult).then_inc(gated[x], 1)
                        else:
                            V.scalar_tensor_tensor(out=g, in0=up, scalar=rstd[:, 1, c:c + 1], in1=g,
                                                   op0=ALU.mult, op1=ALU.mult).then_inc(gated[x], 1)

                def low(j):
                    dve.wait_ge(h_hi[x], i * n + j + 1)
                    src = ps[:, bank_tr(x, j % 2), 0:2 * nt * P]
                    hi = ehi[:, 2 * j:2 * j + 2, :] if nt == 1 else hhi[:, 2 * j:2 * j + 2, :]
                    lo = elo[:, 2 * j:2 * j + 2, :] if nt == 1 else hlo[:, 2 * j:2 * j + 2, :]
                    V.tensor_tensor(lo.rearrange("p a s -> p (a s)"), src, hi.bitcast(F32).rearrange("p a s -> p (a s)"),
                                    ALU.subtract).then_inc(h_lo[x], 1)

                for j in range(n):
                    if j >= 1:
                        gate(j - 1)
                    if j >= 2:
                        low(j - 2)
                    for m in range(4):
                        split_low(base + RING + 4 * j + m, i)
                    if x == 2 and j == 4:
                        V.tensor_copy(gt[:, :], g_tab[:, bass.ds(i, 1), :].rearrange("p a c -> p (a c)")).then_inc(gt_ready, 1)
                        V.tensor_copy(pm[:, :, :], pm_tab[:, bass.ds(i + 1, 1), :, :].rearrange("p a b c -> p (a b) c")).then_inc(pm_ready, 1)
                        dve.wait_ge(pm_ready, i + 1)
                        dve.wait_ge(sel_tr, i + 1)
                        for c in range(TC):
                            V.tensor_scalar(sel[:, c, :], iota[:, :], pm[:, 0, c:c + 1], pm[:, 1, c:c + 1],
                                            ALU.is_equal, ALU.mult).then_inc(sel_ready, 1)
                gate(n - 1)
                low(n - 2)
                for f in range(2 * n):
                    if f == 2 * n - 1 and x == 2:
                        for m in range(2):
                            dve.wait_ge(y_hi, i * 2 + m + 1)
                            V.tensor_tensor(xlo[:, 4 * m:4 * m + 4, P:SEQ], ps[:, 4 + m, :].rearrange("p (a s) -> p a s", a=4),
                                            xhi[:, 4 * m:4 * m + 4, P:SEQ].bitcast(F32), ALU.subtract).then_inc(y_lo, 1)
                    split_low(base + RING + 4 * n + f, i)
                    if f == 1:
                        low(n - 1)
                    if f == 17 and x == 2:
                        gathered_low(i + 1)

            def gathered_low(item):
                for b in range(2):
                    dve.wait_ge(xe_hi, item * KD + 4 * b + 4)
                    for k in range(4 * b, 4 * b + 4):
                        V.scalar_tensor_tensor(out=xlo[:, k, 0:P], in0=ps[:, 6 + b, (k % 4) * P:(k % 4 + 1) * P],
                                               scalar=gcol[:, G_FFN1 + k:G_FFN1 + k + 1], in1=xhi[:, k, 0:P].bitcast(F32),
                                               op0=ALU.mult, op1=ALU.subtract).then_inc(xe_lo, 1)

            x_low(1, G_FFN0)
            split_low(31)
            squares(1, 1, xm[:, 1, :])
            dve.wait_ge(rstd_ready[1], 1)
            for x in range(2):
                ffn(x)
                dve.wait_ge(used, FFN[x][2] + 6 * FFN[x][0])
                residual(h_ready[2], lambda c, n: bank_out(x, c, n))

            x_low(2, G_KVSH)
            squares(2, 1, sp[:, :, :].rearrange("p a s -> p (a s)")[:, D:2 * D])
            for m in range(8):
                split_low(H_SBK + RING + m)
            dve.wait_ge(rstd_ready[2], 1)
            row_factors(1, lambda c: rstd[:, 2, c:c + 1])
            for b in range(4):
                if b == 0:
                    dve.wait_ge(rb_ready, 2)
                    dve.wait_ge(used, H_SBV)
                V.tensor_tensor(skT[:, 2 * b:2 * b + 2, :], ps[:, 4 + b, :].rearrange("p (a s) -> p a s", a=2),
                                rb[:, :].unsqueeze(1).to_broadcast([P, 2, SEQ]), ALU.mult).then_inc(skT_ready, 1)
            for m in range(8):
                split_low(H_SBV + RING + m)
            x_low(3, G_ATTN1)
            for m in range(8):
                split_low(H_SBQ + RING + m)
            dve.wait_ge(used, H_SBO)
            for b in range(4):
                V.scalar_tensor_tensor(out=sqT[:, 2 * b:2 * b + 2, :], in0=ps[:, b, :].rearrange("p (a s) -> p a s", a=2),
                                       scalar=SB_SCALE, in1=rb[:, :].unsqueeze(1).to_broadcast([P, 2, SEQ]),
                                       op0=ALU.mult, op1=ALU.mult).then_inc(sqT_ready, 1)

            def four(g):
                return sp[:, 4 * g:4 * g + 4, :], ps[:, 4 * g:4 * g + 4, 0:384]

            for g in range(2):
                dve.wait_ge(ln_done, g + 1)
                V.scalar_tensor_tensor(out=four(g)[0], in0=four(g)[1], scalar=0.0, in1=four(g)[0],
                                       op0=ALU.max, op1=ALU.add).then_inc(sp_ready, 1)
            for g in range(2):
                dve.wait_ge(so_hi, g + 1)
                V.tensor_tensor(xlo[:, 4 * g:4 * g + 4, :], ps[:, 4 * g:4 * g + 4, 0:SEQ],
                                xhi[:, 4 * g:4 * g + 4, :].bitcast(F32), ALU.subtract).then_inc(so_lo, 1)
            V.memset(router_hl[:, :, :].bitcast(F32), 0.0).then_inc(router_ready, 1)
            for m in range(7):
                split_low(H_SBO + RING + m)
            dve.wait_ge(router_ready, 2)
            V.tensor_tensor(router_hl[:, :, N_EXP:2 * N_EXP], router[:, :, :], router_hl[:, :, 0:N_EXP].bitcast(F32),
                            ALU.subtract).then_inc(router_ready, 1)
            V.tensor_tensor(fold[:, :], ident[:, 0:N_EXP], ident[:, N_EXP:2 * N_EXP], ALU.add).then_inc(router_ready, 1)
            step(V.tensor_scalar(rank[:, :], iota[:, 0:N_EXP], -1.0, float(N_EXP), ALU.mult, ALU.add))
            dve.wait_ge(used, H_MOE)
            residual(h_ready[3], lambda c, n: 2 * c + n)

            x_low(4, G_FFN1)
            squares(3, 1, xm[:, 1, :])
            split_low(H_SBO + RING + 7)
            dve.wait_ge(rstd_ready[3], 1)
            dve.wait_ge(ss_ready[3], 2)
            V.tensor_scalar(xm[:, 0, :], h[:, 0, :], rstd[:, 3, 0:1], None, ALU.mult).then_inc(xm_ready, 1)
            dve.wait_ge(lg_done, 1)
            for c in range(TC):
                last = V.tensor_scalar(lg[:, c, :], ps[:, 5, c * N_EXP:(c + 1) * N_EXP], rstd[:, 3, c:c + 1], None, ALU.mult)
            step(last)

            def per_token(a):
                return a.unsqueeze(2).to_broadcast([P, TC, N_EXP])

            rank_b = rank[:, :].unsqueeze(1).to_broadcast([P, TC, N_EXP])

            def pick(logits, largest, chosen):
                step(V.tensor_reduce(largest, logits, AX, ALU.max))
                step(V.tensor_tensor(sc8[:, :, :], logits, per_token(largest), ALU.is_equal))
                step(V.tensor_tensor(sc8[:, :, :], sc8[:, :, :], rank_b, ALU.mult))
                step(V.tensor_reduce(best[:, :], sc8[:, :, :], AX, ALU.max))
                step(V.tensor_tensor(chosen, sc8[:, :, :], per_token(best[:, :]), ALU.is_equal))

            pick(lg[:, :, :], m1[:, :], oh1[:, :, :])
            step(V.scalar_tensor_tensor(out=lg2[:, :, :], in0=oh1[:, :, :], scalar=NEG, in1=lg[:, :, :],
                                        op0=ALU.mult, op1=ALU.add))
            pick(lg2[:, :, :], m2[:, :], oh2[:, :, :])
            V.tensor_tensor(msk[:, :, :], oh1[:, :, :], oh2[:, :, :], ALU.add).then_inc(msk_ready, 1)
            V.tensor_tensor(best[:, :], m2[:, :], m1[:, :], ALU.subtract).then_inc(gap_ready, 1)
            dve.wait_ge(pos_done, 1)
            step(V.tensor_copy(posn[:, :, :].rearrange("p c e -> p (c e)"), ps[:, 5, 16:32]))
            for c in range(TC):
                V.tensor_scalar(sel[:, c, :], iota[:, :], posn[:, c, 0:1], msk[:, c, 0:1],
                                ALU.is_equal, ALU.mult).then_inc(sel_ready, 1)
            step(V.tensor_copy(cnt[:, :], ps[:, 5, 32:40]))
            step(V.tensor_scalar(ovf[:, :], cnt[:, :], float(P), None, ALU.is_gt))
            step(V.tensor_tensor_scan(csum[:, :], ones[:, 0:N_EXP], ovf[:, :], 0.0, ALU.mult, ALU.add))
            for r in range(3):
                last = V.tensor_scalar(selr[:, r, :], csum[:, :], float(r + 1), None, ALU.is_equal)
            step(last)
            step(V.tensor_tensor(selr[:, :, :], selr[:, :, :], ovf[:, :].unsqueeze(1).to_broadcast([P, 3, N_EXP]), ALU.mult))
            step(V.tensor_copy(tf[:, :], iota[:, 0:ITEMS]))
            step(V.memset(tf[:, N_EXP:ITEMS], 0.0))
            step(V.tensor_tensor(prod[:, :, :], selr[:, :, :], iota[:, 0:N_EXP].unsqueeze(1).to_broadcast([P, 3, N_EXP]), ALU.mult))
            step(V.tensor_reduce(tf[:, N_EXP:N_EXP + 3], prod[:, :, :], AX, ALU.add))
            V.tensor_copy(item_expert[:, :], tf[:, :]).then_inc(items_ready, 1)
            V.tensor_scalar(n_items_i[:, :], csum[:, N_EXP - 1:N_EXP], float(N_EXP), None, ALU.add).then_inc(items_ready, 1)
            gathered_low(0)
            dve.wait_ge(gap_exp, 1)
            step(V.tensor_scalar(m1[:, :], den[:, :], 1.0, None, ALU.add))
            step(V.reciprocal(m1[:, :], m1[:, :]))
            step(V.tensor_tensor(m2[:, :], den[:, :], m1[:, :], ALU.mult))
            step(V.tensor_tensor(oh1[:, :, :], oh1[:, :, :], per_token(m1[:, :]), ALU.mult))
            step(V.tensor_tensor(oh2[:, :, :], oh2[:, :, :], per_token(m2[:, :]), ALU.mult))
            step(V.tensor_tensor(gates[:, :, :], oh1[:, :, :], oh2[:, :, :], ALU.add))
            for c in range(TC):
                V.tensor_copy(pm_tab[:, 0:N_EXP, 0, c], posn[:, c, :])
                V.tensor_copy(pm_tab[:, 0:N_EXP, 1, c], msk[:, c, :])
                V.tensor_copy(g_tab[:, 0:N_EXP, c], gates[:, c, :])
            V.memset(pm_tab[:, N_EXP:ITEMS, :, :], 0.0).then_inc(h_ready[4], 4)
            step(V.memset(g_tab[:, N_EXP:ITEMS, :], 0.0))
            for c in range(TC):
                for src, dst in ((posn, pm_tab[:, N_EXP:N_EXP + 3, 0, c]), (msk, pm_tab[:, N_EXP:N_EXP + 3, 1, c]),
                                 (gates, g_tab[:, N_EXP:N_EXP + 3, c])):
                    step(V.tensor_tensor(prod[:, :, :], selr[:, :, :], src[:, c, :].unsqueeze(1).to_broadcast([P, 3, N_EXP]), ALU.mult))
                    step(V.tensor_reduce(dst, prod[:, :, :], AX, ALU.add))
                step(V.tensor_scalar(pm_tab[:, N_EXP:N_EXP + 3, 0, c], pm_tab[:, N_EXP:N_EXP + 3, 0, c], -float(P), None, ALU.add))
            dve.wait_ge(items_ready, 2)
            n_items = dve.value_load(n_items_i[0:1, 0:1], min_val=N_EXP, max_val=ITEMS - 1)
            with dve.Fori(0, n_items) as i:
                ffn(2, i)
                dve.wait_ge(gt_ready, i + 1)
                for c in range(TC):
                    for n in range(2):
                        dve.wait_ge(scattered, i * 4 + 2 * c + n + 1)
                        hv = h[:, c, n * 512:(n + 1) * 512]
                        V.scalar_tensor_tensor(out=hv, in0=ps[:, 2 + 2 * c + n, :], scalar=gt[:, c:c + 1], in1=hv,
                                               op0=ALU.mult, op1=ALU.add).then_inc(h_ready[4], 1)

            dve.wait_ge(rstd_ready[4], 1)
            dve.wait_ge(gbc_in, 16)
            for c in range(TC):
                V.scalar_tensor_tensor(out=yout[:, c, :], in0=h[:, c, :], scalar=rstd[:, 4, c:c + 1], in1=gbc,
                                       op0=ALU.mult, op1=ALU.mult).then_inc(y_ready, 1)

        @block.tensor
        def _(pe):
            def mm3(o, a_hi, a_lo, b_hi, b_lo, start, stop):
                pe.matmul(o, a_hi, b_hi, start=start, stop=False, skip_group_check=True)
                pe.matmul(o, a_lo, b_hi, start=False, stop=False, skip_group_check=True)
                return pe.matmul(o, a_hi, b_lo, start=False, stop=stop, skip_group_check=True)

            def mm(o, a, b, start, stop):
                return pe.matmul(o, a, b, start=start, stop=stop, skip_group_check=True)

            def transpose_x(n, first, second):
                for b in range(4):
                    if b % 2 == 0:
                        pe.wait_ge(*(second if b else first))
                    for k in (2 * b, 2 * b + 1):
                        for c in range(TC):
                            last = pe.transpose(ps[:, X_BANKS[n][b], (k % 2) * SEQ + c * P:(k % 2) * SEQ + (c + 1) * P],
                                                h[:, c, k * P:(k + 1) * P], ident[:, :])
                    last.then_inc(x_tr[n], 1)

            def tokens_out(k, hh, banks, width=512):
                for c in range(TC):
                    for n in range(2):
                        w = slice(n * 512, (n + 1) * 512)
                        last = mm3(ps[:, banks[c][n], :], xhi[:, k, c * P:(c + 1) * P], xlo[:, k, c * P:(c + 1) * P],
                                   w_hi(hh)[:, w], w_lo(hh)[:, w], k == 0, k == KD - 1)
                last.then_inc(used, 1)

            def features_out(k, hh, bank0):
                for hd in range(HEADS):
                    w = slice(hd * P, (hd + 1) * P)
                    last = mm3(ps[:, bank0 + hd // 2, (hd % 2) * SEQ:(hd % 2 + 1) * SEQ], w_hi(hh)[:, w], w_lo(hh)[:, w],
                               xhi[:, k, :], xlo[:, k, :], k == 0 and hd % 2 == 0, k == KD - 1)
                last.then_inc(used, 1)

            pe.wait_ge(consts, 1)
            transpose_x(0, (x_in[0], 16), (x_in[1], 16))
            pe.wait_ge(small_in, 16 * 7)
            pe.transpose(ps[:, 7, 0:G_ALL], grow[0:G_ALL, :], ident[0:G_ALL, 0:G_ALL]).then_inc(g_tr, 1)
            pe.wait_ge(g_ready, 1)
            for k in range(KD):
                pe.wait_ge(xlo_ready[0], k + 1)
                pe.wait_ge(lo_made, H_DOWN + k + 1)
                for c in range(TC):
                    for n, (a, b) in enumerate(((0, Q_LORA), (Q_LORA, DOWN))):
                        last = mm3(ps[:, 4 + 2 * c + n, 0:b - a], xhi[:, k, c * P:(c + 1) * P], xlo[:, k, c * P:(c + 1) * P],
                                   w_hi(H_DOWN + k)[:, a:b], w_lo(H_DOWN + k)[:, a:b], k == 0, k == KD - 1)
                last.then_inc(used, 1)
            pe.wait_ge(cn_ready, 4)
            for b in range(3):
                for j in (2 * b, 2 * b + 1):
                    if j == CC:
                        pe.wait_ge(kr_ready, 1)
                    for c in range(TC):
                        src = cn[:, c, j * P:(j + 1) * P] if j < CC else kr[:, c, :]
                        last = pe.transpose(ps[:, b, (j % 2) * SEQ + c * P:(j % 2) * SEQ + (c + 1) * P], src, ident[:, :])
                last.then_inc(c_tr, 1)
            pe.wait_ge(clo_ready, CC)
            pe.wait_ge(chi_ready, CC + 1)
            for g in range(2):
                pe.wait_ge(lo_made, H_UQ + 3 * g + 3)
                for hd in range(4 * g, 4 * g + 4):
                    for k in range(3):
                        hh = H_UQ + 3 * g + k
                        w = slice((hd % 4) * QH, (hd % 4) * QH + P)
                        last = mm3(ps[:, 4 + hd // 2, (hd % 2) * SEQ:(hd % 2 + 1) * SEQ], w_hi(hh)[:, w], w_lo(hh)[:, w],
                                   chi[:, k, :], clo[:, k, :], k == 0 and hd % 2 == 0, k == 2)
                    if hd % 2:
                        last.then_inc(qn_done, 1)
                for c in range(TC):
                    for k in range(3):
                        hh = H_UQ + 3 * g + k
                        r_hi, r_lo = (f(hh)[:, 0:4 * QH].rearrange("p (a r) -> p a r", r=QH)[:, :, P:QH] for f in (w_hi, w_lo))
                        last = mm3(ps[:, c, g * 256:(g + 1) * 256].rearrange("p (a r) -> p a r", r=ROPE),
                                   chi[:, k, c * P:(c + 1) * P], clo[:, k, c * P:(c + 1) * P], r_hi, r_lo,
                                   k == 0 and g == 0, k == 2)
                last.then_inc(used, 3)
            pe.wait_ge(rb_diag, 2)
            for c in range(TC):
                last = mm(ps[:, 3, c * P:(c + 1) * P], ones[:, :], diag[:, c, :], c == 0, c == TC - 1)
            last.then_inc(rb_mm, 1)
            for hd in range(HEADS):
                if hd % 4 == 0:
                    pe.wait_ge(lo_made, H_UKV + hd // 2 + 2)
                if hd % 2 == 0:
                    pe.wait_ge(qT_ready, hd // 2 + 1)
                for k in range(2):
                    hh = H_UKV + 2 * (hd // 4) + k
                    w = slice((hd % 4) * 2 * P, (hd % 4) * 2 * P + P)
                    last = mm3(ps[:, 4 + hd // 2, (hd % 2) * SEQ:(hd % 2 + 1) * SEQ], w_hi(hh)[:, w], w_lo(hh)[:, w],
                               chi[:, 3 + k, :], clo[:, 3 + k, :], k == 0 and hd % 2 == 0, k == 1)
                if hd % 2:
                    last.then_inc(kn_done, 1)
            pe.wait_ge(rot_ready, 2)
            pe.wait_ge(rb_ready, 1)
            for g in range(2):
                for c in range(TC):
                    for k in range(2):
                        hh = H_UKV + 2 * g + k
                        v_hi, v_lo = (f(hh).rearrange("p (a r) -> p a r", r=2 * P)[:, :, P:2 * P] for f in (w_hi, w_lo))
                        last = mm3(ps[:, 2 * c + g, :].rearrange("p (a r) -> p a r", r=P),
                                   chi[:, 3 + k, c * P:(c + 1) * P], clo[:, 3 + k, c * P:(c + 1) * P], v_hi, v_lo,
                                   k == 0, k == 1)
                last.then_inc(used, 2)
            for b in range(2):
                pe.wait_ge(kT_ready, b + 1)
                for pair in (2 * b, 2 * b + 1):
                    for c in range(TC):
                        last = pe.transpose(ps[:, 4 + b, (pair % 2) * SEQ + c * P:(pair % 2) * SEQ + (c + 1) * P],
                                            rot[:, c, 2 * pair:2 * pair + 2, :].rearrange("p a r -> p (a r)"), ident[:, :])
                last.then_inc(rot_tr, 1)

            def scores(hd):
                b = hd % 3
                if hd >= 3:
                    pe.wait_ge(o_lo, hd - 2)
                lo = (hd % 2) * ROPE
                for c, (a, e) in enumerate(((0, 128), (128, 384))):
                    mm(ps[:, b, a:e], qT[:, hd, c * P:(c + 1) * P], kT[:, hd, 0:e - a], c == 0, False)
                for c, (a, e) in enumerate(((0, 128), (128, 384))):
                    mm(ps[:, b, a:e], qrT[lo:lo + ROPE, hd // 2, c * P:(c + 1) * P], krT[lo:lo + ROPE, 0:e - a], False, False)
                for a in (CHUNK, 128 + 192):
                    last = mm(ps[:, b, a:a + CHUNK], half_mask[0:1, 0:P], half_mask[0:1, P:P + CHUNK], False, True)
                last.then_inc(s_done, 1)

            def outputs(hd):
                pe.wait_ge(probT_ready, hd + 1)
                o = ps[:, hd % 3, :]
                mm(o[:, 0:SEQ], v[:, 0, hd * P:(hd + 1) * P], probT[:, hd % 2, 0:SEQ], True, False)
                mm(o[:, P:SEQ], v[:, 1, hd * P:(hd + 1) * P], probT[:, hd % 2, SEQ:384], False, True).then_inc(o_done, 1)

            pe.wait_ge(qrT_ready, 2)
            pe.wait_ge(kT_ready, 4)
            pe.wait_ge(v_ready, 4)
            scores(0)
            scores(1)
            for hd in range(HEADS):
                pe.wait_ge(pn_ready, 2 * hd + 2)
                if hd >= 1:
                    pe.wait_ge(probT_ready, hd)
                for n in range(3):
                    last = pe.transpose(ps[:, 3, n * P:(n + 1) * P], prob[:, hd % 2, n * P:(n + 1) * P], ident[:, :])
                last.then_inc(pt_done, 1)
                if hd + 2 < HEADS:
                    scores(hd + 2)
                outputs(hd)
                if hd >= 1:
                    pe.wait_ge(o_lo, hd)
                    pe.wait_ge(lo_made, H_WO + hd)
                    tokens_out(hd - 1, H_WO + hd - 1, ((4, 5), (6, 7)))
            pe.wait_ge(o_lo, HEADS)
            pe.wait_ge(lo_made, H_WO + HEADS)
            tokens_out(HEADS - 1, H_WO + HEADS - 1, ((4, 5), (6, 7)))

            def ffn(x, i=0):
                n, nt, base = FFN[x]

                def products(j):
                    if j >= 2:
                        pe.wait_ge(gated[x], (i * n + j - 1) * nt)
                    for m in range(4):
                        hh = base + 4 * j + m
                        pe.wait_ge(lo_made, i * FH + hh + 1)
                        if x == 0 and j == 0:
                            pe.wait_ge(xlo_ready[1], 2 * m + 2)
                        for c in range(nt):
                            for kk in range(2):
                                k = 2 * m + kk
                                w = slice(kk * 512, (kk + 1) * 512)
                                last = mm3(ps[:, bank_gu(x, c, parity(x, j)), :],
                                           xhi[:, k, c * P:(c + 1) * P], xlo[:, k, c * P:(c + 1) * P],
                                           w_hi(hh)[:, w], w_lo(hh)[:, w], k == 0, k == KD - 1)
                        last.then_inc(used, 1)

                def transposes(j):
                    pe.wait_ge(gated[x], (i * n + j + 1) * nt)
                    if j >= 2:
                        pe.wait_ge(h_lo[x], i * n + j - 1)
                    for b in range(2):
                        for c in range(nt):
                            o = (b * nt + c) * P
                            last = pe.transpose(ps[:, bank_tr(x, j % 2), o:o + P], gu[:, j % 2, c, b * P:(b + 1) * P], ident[:, :])
                    last.then_inc(gu_tr[x], 1)

                for j in range(n):
                    if x == 1 and j == 1:
                        pe.wait_ge(h_ready[2], 4)
                    products(j)
                    if j == 1 and x == 2:
                        pe.wait_ge(h_ready[4], i * 4 + 4)
                    if j >= 1:
                        transposes(j - 1)
                hi, lo = (ehi, elo) if nt == 1 else (hhi, hlo)
                for f in range(2 * n):
                    hh = base + 4 * n + f
                    pe.wait_ge(lo_made, i * FH + hh + 1)
                    if f % 2 == 0:
                        pe.wait_ge(h_lo[x], i * n + f // 2 + 1)
                    for c in range(nt):
                        for m in range(2):
                            w = slice(m * 512, (m + 1) * 512)
                            last = mm3(ps[:, bank_out(x, c, m), :], hi[:, f, c * P:(c + 1) * P], lo[:, f, c * P:(c + 1) * P],
                                       w_hi(hh)[:, w], w_lo(hh)[:, w], f == 0, f == 2 * n - 1)
                    last.then_inc(used, 1)
                    if f == 1:
                        transposes(n - 1)
                    if f == 11 and x == 2:
                        gather(i + 1)

            def gather(item):
                pe.wait_ge(sel_ready, item * 2 + 2)
                if not isinstance(item, int):
                    pe.wait_ge(selT_ready, item)
                for k in range(KD):
                    o = ps[:, 6 + k // 4, (k % 4) * P:(k % 4 + 1) * P]
                    for c in range(TC):
                        last = mm(o, xm[:, c, k * P:(k + 1) * P], sel[:, c, :], c == 0 and k % 4 == 0, c == TC - 1)
                    if k % 4 == 3:
                        last.then_inc(gathered, 1)

            def transpose_sel(item):
                pe.wait_ge(xe_lo, item * KD + KD)
                for c in range(TC):
                    last = pe.transpose(ps[:, 6, c * P:(c + 1) * P], sel[:, c, :], ident[:, :])
                last.then_inc(sel_tr, 1)

            transpose_x(1, (h_ready[1], 2), (h_ready[1], 4))
            ffn(0)
            ffn(1)

            transpose_x(2, (h_ready[2], 6), (h_ready[2], 8))
            for k in range(KD):
                pe.wait_ge(xlo_ready[2], k + 1)
                pe.wait_ge(lo_made, H_SBK + k + 1)
                features_out(k, H_SBK + k, 4)
            pe.wait_ge(rb_diag, 4)
            for c in range(TC):
                last = mm(ps[:, 0, c * P:(c + 1) * P], ones[:, :], sp[:, c, 0:P], c == 0, c == TC - 1)
            last.then_inc(rb_mm, 1)
            pe.wait_ge(rb_ready, 2)
            for k in range(KD):
                pe.wait_ge(lo_made, H_SBV + k + 1)
                tokens_out(k, H_SBV + k, ((0, 1), (2, 3)))
            pe.wait_ge(skT_ready, 4)
            transpose_x(3, (h_ready[2], 6), (h_ready[2], 8))
            pe.wait_ge(sv_ready, 4)
            for k in range(KD):
                pe.wait_ge(xlo_ready[3], k + 1)
                pe.wait_ge(lo_made, H_SBQ + k + 1)
                features_out(k, H_SBQ + k, 0)

            def logits(hd):
                z = ps[:, hd, :]
                mm(z[:, 0:SEQ], skT[:, hd, 0:P], sqT[:, hd, :], True, False)
                mm(z[:, SEQ:384], skT[:, hd, P:SEQ], sqT[:, hd, P:SEQ], False, False)
                mm(z[:, 0:P], ident_r[:, :], hide_r[:, :], False, False)
                mm(z[:, SEQ:384], ident_r[:, :], hide_r[:, :], False, True).then_inc(z_done, 1)

            def sb_outputs(hd):
                o = ps[:, hd, :]
                mm(o[:, 0:SEQ], sv[:, 0, hd * P:(hd + 1) * P], sp[:, hd, 0:SEQ], True, False)
                mm(o[:, P:SEQ], sv[:, 1, hd * P:(hd + 1) * P], sp[:, hd, SEQ:384], False, True).then_inc(so_done, 1)

            pe.wait_ge(sqT_ready, 4)
            for hd in range(HEADS):
                logits(hd)
            for hd in range(HEADS):
                if hd % 4 == 0:
                    pe.wait_ge(sp_ready, hd // 4 + 1)
                z, s = ps[:, hd, :], sp[:, hd, :]
                mm(z[:, 0:SEQ], neg_from[:, :], s[:, 0:SEQ], False, False)
                mm(z[:, SEQ:384], neg_from[:, :], s[:, SEQ:384], False, False)
                mm(z[:, P:SEQ], neg_ones[:, :], s[:, SEQ:384], False, True).then_inc(c_done, 1)
            for hd in range(HEADS):
                if hd % 4 == 0:
                    pe.wait_ge(a_ready, hd // 4 + 1)
                sb_outputs(hd)
            for k in range(HEADS):
                if k % 4 == 0:
                    pe.wait_ge(so_lo, k // 4 + 1)
                pe.wait_ge(lo_made, H_SBO + k + 1)
                tokens_out(k, H_SBO + k, ((0, 1), (2, 3)))

            transpose_x(4, (h_ready[3], 2), (h_ready[3], 4))
            pe.wait_ge(router_ready, 4)
            for k in range(KD):
                pe.wait_ge(xlo_ready[4], k + 1)
                mm(ps[:, 4, 0:SEQ], router_hl[:, k, :], xhi[:, k, :], k == 0, False)
                last = mm(ps[:, 4, 0:SEQ], router_hl[:, k, :], xlo[:, k, :], False, k == KD - 1)
            last.then_inc(lgT_done, 1)
            pe.wait_ge(lgT_ready, 1)
            for c in range(TC):
                last = mm(ps[:, 5, c * N_EXP:(c + 1) * N_EXP], lgT[0:2 * N_EXP, c * P:(c + 1) * P], fold[0:2 * N_EXP, :],
                          c == 0, True)
            last.then_inc(lg_done, 1)
            pe.wait_ge(msk_ready, 1)
            mm(ps[:, 5, 16:24], before[:, :], msk[:, 0, :], False, True)
            mm(ps[:, 5, 24:32], ones[:, :], msk[:, 0, :], False, False)
            mm(ps[:, 5, 24:32], before[:, :], msk[:, 1, :], False, True)
            mm(ps[:, 5, 32:40], ones[:, :], msk[:, 0, :], False, False)
            mm(ps[:, 5, 32:40], ones[:, :], msk[:, 1, :], False, True).then_inc(pos_done, 1)

            pe.wait_ge(xm_ready, 2)
            gather(0)
            transpose_sel(0)
            pe.wait_ge(items_ready, 2)
            n_items = pe.value_load(n_items_i[0:1, 0:1], min_val=N_EXP, max_val=ITEMS - 1)
            with pe.Fori(0, n_items) as i:
                pe.wait_ge(xe_lo, i * KD + KD)
                ffn(2, i)
                pe.wait_ge(y_lo, i * 2 + 2)
                pe.wait_ge(selT_ready, i + 1)
                for c in range(TC):
                    for n in range(2):
                        o = ps[:, 2 + 2 * c + n, :].rearrange("p (a s) -> p a s", a=4)
                        w = selT[:, c * P:(c + 1) * P]
                        mm(o, w, xhi[:, 4 * n:4 * n + 4, P:SEQ], True, False)
                        mm(o, w, xlo[:, 4 * n:4 * n + 4, P:SEQ], False, True).then_inc(scattered, 1)
                transpose_sel(i + 1)


INPUTS = ["x", "positions", "attn_norm_0", "mla_w_down_0", "mla_q_norm_0", "mla_w_uq_0", "mla_kv_norm_0",
          "mla_w_ukv_0", "mla_w_o_0", "ffn_norm_0", "ffn_w_gate_up_0", "ffn_w_down_0", "attn_norm_1",
          "ffn_norm_1", "moe_router_1", "moe_w_gate_up_1", "moe_w_down_1", "kv_shared_norm", "kv_shared_w",
          "sb_w_q_2", "sb_w_o_2", "final_norm"]


def kernel(**inputs):
    import concourse.bacc as bacc
    from concourse.bass_utils import run_bass_kernel_spmd as run

    nc = bacc.Bacc("TRN2", target_bir_lowering=False, num_devices=1)
    arrays, t = {}, {}
    for name in INPUTS:
        a = np.ascontiguousarray(inputs[name])
        arrays[f"{name}_dram"] = a
        t[name] = nc.dram_tensor(f"{name}_dram", a.shape, mybir.dt.from_np(a.dtype), kind="ExternalInput").ap()
    out = nc.dram_tensor("out_dram", (1, SEQ, D), F32, kind="ExternalOutput").ap()
    build(nc, t, out)
    r = run(nc, [arrays], core_ids=[0])
    return r.results[0]["out_dram"]
```

```python
import numpy as np
from contextlib import ExitStack

import concourse.bass as bass
from concourse import mybir

F32 = mybir.dt.float32
F32R = mybir.dt.float32r
I32 = mybir.dt.int32
ALU = mybir.AluOpType
ACT = mybir.ActivationFunctionType
AX = mybir.AxisListType.X

P = 128
SEQ, D = 256, 1024
TC = SEQ // P
KD = D // P
HEADS = 8
Q_LORA, KV_LORA, ROPE = 384, 256, 64
DOWN = Q_LORA + KV_LORA + ROPE
QH = P + ROPE
CC = (Q_LORA + KV_LORA) // P
FF = 2816
N_EXP = 8
CHUNK = 64
EPS = 1e-6
MLA_SCALE = float(QH) ** -0.5
SB_SCALE = float(P) ** -0.5
NEG = -1e30

RAW = 11
RING = 6
HALF = 1024
GW = 256
NG = FF // GW
FU = 3 * NG
FH = 2 * FU
FC = FF // P
H_DOWN, H_UQ, H_UKV, H_WO = 0, 8, 14, 18
H_FFN = 26
GA = 6
H_FFN_B = H_FFN + 6 * GA
H_SBK = H_FFN + FH
H_SBQ, H_SBV, H_SBO = H_SBK + 8, H_SBK + 16, H_SBK + 24
H_MOE = H_SBK + 32
U_MOE = H_MOE // 2
AHEAD = (RING + 4 + 1) // 2
assert H_MOE % 2 == 0 and FU % RAW == 0 and FH % RING == 0
ITEMS = 12

G_ATTN0, G_Q, G_KV, G_FFN0, G_KVSH, G_ATTN1, G_FFN1, G_ALL = 0, 8, 11, 13, 21, 29, 37, 45


def half_width(h):
    return DOWN if h < H_UQ else 4 * QH if h < H_UKV else HALF


def gain_of(h):
    for first, last, g, chunks in ((H_DOWN, H_UQ, G_ATTN0, KD), (H_UQ, H_UKV, G_Q, 3), (H_UKV, H_WO, G_KV, 2),
                                   (H_SBK, H_SBQ, G_KVSH, KD), (H_SBQ, H_SBV, G_ATTN1, KD), (H_SBV, H_SBO, G_KVSH, KD)):
        if first <= h < last:
            return g + (h - first) % chunks
    return None


def build(nc, t, out):
    with ExitStack() as ctx:
        def sb(name, shape, dt=F32):
            return ctx.enter_context(nc.sbuf_tensor(name, shape, dt))

        def sem(name):
            return ctx.enter_context(nc.semaphore(name))

        raw = sb("raw", [P, RAW, 2 * HALF])
        whi = sb("whi", [P, RING, HALF], F32R)
        wlo = sb("wlo", [P, RING, HALF], F32R)
        h = sb("h", [P, TC, D])
        xhi = sb("xhi", [P, KD, SEQ], F32R)
        xlo = sb("xlo", [P, KD, SEQ], F32R)
        ident = sb("ident", [P, P])
        ones = sb("ones", [P, P])
        neg_ones = sb("neg_ones", [P, P])
        before = sb("before", [P, P])
        neg_from = sb("neg_from", [P, P])
        iota = sb("iota", [P, P])
        gcol = sb("gcol", [P, G_ALL])
        ss = sb("ss", [P, 5, TC])
        ms = sb("ms", [P, 5, TC])
        rstd = sb("rstd", [P, 5, TC])
        minus_half = sb("minus_half", [P, 4])
        rb = sb("rb", [P, SEQ])
        ident_r = sb("ident_r", [P, P], F32R)
        hide_r = sb("hide_r", [P, P], F32R)
        one = sb("one", [P, 1])
        table_scratch = sb("table_scratch", [P, 1])
        router = sb("router", [P, KD, N_EXP])
        pm_tab = sb("pm_tab", [P, ITEMS, 2, TC])
        g_tab = sb("g_tab", [P, ITEMS, TC])
        item_expert = sb("item_expert", [P, ITEMS], I32)
        n_items_i = sb("n_items_i", [P, 1], I32)
        pm = sb("pm", [P, 2, TC])
        gt = sb("gt", [P, TC])

        def over(*specs):
            with ExitStack() as e:
                return [e.enter_context(nc.sbuf_tensor(n, s, d)) for n, s, d in specs]

        kT, qT, v, qrT, krT, chi, clo = over(
            ("kT", [P, HEADS, SEQ], F32), ("qT", [P, HEADS, SEQ], F32), ("v", [P, TC, D], F32),
            ("qrT", [P, 4, SEQ], F32), ("krT", [P, SEQ], F32),
            ("chi", [P, CC, SEQ], F32R), ("clo", [P, CC, SEQ], F32R))
        squares_out_0, cn, _, rot, rt, kr, _, prob, probT, hide, grow = over(
            ("squares_out_0", [P, TC, D], F32), ("cn", [P, TC, Q_LORA + KV_LORA], F32), ("gap0", [P, 768], F32),
            ("rot", [P, TC, HEADS, ROPE], F32), ("rt", [P, 2, HEADS, ROPE // 2], F32),
            ("kr", [P, TC, 2 * ROPE], F32),
            ("gap1", [P, 5 * SEQ + 256], F32), ("prob", [P, 2, 384], F32), ("probT", [P, 2, 384], F32),
            ("hide", [P, P], F32), ("grow", [P, P], F32))
        diag, = over(("diag", [P, TC, P], F32))
        _, ang, ang_k, cos, sin, invf, posi, posf, mx, nmx, rs, rr, css, cfac, qscale, half_mask = over(
            ("gap2", [P, 6 * 1024 + 1280 + 2560], F32), ("ang", [P, TC, 32], F32), ("ang_k", [P, TC, 32], F32),
            ("cos", [P, TC, 32], F32), ("sin", [P, TC, 32], F32), ("invf", [P, 32], F32),
            ("posi", [P, TC], I32), ("posf", [P, TC], F32),
            ("mx", [P, HEADS, 2], F32), ("nmx", [P, HEADS, 2], F32), ("rs", [P, HEADS, 2], F32),
            ("rr", [P, HEADS, 2], F32), ("css", [P, 2, TC], F32), ("cfac", [P, 2, TC], F32),
            ("qscale", [P, 2, TC], F32), ("half_mask", [P, 192], F32))
        hhi, hlo, xm, gu, sel, selT = over(
            ("hhi", [P, 2 * GA, SEQ], F32R), ("hlo", [P, 2 * GA, SEQ], F32R),
            ("xm", [P, TC, D], F32), ("gu", [P, 2, TC, GW], F32), ("sel", [P, TC, P], F32),
            ("selT", [P, SEQ], F32R))
        gbc = gu[:, :, :, :].rearrange("p a c g -> p (a c g)")
        ehi = hhi[:, :, :].rearrange("p c t -> p (c t)").rearrange("p (c t) -> p c t", t=P)
        elo = hlo[:, :, :].rearrange("p c t -> p (c t)").rearrange("p (c t) -> p c t", t=P)
        skT, sqT, sv, sp = over(
            ("skT", [P, HEADS, SEQ], F32), ("sqT", [P, HEADS, SEQ], F32), ("sv", [P, TC, D], F32),
            ("sp", [P, HEADS, 384], F32))
        lg, lg2, oh1, oh2, sc8, msk, gates, posn, ovf, csum, selr, prod, m1, m2, den, best, \
            rank, cnt, tf, xr = over(
                *[(f"rt_{n}", [P, TC, N_EXP], F32) for n in
                  ("lg", "lg2", "oh1", "oh2", "sc8", "msk", "gates", "posn")],
                ("rt_ovf", [P, N_EXP], F32), ("rt_csum", [P, N_EXP], F32), ("rt_selr", [P, 3, N_EXP], F32),
                ("rt_prod", [P, 3, N_EXP], F32), ("rt_m1", [P, TC], F32), ("rt_m2", [P, TC], F32),
                ("rt_den", [P, TC], F32), ("rt_best", [P, TC], F32), ("rt_rank", [P, N_EXP], F32),
                ("rt_cnt", [P, N_EXP], F32), ("rt_tf", [P, ITEMS], F32),
                ("xr", [P, KD, SEQ], F32))
        yout, yg = over(("yout", [P, TC, D], F32), ("yg", [P, TC, D], F32))

        ps = ctx.enter_context(nc.psum_tensor("ps", [P, 8, 512], F32))

        landed = [sem(f"landed{i}") for i in range(RAW)]
        hi_made = sem("hi_made")
        lo_made = sem("lo_made")
        used = sem("used")
        gain0_in = sem("gain0_in")
        small_in = sem("small_in")
        pos_in = sem("pos_in")
        x_in = [sem(f"x_in{n}") for n in range(2)]
        h_ready = [None] + [sem(f"h_ready{n}") for n in range(1, 5)]
        consts = sem("consts")
        pool_step = sem("pool_step")
        dve_step = sem("dve_step")
        act_step = sem("act_step")
        ss_ready = [sem(f"ss_ready{n}") for n in range(5)]
        rstd_ready = [sem(f"rstd_ready{n}") for n in range(5)]
        rb_diag, rb_mm, rb_ready = sem("rb_diag"), sem("rb_mm"), sem("rb_ready")
        xm_ready = sem("xm_ready")
        TRS = 4
        x_tr = [sem(f"x_tr{n}") for n in range(TRS)]
        xhi_ready = [sem(f"xhi_ready{n}") for n in range(TRS)]
        xlo_ready = [sem(f"xlo_ready{n}") for n in range(TRS)]
        g_tr, g_ready = sem("g_tr"), sem("g_ready")
        rc_ready, sin_ready, ident_ready = sem("rc_ready"), sem("sin_ready"), sem("ident_ready")
        c_ss, cfac_ready, cq_ready, ckv_ready, kr_scaled, kr_ready, kr_tr, krT_ready = (
            sem(n) for n in ("c_ss", "cfac_ready", "cq_ready", "ckv_ready", "kr_scaled", "kr_ready", "kr_tr", "krT_ready"))
        c_tr, chi_ready, clo_ready = sem("c_tr"), sem("chi_ready"), sem("clo_ready")
        qn_done, qT_ready, kn_done, kT_ready = sem("qn_done"), sem("qT_ready"), sem("kn_done"), sem("kT_ready")
        rot_done = sem("rot_done")
        rot_ready, v_ready, rot_tr, qrT_ready = sem("rot_ready"), [sem(f"v_ready{c}") for c in range(TC)], sem("rot_tr"), sem("qrT_ready")
        s_done, max_done, exp_done, pn_ready = sem("s_done"), sem("max_done"), sem("exp_done"), sem("pn_ready")
        pt_done, probT_ready, o_done, o_hi, o_lo = (sem(n) for n in ("pt_done", "probT_ready", "o_done", "o_hi", "o_lo"))
        skT_ready, sv_ready, sqT_ready = sem("skT_ready"), [sem(f"sv_ready{c}") for c in range(TC)], sem("sqT_ready")
        z_done, ln_done, sp_ready, c_done, a_ready = (
            sem(n) for n in ("z_done", "ln_done", "sp_ready", "c_done", "a_ready"))
        so_done, so_hi, so_lo = sem("so_done"), sem("so_hi"), sem("so_lo")
        silu_done = [sem(f"silu_done{n}") for n in range(3)]
        gated = [sem(f"gated{n}") for n in range(3)]
        gu_tr = [sem(f"gu_tr{n}") for n in range(3)]
        h_hi = [sem(f"h_hi{n}") for n in range(3)]
        h_lo = [sem(f"h_lo{n}") for n in range(3)]
        lg_done, gap_ready, gap_exp = (sem(n) for n in ("lg_done", "gap_ready", "gap_exp"))
        msk_ready, pos_done, items_ready = sem("msk_ready"), sem("pos_done"), sem("items_ready")
        pm_ready, sel_ready, gathered, xe_hi, xe_lo = (sem(n) for n in ("pm_ready", "sel_ready", "gathered", "xe_hi", "xe_lo"))
        sel_tr, selT_ready, y_hi, y_lo, scattered, gt_ready = (sem(n) for n in ("sel_tr", "selT_ready", "y_hi", "y_lo", "scattered", "gt_ready"))
        gbc_in, yg_ready, stored = sem("gbc_in"), sem("yg_ready"), sem("stored")
        y_ready = [sem(f"y_ready{c}") for c in range(TC)]

        block = ctx.enter_context(nc.Block())

        def raw_half(hh):
            return raw[:, (hh // 2) % RAW, (hh % 2) * HALF:(hh % 2) * HALF + half_width(hh)]

        def w_hi(hh):
            return whi[:, hh % RING, :]

        def w_lo(hh):
            return wlo[:, hh % RING, :]

        def bank_gu(x, c, par):
            return par if x == 2 else 2 * par + c

        def bank_tr(x, par):
            return 2 + par if x == 2 else 4 + par

        def bank_out(x, c, n):
            return 4 + n if x == 2 else (6 + n if c == 0 else n)

        def parity(x, j):
            return (j + 1) % 2 if x == 1 else j % 2

        X_BANKS = [(0, 1, 2, 3), (4, 6, 5, 7), (0, 2, 1, 3), (0, 2, 1, 3)]

        LAST_TR = 5

        def first_group(x):
            return 1 if x == 2 else 0

        FFN = [(GA, 2, H_FFN), (NG - GA, 2, H_FFN_B), (NG, 1, H_MOE)]

        @block.sync
        def _(sp_eng):
            def slot_free(u, i=0):
                if u >= RAW:
                    sp_eng.wait_ge(lo_made, i * FH + 2 * (u - RAW) + 2)

            def load(u, halves, i=0):
                slot_free(u, i)
                for dst, src in halves:
                    sp_eng.dma_start(dst, src).then_inc(landed[u % RAW], 16)

            def rows(u, w, r, width=HALF):
                return [(raw[:, u % RAW, n * HALF:n * HALF + width], w[r + n * P:r + (n + 1) * P, :]) for n in range(2)]

            def square(u0, w):
                for n in range(4):
                    load(u0 + n, rows(u0 + n, w, 256 * n))

            def swiglu_unit(u, x_unit, w_gu, w_dn, i=0):
                if x_unit < 2 * NG:
                    j, q = x_unit // 2, x_unit % 2
                    src = w_gu.rearrange("(k p) f -> p k f", p=P)[:, 4 * q:4 * q + 4, :]
                    dst = raw[:, u % RAW, :].rearrange("p (k f) -> p k f", k=4)
                    load(u, [(dst[:, :, g * GW:(g + 1) * GW], src[:, :, g * FF + j * GW:g * FF + (j + 1) * GW])
                             for g in range(2)], i)
                else:
                    load(u, rows(u, w_dn, (x_unit - 2 * NG) * 256), i)

            for n in range(2):
                w = slice(n * 512, (n + 1) * 512)
                sp_eng.dma_start(h[:, :, w], t["x"].rearrange("a (c p) d -> p (a c) d", p=P)[:, :, w]).then_inc(x_in[n], 16)
            gains = (("attn_norm_0", 8), ("mla_q_norm_0", 3), ("mla_kv_norm_0", 2), ("ffn_norm_0", 8),
                     ("kv_shared_norm", 8), ("attn_norm_1", 8), ("ffn_norm_1", 8))
            assert sum(n for _, n in gains) == G_ALL

            def gain_rows(names, row, ready):
                for name, n in names:
                    sp_eng.dma_start(grow[row:row + n, :], t[name].rearrange("(k c) -> k c", c=P)).then_inc(ready, 16)
                    row += n

            gain_rows(gains[:1], 0, gain0_in)
            for u in range(2):
                load(u, rows(u, t["mla_w_down_0"], u * 256, DOWN))
            gain_rows(gains[1:], 8, small_in)
            for u in range(2, 4):
                load(u, rows(u, t["mla_w_down_0"], u * 256, DOWN))
            sp_eng.dma_start(posi[:, :], t["positions"].rearrange("a (c p) -> p (a c)", p=P),
                             allow_slow_non_contiguous=True).then_inc(pos_in, 16)
            sp_eng.dma_start(router[:, :, :], t["moe_router_1"].rearrange("(k p) e -> p k e", p=P)).then_inc(pos_in, 16)
            for hh0, w, ks, cols in ((H_UQ, t["mla_w_uq_0"], 3, 4 * QH), (H_UKV, t["mla_w_ukv_0"], 2, HALF)):
                for m in range(0, 2 * ks, 2):
                    load((hh0 + m) // 2, [
                        (raw_half(hh0 + x), w[(x % ks) * P:(x % ks + 1) * P, (x // ks) * cols:(x // ks + 1) * cols])
                        for x in (m, m + 1)])
            square(H_WO // 2, t["mla_w_o_0"])
            order = list(range(2 * GA)) + [2 * NG + n for n in range(GA)] + \
                list(range(2 * GA, 2 * NG)) + [2 * NG + n for n in range(GA, NG)]
            for n, x_unit in enumerate(order):
                swiglu_unit(H_FFN // 2 + n, x_unit, t["ffn_w_gate_up_0"], t["ffn_w_down_0"])
            square(H_SBK // 2, t["kv_shared_w"][:, 0:D])
            square(H_SBQ // 2, t["sb_w_q_2"])
            square(H_SBV // 2, t["kv_shared_w"][:, D:2 * D])
            square(H_SBO // 2, t["sb_w_o_2"])

            def expert(e):
                return (t["moe_w_gate_up_1"][bass.ds(e, 1), :, :].rearrange("a k f -> (a k) f"),
                        t["moe_w_down_1"][bass.ds(e, 1), :, :].rearrange("a k f -> (a k) f"))

            def item_loads(i, now):
                for n in range(AHEAD, FU):
                    swiglu_unit(U_MOE + n, n, *now, i=i)

            def first_loads(i, following):
                for n in range(AHEAD):
                    swiglu_unit(U_MOE + FU + n, n, *following, i=i)

            for n in range(AHEAD):
                swiglu_unit(U_MOE + n, n, t["moe_w_gate_up_1"][0], t["moe_w_down_1"][0])
            with sp_eng.Fori(0, N_EXP - 2) as i:
                item_loads(i, expert(i))
                first_loads(i, expert(i + 1))
            sp_eng.wait_ge(items_ready, 2)
            n_items = sp_eng.value_load(n_items_i[0:1, 0:1], min_val=N_EXP, max_val=ITEMS - 1)
            with sp_eng.Fori(N_EXP - 2, n_items - 1) as i:
                e = sp_eng.value_load(item_expert[0:1, bass.ds(i, 1)], min_val=0, max_val=N_EXP - 1)
                e_next = sp_eng.value_load(item_expert[0:1, bass.ds(i + 1, 1)], min_val=0, max_val=N_EXP - 1)
                item_loads(i, expert(e))
                first_loads(i, expert(e_next))
            e = sp_eng.value_load(item_expert[0:1, bass.ds(n_items - 1, 1)], min_val=0, max_val=N_EXP - 1)
            item_loads(n_items - 1, expert(e))
            for n in range(AHEAD):
                u = U_MOE + FU + n
                load(u, [(raw[0:1, u % RAW, m * HALF:m * HALF + P], t["moe_w_down_1"][0, m:m + 1, 0:P]) for m in range(2)],
                     n_items - 1)
            for c in range(TC):
                sp_eng.wait_ge(y_ready[c], 1)
                sp_eng.dma_start(out[0, c * P:(c + 1) * P, :], yout[:, c, :]).then_inc(stored, 16)
            sp_eng.wait_ge(stored, 16 * TC)

        @block.gpsimd
        def _(pool):
            n = [0]

            def step(ins):
                n[0] += 1
                ins.then_inc(pool_step, 1)
                pool.wait_ge(pool_step, n[0])

            step(nc.gpsimd.memset(ident[:, :], 0.0))
            nc.gpsimd.affine_select(out=ident[:, :], in_=ident[:, :], compare_op=ALU.not_equal, fill=1.0,
                                    base=0, pattern=[[-1, P]], channel_multiplier=1).then_inc(ident_ready, 1)
            inv = 1.0 / (10000.0 ** (np.arange(0, ROPE, 2, dtype=np.float64) / ROPE))
            for c in range(ROPE // 2):
                nc.gpsimd.memset(invf[:, c:c + 1], float(np.float32(inv[c])))
            nc.gpsimd.memset(minus_half[:, :], -0.5)
            nc.gpsimd.memset(one[:, :], 1.0)
            nc.gpsimd.memset(ones[:, :], 1.0)
            nc.gpsimd.memset(neg_ones[:, :], -1.0)
            nc.gpsimd.memset(half_mask[0:1, 0:64], 1.0)
            nc.gpsimd.memset(half_mask[0:1, 64:128], 0.0)
            nc.gpsimd.memset(half_mask[0:1, 128:192], NEG)
            nc.gpsimd.memset(hide[:, :], 0.0)
            step(nc.gpsimd.memset(before[:, :], 0.0))
            nc.gpsimd.affine_select(out=before[:, :], in_=before[:, :], compare_op=ALU.is_ge, fill=1.0,
                                    base=0, pattern=[[-1, P]], channel_multiplier=1)
            nc.gpsimd.affine_select(out=hide[:, :], in_=hide[:, :], compare_op=ALU.is_gt, fill=NEG,
                                    base=0, pattern=[[1, P]], channel_multiplier=-1)
            nc.gpsimd.affine_select(out=neg_from[:, :], in_=neg_ones[:, :], compare_op=ALU.is_ge, fill=0.0,
                                    base=0, pattern=[[-1, P]], channel_multiplier=1)
            nc.gpsimd.iota(iota[:, :], [[1, P]], base=0, channel_multiplier=0,
                           allow_small_or_imprecise_dtypes=True).then_inc(consts, 1)

            def norm(k):
                pool.wait_ge(ss_ready[k], 2)
                step(nc.gpsimd.tensor_scalar(ms[:, k, :], ss[:, k, :], 1.0 / D, EPS, ALU.mult, ALU.add))
                nc.gpsimd.tensor_tensor(rstd[:, k, :], ms[:, k, :], minus_half[:, 0:TC], ALU.pow).then_inc(rstd_ready[k], 1)

            norm(0)
            pool.wait_ge(rstd_ready[0], 1)
            pool.wait_ge(c_ss, 4)
            for m, width in ((0, Q_LORA), (1, KV_LORA)):
                step(nc.gpsimd.tensor_tensor(cfac[:, m, :], css[:, m, :], rstd[:, 0, :], ALU.mult))
                step(nc.gpsimd.tensor_tensor(cfac[:, m, :], cfac[:, m, :], rstd[:, 0, :], ALU.mult))
                step(nc.gpsimd.tensor_scalar(cfac[:, m, :], cfac[:, m, :], 1.0 / width, EPS, ALU.mult, ALU.add))
                step(nc.gpsimd.tensor_tensor(cfac[:, m, :], cfac[:, m, :], minus_half[:, 0:TC], ALU.pow))
                step(nc.gpsimd.tensor_tensor(cfac[:, m, :], cfac[:, m, :], rstd[:, 0, :], ALU.mult))
            nc.gpsimd.tensor_scalar(qscale[:, 1, :], cfac[:, 0, :], -MLA_SCALE, None, ALU.mult)
            nc.gpsimd.tensor_scalar(qscale[:, 0, :], cfac[:, 0, :], MLA_SCALE, None, ALU.mult).then_inc(cfac_ready, 1)
            for k in range(1, 5):
                norm(k)

        @block.scalar
        def _(act):
            steps = [0]

            def step(ins):
                steps[0] += 1
                ins.then_inc(act_step, 1)
                act.wait_ge(act_step, steps[0])

            def copy(o, i, scale=1.0):
                return nc.scalar.activation(o, i, ACT.Copy, scale=scale)

            def split_high(hh, i=0):
                u = hh // 2
                act.wait_ge(landed[u % RAW], i * (32 * FU // RAW) + 32 * (u // RAW + 1))
                if hh >= RING:
                    act.wait_ge(used, i * FH + hh - RING + 1)
                g = gain_of(hh)
                copy(w_hi(hh)[:, 0:half_width(hh)], raw_half(hh),
                     scale=1.0 if g is None else gcol[:, g:g + 1]).then_inc(hi_made, 1)

            def split_high_unit(hh, i=0):
                if gain_of(hh) is not None:
                    split_high(hh)
                    split_high(hh + 1)
                    return
                u = hh // 2
                act.wait_ge(landed[u % RAW], i * (32 * FU // RAW) + 32 * (u // RAW + 1))
                act.wait_ge(used, i * FH + hh - RING + 2)
                copy(whi[:, hh % RING:hh % RING + 2, :].rearrange("p a w -> p (a w)"), raw[:, u % RAW, :]).then_inc(hi_made, 2)

            def squares(n, c, junk):
                nc.scalar.activation(junk, h[:, c, :], ACT.Square, accum_out=ss[:, n, c:c + 1]).then_inc(ss_ready[n], 1)

            def x_high(n, gain=None, banks=range(4)):
                for b in banks:
                    act.wait_ge(x_tr[n], b + 1)
                    if gain is None:
                        copy(xhi[:, 2 * b:2 * b + 2, :], ps[:, X_BANKS[n][b], :].rearrange("p (a s) -> p a s", a=2)
                             ).then_inc(xhi_ready[n], 2)
                        continue
                    for k in (2 * b, 2 * b + 1):
                        copy(xhi[:, k, :], ps[:, X_BANKS[n][b], (k % 2) * SEQ:(k % 2 + 1) * SEQ],
                             scale=gcol[:, gain + k:gain + k + 1]).then_inc(xhi_ready[n], 1)

            x_high(0, banks=[0])
            act.wait_ge(g_tr, 1)
            copy(gcol[:, 0:KD], ps[:, 7, 0:KD]).then_inc(g_ready, 1)
            x_high(0, banks=[1])
            act.wait_ge(g_ready, 1)
            split_high(0)
            x_high(0, banks=[2])
            split_high(1)
            x_high(0, banks=[3])
            for hh in range(2, 8):
                split_high(hh)
            act.wait_ge(g_tr, 2)
            copy(gcol[:, KD:], ps[:, 0, KD:G_ALL]).then_inc(g_ready, 1)
            act.wait_ge(g_ready, 2)
            for hh in range(8, 11):
                split_high(hh)
            squares(0, 0, squares_out_0[:, 0, :])
            act.wait_ge(rc_ready, 2)
            nc.scalar.activation(sin[:, :, :], ang[:, :, :], ACT.Sin).then_inc(sin_ready, 1)
            nc.scalar.activation(cos[:, :, :], ang_k[:, :, :], ACT.Sin).then_inc(sin_ready, 1)
            for hh in range(11, 14):
                split_high(hh)

            act.wait_ge(used, H_UQ)
            for c in range(TC):
                copy(cn[:, c, 0:Q_LORA], ps[:, 4 + 2 * c, 0:Q_LORA]).then_inc(cq_ready, 1)
            for b in range(3):
                act.wait_ge(c_tr, b + 1)
                n = min(2, CC - 2 * b)
                copy(chi[:, 2 * b:2 * b + n, :], ps[:, b, 0:n * SEQ].rearrange("p (a s) -> p a s", a=n)).then_inc(chi_ready, 1)
            act.wait_ge(cq_ready, 2)
            act.wait_ge(ckv_ready, 2)
            nc.scalar.activation(squares_out_0[:, 1, 0:Q_LORA], cn[:, 0, 0:Q_LORA], ACT.Square, accum_out=css[:, 0, 0:1]).then_inc(c_ss, 1)
            nc.scalar.activation(squares_out_0[:, 1, Q_LORA:Q_LORA + KV_LORA], cn[:, 0, Q_LORA:], ACT.Square,
                                 accum_out=css[:, 1, 0:1]).then_inc(c_ss, 1)
            nc.scalar.activation(table_scratch[:, :], one[:, :], ACT.Exp)

            def queries(b):
                copy(qT[:, 2 * b:2 * b + 2, :].rearrange("p a s -> p (a s)"), ps[:, b, :]).then_inc(qT_ready, 1)

            act.wait_ge(c_ss, 4)
            for b in range(2):
                act.wait_ge(qn_done, b + 1)
                queries(b)
            for hh in range(14, 17):
                split_high(hh)
            act.wait_ge(kr_tr, 1)
            copy(krT[:, :], ps[:, 7, 0:SEQ]).then_inc(krT_ready, 1)
            act.wait_ge(qn_done, 3)
            queries(2)
            act.wait_ge(used, H_UKV)
            queries(3)
            act.wait_ge(rb_mm, 1)
            copy(rb[:, :], ps[:, 6, 0:SEQ]).then_inc(rb_ready, 1)
            for hh in range(17, 20):
                split_high(hh)
            for b in range(2):
                act.wait_ge(rot_tr, b + 1)
                copy(qrT[:, 2 * b:2 * b + 2, :].rearrange("p a s -> p (a s)"), ps[:, 6 + b, :]).then_inc(qrT_ready, 1)

            def values(g):
                copy(v[:, 0, g * 512:(g + 1) * 512], ps[:, 4 + 2 * g, :], scale=cfac[:, 1, 0:1]).then_inc(v_ready[0], 1)

            act.wait_ge(cfac_ready, 1)
            act.wait_ge(used, H_UKV + 2)
            values(0)
            for hh in range(20, 22):
                split_high(hh)
            act.wait_ge(used, H_WO)
            values(1)

            def mla_exp(hd):
                act.wait_ge(max_done, hd + 1)
                if hd >= 2:
                    act.wait_ge(pt_done, hd - 1)
                for c, (a, b) in enumerate(((0, 128), (128, 384))):
                    nc.scalar.activation(prob[:, hd % 2, a:b], ps[:, hd % 3, a:b], ACT.Exp, bias=nmx[:, hd, c:c + 1],
                                         scale=qscale[:, 0, c:c + 1], accum_out=rs[:, hd, c:c + 1]).then_inc(exp_done, 1)

            mla_exp(0)
            mla_exp(1)
            for hd in range(HEADS):
                act.wait_ge(pt_done, hd + 1)
                if hd >= 2:
                    act.wait_ge(o_done, hd - 1)
                copy(probT[:, hd % 2, :], ps[:, 3, 0:384]).then_inc(probT_ready, 1)
                act.wait_ge(o_done, hd + 1)
                copy(xhi[:, hd, :], ps[:, hd % 3, 0:SEQ]).then_inc(o_hi, 1)
                if hd + 2 < HEADS:
                    mla_exp(hd + 2)
                split_high(22 + hd)
            for hh in range(30, 32):
                split_high(hh)

            def ffn(x, i=0):
                n, nt, base = FFN[x]

                def silu(j):
                    act.wait_ge(used, i * FH + base + 4 * (j + 1))
                    for c in range(nt):
                        if j >= 2 and c == 0:
                            act.wait_ge(gu_tr[x], i * n + j - 1)
                        nc.scalar.activation(gu[:, j % 2, c, :], ps[:, bank_gu(x, c, parity(x, j)), 0:GW], ACT.Silu,
                                             scale=1.0 if x == 2 else rstd[:, 1, c:c + 1]).then_inc(silu_done[x], 1)

                def high(j):
                    act.wait_ge(gu_tr[x], i * n + j + 1)
                    src = ps[:, bank_tr(x, j % 2), 0:2 * nt * P]
                    dst = ehi[:, 2 * j:2 * j + 2, :] if nt == 1 else hhi[:, 2 * j:2 * j + 2, :]
                    copy(dst.rearrange("p a s -> p (a s)"), src).then_inc(h_hi[x], 1)

                for j in range(first_group(x), n):
                    if j >= 1:
                        silu(j - 1)
                    if j >= 2:
                        high(j - 2)
                    for m in range(0, 4, 2):
                        split_high_unit(base + RING + 4 * j + m, i)
                silu(n - 1)
                high(n - 2)
                for f in range(2 * n):
                    if f == 2 * n - 1 and x == 2:
                        act.wait_ge(used, i * FH + H_MOE + FH)
                        for m in range(2):
                            copy(xhi[:, 4 * m:4 * m + 4, P:SEQ], ps[:, 4 + m, :].rearrange("p (a s) -> p a s", a=4)).then_inc(y_hi, 1)
                    split_high(base + RING + 4 * n + f, i)
                    if f == LAST_TR:
                        high(n - 1)
                    if f == 17 and x == 2:
                        for b in range(2):
                            act.wait_ge(gathered, i * 2 + 2 + b + 1)
                            for k in range(4 * b, 4 * b + 4):
                                copy(xhi[:, k, 0:P], ps[:, 6 + b, (k % 4) * P:(k % 4 + 1) * P],
                                     scale=gcol[:, G_FFN1 + k:G_FFN1 + k + 1]).then_inc(xe_hi, 1)

            x_high(1, G_FFN0)
            squares(1, 0, xm[:, 0, :])
            act.wait_ge(rstd_ready[1], 1)
            ffn(0)
            ffn(1)

            def four(g):
                return sp[:, 4 * g:4 * g + 4, :], ps[:, 4 * g:4 * g + 4, 0:384]

            def softplus_part(g):
                step(nc.scalar.activation(four(g)[0], four(g)[0], ACT.Exp, scale=-1.0))
                nc.scalar.activation(four(g)[0], four(g)[0], ACT.Ln, bias=one[:, 0:1]).then_inc(ln_done, 1)

            def absolute(g):
                act.wait_ge(z_done, 4 * g + 4)
                step(nc.scalar.activation(four(g)[0], four(g)[1], ACT.Abs))

            def attend(g):
                for hd in range(4 * g, 4 * g + 4):
                    act.wait_ge(c_done, hd + 1)
                    nc.scalar.activation(sp[:, hd, :], ps[:, hd, 0:384], ACT.Exp).then_inc(a_ready, 1)

            def heads_high(g):
                for hd in range(4 * g, 4 * g + 4):
                    act.wait_ge(so_done, hd + 1)
                    copy(xhi[:, hd, :], ps[:, hd, 0:SEQ]).then_inc(so_hi, 1)

            x_high(2)
            squares(2, 0, sp[:, :, :].rearrange("p a s -> p (a s)")[:, 0:D])
            for m in range(8):
                if m == 6:
                    act.wait_ge(rb_mm, 2)
                    copy(rb[:, :], ps[:, 0, 0:SEQ]).then_inc(rb_ready, 1)
                split_high(H_SBK + RING + m)
            for m in range(8):
                split_high(H_SBQ + RING + m)
            for m in range(2):
                split_high(H_SBV + RING + m)
            absolute(0)
            softplus_part(0)
            for m in range(2, 7):
                split_high(H_SBV + RING + m)
            attend(0)
            act.wait_ge(used, H_SBO)
            for n in range(2):
                copy(sv[:, 0, n * 512:(n + 1) * 512], ps[:, 4 + n, :], scale=rstd[:, 2, 0:1]).then_inc(sv_ready[0], 1)
            split_high(H_SBV + RING + 7)
            absolute(1)
            heads_high(0)
            softplus_part(1)
            for m in range(4):
                split_high(H_SBO + RING + m)
            attend(1)
            heads_high(1)
            for m in range(4, 8):
                split_high(H_SBO + RING + m)

            for b in range(3):
                act.wait_ge(x_tr[3], b + 1)
                copy(xr[:, 2 * b:2 * b + 2, :], ps[:, X_BANKS[3][b], :].rearrange("p (a s) -> p a s", a=2)).then_inc(xhi_ready[3], 1)
            squares(3, 0, xm[:, 0, :])
            act.wait_ge(rstd_ready[3], 1)
            act.wait_ge(ss_ready[3], 2)
            copy(xm[:, 1, :], h[:, 1, :], scale=rstd[:, 3, 1:2]).then_inc(xm_ready, 1)
            act.wait_ge(gap_ready, 1)
            nc.scalar.activation(den[:, :], best[:, :], ACT.Exp).then_inc(gap_exp, 1)
            for b in range(2):
                act.wait_ge(gathered, b + 1)
                for k in range(4 * b, 4 * b + 4):
                    copy(xhi[:, k, 0:P], ps[:, 6 + b, (k % 4) * P:(k % 4 + 1) * P],
                         scale=gcol[:, G_FFN1 + k:G_FFN1 + k + 1]).then_inc(xe_hi, 1)
            for m in range(0, 4, 2):
                split_high_unit(H_MOE + RING + m)
            act.wait_ge(sel_tr, 1)
            copy(selT[:, :], ps[:, 6, 0:SEQ]).then_inc(selT_ready, 1)
            act.wait_ge(items_ready, 2)
            n_items = act.value_load(n_items_i[0:1, 0:1], min_val=N_EXP, max_val=ITEMS - 1)
            with act.Fori(0, n_items) as i:
                ffn(2, i)
                for m in range(4):
                    split_high(H_MOE + RING + m, i + 1)
                act.wait_ge(sel_tr, i + 2)
                copy(selT[:, :], ps[:, 6, 0:SEQ]).then_inc(selT_ready, 1)

            act.wait_ge(gu_tr[2], n_items * NG)
            act.dma_start(gbc, t["final_norm"].partition_broadcast(P)).then_inc(gbc_in, 16)
            for c in range(TC):
                act.wait_ge(h_ready[4], n_items * 4 + 2 * c + 2)
                squares(4, c, yout[:, c, :])
            act.wait_ge(rstd_ready[4], 1)
            act.wait_ge(yg_ready, 1)
            copy(yout[:, 0, :], yg[:, 0, :], scale=rstd[:, 4, 0:1]).then_inc(y_ready[0], 1)

        @block.vector
        def _(dve):
            V = nc.vector
            steps = [0]

            def step(ins):
                steps[0] += 1
                ins.then_inc(dve_step, 1)
                dve.wait_ge(dve_step, steps[0])

            def split_low(hh, i=0):
                dve.wait_ge(hi_made, i * FH + hh + 1)
                w, g = half_width(hh), gain_of(hh)
                hi = w_hi(hh)[:, 0:w].bitcast(F32)
                if g is None:
                    V.tensor_tensor(w_lo(hh)[:, 0:w], raw_half(hh), hi, ALU.subtract).then_inc(lo_made, 1)
                else:
                    V.scalar_tensor_tensor(out=w_lo(hh)[:, 0:w], in0=raw_half(hh), scalar=gcol[:, g:g + 1], in1=hi,
                                           op0=ALU.mult, op1=ALU.subtract).then_inc(lo_made, 1)

            def split_low_unit(hh, i=0):
                if gain_of(hh) is not None:
                    split_low(hh)
                    split_low(hh + 1)
                    return
                dve.wait_ge(hi_made, i * FH + hh + 2)
                s = slice(hh % RING, hh % RING + 2)
                V.tensor_tensor(wlo[:, s, :].rearrange("p a w -> p (a w)"), raw[:, (hh // 2) % RAW, :],
                                whi[:, s, :].bitcast(F32).rearrange("p a w -> p (a w)"), ALU.subtract).then_inc(lo_made, 2)

            def squares(n, c, junk):
                V.tensor_tensor_reduce(out=junk, in0=h[:, c, :], in1=h[:, c, :], scale=1.0, scalar=0.0,
                                       op0=ALU.mult, op1=ALU.add, accum_out=ss[:, n, c:c + 1]).then_inc(ss_ready[n], 1)

            def row_factors(n, col):
                for c in range(TC):
                    V.tensor_scalar(diag[:, c, :] if n == 0 else sp[:, c, 0:P], ident[:, :], col(c), None, ALU.mult).then_inc(rb_diag, 1)

            def x_low(n, gain=None, banks=range(4)):
                for b in banks:
                    dve.wait_ge(xhi_ready[n], 2 * b + 2)
                    if gain is None:
                        V.tensor_tensor(xlo[:, 2 * b:2 * b + 2, :], ps[:, X_BANKS[n][b], :].rearrange("p (a s) -> p a s", a=2),
                                        xhi[:, 2 * b:2 * b + 2, :].bitcast(F32), ALU.subtract).then_inc(xlo_ready[n], 2)
                        continue
                    for k in (2 * b, 2 * b + 1):
                        V.scalar_tensor_tensor(out=xlo[:, k, :], in0=ps[:, X_BANKS[n][b], (k % 2) * SEQ:(k % 2 + 1) * SEQ],
                                               scalar=gcol[:, gain + k:gain + k + 1], in1=xhi[:, k, :].bitcast(F32),
                                               op0=ALU.mult, op1=ALU.subtract).then_inc(xlo_ready[n], 1)

            x_low(0, banks=[0, 1])
            dve.wait_ge(g_ready, 1)
            split_low(0)
            x_low(0, banks=[2])
            split_low(1)
            x_low(0, banks=[3])
            for hh in range(2, 8):
                split_low(hh)

            dve.wait_ge(pos_in, 32)
            dve.wait_ge(consts, 1)
            step(V.tensor_copy(posf[:, :], posi[:, :]))
            for c in range(TC):
                last = V.tensor_scalar(ang[:, c, :], invf[:, :], posf[:, c:c + 1], None, ALU.mult)
            step(last)
            PI, MAGIC = 3.1415925, 12582912.0
            C1 = float(np.float32(6.28125))
            C2 = float(np.float32(np.float32(2 * np.pi - C1).view(np.uint32) & np.uint32(0xFFFFF000)).astype(np.uint32).view(np.float32))
            C3 = float(np.float32(2 * np.pi - C1 - C2))
            step(V.tensor_scalar(ang_k[:, :, :], ang[:, :, :], 1.0 / (2 * np.pi), MAGIC, ALU.mult, ALU.add))
            step(V.tensor_scalar(ang_k[:, :, :], ang_k[:, :, :], MAGIC, None, ALU.subtract))
            for part in (C1, C2, C3):
                step(V.scalar_tensor_tensor(out=ang[:, :, :], in0=ang_k[:, :, :], scalar=-part, in1=ang[:, :, :],
                                            op0=ALU.mult, op1=ALU.add))
            step(V.tensor_scalar(ang_k[:, :, :], ang[:, :, :], PI, -2 * np.pi, ALU.is_gt, ALU.mult))
            step(V.tensor_tensor(ang[:, :, :], ang[:, :, :], ang_k[:, :, :], ALU.add))
            step(V.tensor_scalar(ang_k[:, :, :], ang[:, :, :], -PI, 2 * np.pi, ALU.is_lt, ALU.mult))
            step(V.tensor_tensor(ang[:, :, :], ang[:, :, :], ang_k[:, :, :], ALU.add))
            step(V.tensor_scalar(ang_k[:, :, :], ang[:, :, :], np.pi / 2, None, ALU.add))
            over_pi = rt[:, :, 0, :]
            step(V.tensor_scalar(over_pi, ang_k[:, :, :], PI, -2 * np.pi, ALU.is_gt, ALU.mult))
            step(V.tensor_tensor(ang_k[:, :, :], ang_k[:, :, :], over_pi, ALU.add))
            V.tensor_scalar(ang[:, :, :], ang[:, :, :], PI, -PI, ALU.min, ALU.max).then_inc(rc_ready, 1)
            V.tensor_scalar(ang_k[:, :, :], ang_k[:, :, :], PI, -PI, ALU.min, ALU.max).then_inc(rc_ready, 1)
            V.tensor_copy(ident_r[:, :], ident[:, :])
            step(V.tensor_copy(hide_r[:, :], hide[:, :]))
            dve.wait_ge(g_ready, 2)
            split_low(8)
            for n in range(2):
                dve.wait_ge(x_in[n], 16)
            squares(0, 1, squares_out_0[:, 1, :])
            for hh in range(9, 14):
                split_low(hh)

            dve.wait_ge(used, H_UQ)
            for c in range(TC):
                V.tensor_copy(cn[:, c, Q_LORA:], ps[:, 5 + 2 * c, 0:KV_LORA]).then_inc(ckv_ready, 1)
            dve.wait_ge(rstd_ready[0], 1)
            for c in range(TC):
                V.tensor_scalar(kr[:, c, ROPE:2 * ROPE], ps[:, 5 + 2 * c, KV_LORA:KV_LORA + ROPE], rstd[:, 0, c:c + 1], None,
                                ALU.mult).then_inc(kr_scaled, 1)
            for b in range(3):
                dve.wait_ge(chi_ready, b + 1)
                n = min(2, CC - 2 * b)
                V.tensor_tensor(clo[:, 2 * b:2 * b + n, :], ps[:, b, 0:n * SEQ].rearrange("p (a s) -> p a s", a=n),
                                chi[:, 2 * b:2 * b + n, :].bitcast(F32), ALU.subtract).then_inc(clo_ready, 1)

            def rope(x1, x2, co, si, t1, t2, o1, o2, done=None):
                step(V.tensor_tensor(t1, x1, co, ALU.mult))
                step(V.tensor_tensor(t2, x2, si, ALU.mult))
                step(V.tensor_tensor(o1, t1, t2, ALU.subtract))
                step(V.tensor_tensor(t1, x1, si, ALU.mult))
                step(V.tensor_tensor(t2, x2, co, ALU.mult))
                if done is None:
                    step(V.tensor_tensor(o2, t1, t2, ALU.add))
                else:
                    V.tensor_tensor(o2, t1, t2, ALU.add).then_inc(done, 1)

            dve.wait_ge(sin_ready, 2)
            R2 = ROPE // 2
            dve.wait_ge(kr_scaled, 2)
            x = kr[:, :, ROPE:2 * ROPE]
            rope(x[:, :, 0:R2], x[:, :, R2:ROPE], cos[:, :, :], sin[:, :, :], rt[:, 0, 0:2, :], rt[:, 1, 0:2, :],
                 kr[:, :, 0:R2], kr[:, :, R2:ROPE])
            V.tensor_copy(kr[:, :, ROPE:2 * ROPE], kr[:, :, 0:ROPE]).then_inc(kr_ready, 1)
            dve.wait_ge(cq_ready, 2)
            dve.wait_ge(ckv_ready, 2)
            V.tensor_tensor_reduce(out=squares_out_0[:, 0, 0:Q_LORA], in0=cn[:, 1, 0:Q_LORA], in1=cn[:, 1, 0:Q_LORA], scale=1.0, scalar=0.0,
                                   op0=ALU.mult, op1=ALU.add, accum_out=css[:, 0, 1:2]).then_inc(c_ss, 1)
            V.tensor_tensor_reduce(out=squares_out_0[:, 0, Q_LORA:Q_LORA + KV_LORA], in0=cn[:, 1, Q_LORA:], in1=cn[:, 1, Q_LORA:], scale=1.0,
                                   scalar=0.0, op0=ALU.mult, op1=ALU.add, accum_out=css[:, 1, 1:2]).then_inc(c_ss, 1)

            def rope_queries(g):
                dve.wait_ge(rot_done, g + 1)
                x = ps[:, 4 + g, :].rearrange("p (c a r) -> p c a r", c=TC, r=ROPE)
                for c in range(TC):
                    co = cos[:, c, :].unsqueeze(1).to_broadcast([P, 4, R2])
                    si = sin[:, c, :].unsqueeze(1).to_broadcast([P, 4, R2])
                    o = rot[:, c, 4 * g:4 * g + 4, :]
                    rope(x[:, c, :, 0:R2], x[:, c, :, R2:ROPE], co, si, rt[:, 0, 4 * c:4 * c + 4, :], rt[:, 1, 4 * c:4 * c + 4, :],
                         o[:, :, 0:R2], o[:, :, R2:ROPE], rot_ready)

            rope_queries(0)
            for hh in range(14, 17):
                split_low(hh)
            dve.wait_ge(cfac_ready, 1)
            row_factors(0, lambda c: cfac[:, 1, c:c + 1])
            dve.wait_ge(rot_ready, 2)
            rope_queries(1)
            split_low(17)
            dve.wait_ge(rb_ready, 1)
            for b in range(4):
                dve.wait_ge(kn_done, b + 1)
                V.tensor_tensor(kT[:, 2 * b:2 * b + 2, :], ps[:, b, :].rearrange("p (a s) -> p a s", a=2),
                                rb[:, :].unsqueeze(1).to_broadcast([P, 2, SEQ]), ALU.mult).then_inc(kT_ready, 1)
            for hh in range(18, 20):
                split_low(hh)

            def values(g):
                V.tensor_scalar(v[:, 1, g * 512:(g + 1) * 512], ps[:, 5 + 2 * g, :], cfac[:, 1, 1:2], None, ALU.mult).then_inc(v_ready[1], 1)

            dve.wait_ge(used, H_UKV + 2)
            values(0)
            for hh in range(20, 22):
                split_low(hh)
            dve.wait_ge(used, H_WO)
            values(1)

            def mla_max(hd):
                dve.wait_ge(s_done, hd + 1)
                V.tensor_reduce(mx[:, hd, 0:1], ps[:, hd % 3, 0:128], AX, ALU.max)
                step(V.tensor_reduce(mx[:, hd, 1:2], ps[:, hd % 3, 128:384], AX, ALU.max))
                V.tensor_tensor(nmx[:, hd, :], mx[:, hd, :], qscale[:, 1, :], ALU.mult).then_inc(max_done, 1)

            def mla_low(hd):
                dve.wait_ge(o_hi, hd + 1)
                V.tensor_tensor(xlo[:, hd, :], ps[:, hd % 3, 0:SEQ], xhi[:, hd, :].bitcast(F32), ALU.subtract).then_inc(o_lo, 1)

            def normalise(hd):
                dve.wait_ge(exp_done, 2 * hd + 2)
                step(V.reciprocal(rr[:, hd, :], rs[:, hd, :]))
                for c, (a, b) in enumerate(((0, 128), (128, 384))):
                    V.tensor_scalar(prob[:, hd % 2, a:b], prob[:, hd % 2, a:b], rr[:, hd, c:c + 1], None, ALU.mult).then_inc(pn_ready, 1)

            mla_max(0)
            mla_max(1)
            normalise(0)
            for hd in range(HEADS):
                if hd + 2 < HEADS:
                    mla_max(hd + 2)
                if hd + 1 < HEADS:
                    normalise(hd + 1)
                mla_low(hd)
                split_low(22 + hd)
            split_low(30)

            def residual(ready, bank):
                for n in range(2):
                    for c in range(TC):
                        hv = h[:, c, n * 512:(n + 1) * 512]
                        V.tensor_tensor(hv, ps[:, bank(c, n), :], hv, ALU.add).then_inc(ready, 1)

            dve.wait_ge(used, H_FFN)
            residual(h_ready[1], lambda c, n: 4 + 2 * c + n)

            def ffn(x, i=0):
                n, nt, base = FFN[x]

                def gate(j):
                    for c in range(nt):
                        dve.wait_ge(silu_done[x], (i * n + j) * nt + c + 1)
                        g = gu[:, j % 2, c, :]
                        up = ps[:, bank_gu(x, c, parity(x, j)), GW:2 * GW]
                        if x == 2:
                            V.tensor_tensor(g, up, g, ALU.mult).then_inc(gated[x], 1)
                        else:
                            V.scalar_tensor_tensor(out=g, in0=up, scalar=rstd[:, 1, c:c + 1], in1=g,
                                                   op0=ALU.mult, op1=ALU.mult).then_inc(gated[x], 1)

                def low(j):
                    dve.wait_ge(h_hi[x], i * n + j + 1)
                    src = ps[:, bank_tr(x, j % 2), 0:2 * nt * P]
                    hi = ehi[:, 2 * j:2 * j + 2, :] if nt == 1 else hhi[:, 2 * j:2 * j + 2, :]
                    lo = elo[:, 2 * j:2 * j + 2, :] if nt == 1 else hlo[:, 2 * j:2 * j + 2, :]
                    V.tensor_tensor(lo.rearrange("p a s -> p (a s)"), src, hi.bitcast(F32).rearrange("p a s -> p (a s)"),
                                    ALU.subtract).then_inc(h_lo[x], 1)

                for j in range(first_group(x), n):
                    if j >= 1:
                        gate(j - 1)
                    if j >= 2:
                        low(j - 2)
                    for m in range(0, 4, 2):
                        split_low_unit(base + RING + 4 * j + m, i)
                    if x == 2 and j == 4:
                        V.tensor_copy(gt[:, :], g_tab[:, bass.ds(i, 1), :].rearrange("p a c -> p (a c)")).then_inc(gt_ready, 1)
                        V.tensor_copy(pm[:, :, :], pm_tab[:, bass.ds(i + 1, 1), :, :].rearrange("p a b c -> p (a b) c")).then_inc(pm_ready, 1)
                        dve.wait_ge(pm_ready, i + 1)
                        dve.wait_ge(sel_tr, i + 1)
                        for c in range(TC):
                            V.tensor_scalar(sel[:, c, :], iota[:, :], pm[:, 0, c:c + 1], pm[:, 1, c:c + 1],
                                            ALU.is_equal, ALU.mult).then_inc(sel_ready, 1)
                gate(n - 1)
                low(n - 2)
                for f in range(2 * n):
                    if f == 2 * n - 1 and x == 2:
                        for m in range(2):
                            dve.wait_ge(y_hi, i * 2 + m + 1)
                            V.tensor_tensor(xlo[:, 4 * m:4 * m + 4, P:SEQ], ps[:, 4 + m, :].rearrange("p (a s) -> p a s", a=4),
                                            xhi[:, 4 * m:4 * m + 4, P:SEQ].bitcast(F32), ALU.subtract).then_inc(y_lo, 1)
                    if x != 1 or f < 2 * n - 1:
                        split_low(base + RING + 4 * n + f, i)
                    if f == LAST_TR:
                        low(n - 1)
                    if f == 17 and x == 2:
                        gathered_low(i + 1)

            def gathered_low(item):
                for b in range(2):
                    dve.wait_ge(xe_hi, item * KD + 4 * b + 4)
                    for k in range(4 * b, 4 * b + 4):
                        V.scalar_tensor_tensor(out=xlo[:, k, 0:P], in0=ps[:, 6 + b, (k % 4) * P:(k % 4 + 1) * P],
                                               scalar=gcol[:, G_FFN1 + k:G_FFN1 + k + 1], in1=xhi[:, k, 0:P].bitcast(F32),
                                               op0=ALU.mult, op1=ALU.subtract).then_inc(xe_lo, 1)

            x_low(1, G_FFN0)
            split_low(31)
            squares(1, 1, xm[:, 1, :])
            dve.wait_ge(rstd_ready[1], 1)
            for x in range(2):
                ffn(x)
                dve.wait_ge(used, FFN[x][2] + 6 * FFN[x][0])
                residual(h_ready[2], lambda c, n: bank_out(x, c, n))

            def evacuate(dst, bank0, ready, scale):
                for b in range(4):
                    V.scalar_tensor_tensor(out=dst[:, 2 * b:2 * b + 2, :], in0=ps[:, bank0 + b, :].rearrange("p (a s) -> p a s", a=2),
                                           scalar=scale, in1=rb[:, :].unsqueeze(1).to_broadcast([P, 2, SEQ]),
                                           op0=ALU.mult, op1=ALU.mult).then_inc(ready, 1)

            def softplus(g):
                dve.wait_ge(ln_done, g + 1)
                V.scalar_tensor_tensor(out=sp[:, 4 * g:4 * g + 4, :], in0=ps[:, 4 * g:4 * g + 4, 0:384], scalar=0.0,
                                       in1=sp[:, 4 * g:4 * g + 4, :], op0=ALU.max, op1=ALU.add).then_inc(sp_ready, 1)

            def heads_low(g):
                for hd in range(4 * g, 4 * g + 4):
                    dve.wait_ge(so_hi, hd + 1)
                    V.tensor_tensor(xlo[:, hd, :], ps[:, hd, 0:SEQ], xhi[:, hd, :].bitcast(F32), ALU.subtract).then_inc(so_lo, 1)

            x_low(2)
            split_low(H_SBK + RING - 1)
            squares(2, 1, sp[:, :, :].rearrange("p a s -> p (a s)")[:, D:2 * D])
            for m in range(8):
                if m == 1:
                    dve.wait_ge(rstd_ready[2], 1)
                    row_factors(1, lambda c: rstd[:, 2, c:c + 1])
                split_low(H_SBK + RING + m)
            dve.wait_ge(rb_ready, 2)
            dve.wait_ge(used, H_SBQ)
            evacuate(skT, 4, skT_ready, 1.0)
            for m in range(8):
                split_low(H_SBQ + RING + m)
            dve.wait_ge(used, H_SBV)
            evacuate(sqT, 0, sqT_ready, SB_SCALE)
            for m in range(4):
                split_low(H_SBV + RING + m)
            softplus(0)
            for m in range(4, 7):
                split_low(H_SBV + RING + m)
            dve.wait_ge(used, H_SBO)
            for n in range(2):
                V.tensor_scalar(sv[:, 1, n * 512:(n + 1) * 512], ps[:, 6 + n, :], rstd[:, 2, 1:2], None, ALU.mult).then_inc(sv_ready[1], 1)
            split_low(H_SBV + RING + 7)
            step(V.tensor_tensor(router[:, :, :], router[:, :, :],
                                 gcol[:, G_FFN1:G_FFN1 + KD].unsqueeze(2).to_broadcast([P, KD, N_EXP]), ALU.mult))
            heads_low(0)
            softplus(1)
            for m in range(4):
                split_low(H_SBO + RING + m)
            heads_low(1)
            step(V.tensor_scalar(rank[:, :], iota[:, 0:N_EXP], -1.0, float(N_EXP), ALU.mult, ALU.add))
            for m in range(4, 7):
                split_low(H_SBO + RING + m)
            dve.wait_ge(used, H_MOE)
            residual(h_ready[3], lambda c, n: 2 * c + n)

            dve.wait_ge(x_tr[3], 4)
            V.tensor_copy(xr[:, 6:8, :], ps[:, X_BANKS[3][3], :].rearrange("p (a s) -> p a s", a=2)).then_inc(xlo_ready[3], 1)
            squares(3, 1, xm[:, 1, :])
            dve.wait_ge(rstd_ready[3], 1)
            dve.wait_ge(ss_ready[3], 2)
            V.tensor_scalar(xm[:, 0, :], h[:, 0, :], rstd[:, 3, 0:1], None, ALU.mult).then_inc(xm_ready, 1)
            dve.wait_ge(lg_done, 1)
            step(V.tensor_copy(lg[:, :, :].rearrange("p c e -> p (c e)"), ps[:, 5, 0:TC * N_EXP]))

            def per_token(a):
                return a.unsqueeze(2).to_broadcast([P, TC, N_EXP])

            rank_b = rank[:, :].unsqueeze(1).to_broadcast([P, TC, N_EXP])

            def pick(logits, largest, chosen):
                step(V.tensor_reduce(largest, logits, AX, ALU.max))
                step(V.tensor_tensor(sc8[:, :, :], logits, per_token(largest), ALU.is_equal))
                step(V.tensor_tensor(sc8[:, :, :], sc8[:, :, :], rank_b, ALU.mult))
                step(V.tensor_reduce(best[:, :], sc8[:, :, :], AX, ALU.max))
                step(V.tensor_tensor(chosen, sc8[:, :, :], per_token(best[:, :]), ALU.is_equal))

            pick(lg[:, :, :], m1[:, :], oh1[:, :, :])
            step(V.scalar_tensor_tensor(out=lg2[:, :, :], in0=oh1[:, :, :], scalar=NEG, in1=lg[:, :, :],
                                        op0=ALU.mult, op1=ALU.add))
            pick(lg2[:, :, :], m2[:, :], oh2[:, :, :])
            V.tensor_tensor(msk[:, :, :], oh1[:, :, :], oh2[:, :, :], ALU.add).then_inc(msk_ready, 1)
            step(V.tensor_tensor(best[:, :], m2[:, :], m1[:, :], ALU.subtract))
            V.tensor_tensor(best[:, :], best[:, :], rstd[:, 3, :], ALU.mult).then_inc(gap_ready, 1)
            dve.wait_ge(pos_done, 1)
            step(V.tensor_copy(posn[:, :, :].rearrange("p c e -> p (c e)"), ps[:, 5, 16:32]))
            for c in range(TC):
                V.tensor_scalar(sel[:, c, :], iota[:, :], posn[:, c, 0:1], msk[:, c, 0:1],
                                ALU.is_equal, ALU.mult).then_inc(sel_ready, 1)
            step(V.tensor_copy(cnt[:, :], ps[:, 5, 32:40]))
            step(V.tensor_scalar(ovf[:, :], cnt[:, :], float(P), None, ALU.is_gt))
            step(V.tensor_tensor_scan(csum[:, :], ones[:, 0:N_EXP], ovf[:, :], 0.0, ALU.mult, ALU.add))
            for r in range(3):
                last = V.tensor_scalar(selr[:, r, :], csum[:, :], float(r + 1), None, ALU.is_equal)
            step(last)
            step(V.tensor_tensor(selr[:, :, :], selr[:, :, :], ovf[:, :].unsqueeze(1).to_broadcast([P, 3, N_EXP]), ALU.mult))
            step(V.tensor_copy(tf[:, :], iota[:, 0:ITEMS]))
            step(V.memset(tf[:, N_EXP:ITEMS], 0.0))
            step(V.tensor_tensor(prod[:, :, :], selr[:, :, :], iota[:, 0:N_EXP].unsqueeze(1).to_broadcast([P, 3, N_EXP]), ALU.mult))
            step(V.tensor_reduce(tf[:, N_EXP:N_EXP + 3], prod[:, :, :], AX, ALU.add))
            V.tensor_copy(item_expert[:, :], tf[:, :]).then_inc(items_ready, 1)
            V.tensor_scalar(n_items_i[:, :], csum[:, N_EXP - 1:N_EXP], float(N_EXP), None, ALU.add).then_inc(items_ready, 1)
            gathered_low(0)
            split_low(H_SBO + RING + 7)
            dve.wait_ge(gap_exp, 1)
            step(V.tensor_scalar(m1[:, :], den[:, :], 1.0, None, ALU.add))
            step(V.reciprocal(m1[:, :], m1[:, :]))
            step(V.tensor_tensor(m2[:, :], den[:, :], m1[:, :], ALU.mult))
            step(V.tensor_tensor(oh1[:, :, :], oh1[:, :, :], per_token(m1[:, :]), ALU.mult))
            step(V.tensor_tensor(oh2[:, :, :], oh2[:, :, :], per_token(m2[:, :]), ALU.mult))
            step(V.tensor_tensor(gates[:, :, :], oh1[:, :, :], oh2[:, :, :], ALU.add))
            for c in range(TC):
                V.tensor_copy(pm_tab[:, 0:N_EXP, 0, c], posn[:, c, :])
                V.tensor_copy(pm_tab[:, 0:N_EXP, 1, c], msk[:, c, :])
                V.tensor_copy(g_tab[:, 0:N_EXP, c], gates[:, c, :])
            V.memset(pm_tab[:, N_EXP:ITEMS, :, :], 0.0).then_inc(h_ready[4], 4)
            step(V.memset(g_tab[:, N_EXP:ITEMS, :], 0.0))
            for c in range(TC):
                for src, dst in ((posn, pm_tab[:, N_EXP:N_EXP + 3, 0, c]), (msk, pm_tab[:, N_EXP:N_EXP + 3, 1, c]),
                                 (gates, g_tab[:, N_EXP:N_EXP + 3, c])):
                    step(V.tensor_tensor(prod[:, :, :], selr[:, :, :], src[:, c, :].unsqueeze(1).to_broadcast([P, 3, N_EXP]), ALU.mult))
                    step(V.tensor_reduce(dst, prod[:, :, :], AX, ALU.add))
                step(V.tensor_scalar(pm_tab[:, N_EXP:N_EXP + 3, 0, c], pm_tab[:, N_EXP:N_EXP + 3, 0, c], -float(P), None, ALU.add))
            for m in range(0, 4, 2):
                split_low_unit(H_MOE + RING + m)
            dve.wait_ge(items_ready, 2)
            n_items = dve.value_load(n_items_i[0:1, 0:1], min_val=N_EXP, max_val=ITEMS - 1)
            with dve.Fori(0, n_items) as i:
                ffn(2, i)
                for m in range(2):
                    split_low(H_MOE + RING + m, i + 1)
                dve.wait_ge(gt_ready, i + 1)
                for c in range(TC):
                    for n in range(2):
                        dve.wait_ge(scattered, i * 4 + 2 * c + n + 1)
                        hv = h[:, c, n * 512:(n + 1) * 512]
                        V.scalar_tensor_tensor(out=hv, in0=ps[:, 2 + 2 * c + n, :], scalar=gt[:, c:c + 1], in1=hv,
                                               op0=ALU.mult, op1=ALU.add).then_inc(h_ready[4], 1)
                for m in range(2, 4):
                    split_low(H_MOE + RING + m, i + 1)

            dve.wait_ge(gbc_in, 16)
            dve.wait_ge(h_ready[4], n_items * 4 + 4)
            for c in range(TC):
                V.tensor_tensor(yg[:, c, :], h[:, c, :], gbc, ALU.mult).then_inc(yg_ready, 1)
            dve.wait_ge(yg_ready, 2)
            dve.wait_ge(rstd_ready[4], 1)
            V.tensor_scalar(yout[:, 1, :], yg[:, 1, :], rstd[:, 4, 1:2], None, ALU.mult).then_inc(y_ready[1], 1)

        @block.tensor
        def _(pe):
            def mm3(o, a_hi, a_lo, b_hi, b_lo, start, stop):
                pe.matmul(o, a_hi, b_hi, start=start, stop=False, skip_group_check=True)
                pe.matmul(o, a_lo, b_hi, start=False, stop=False, skip_group_check=True)
                return pe.matmul(o, a_hi, b_lo, start=False, stop=stop, skip_group_check=True)

            def mm(o, a, b, start, stop):
                return pe.matmul(o, a, b, start=start, stop=stop, skip_group_check=True)

            def transpose_x(n, first, second):
                for b in range(4):
                    if b % 2 == 0:
                        pe.wait_ge(*(second if b else first))
                    for k in (2 * b, 2 * b + 1):
                        for c in range(TC):
                            last = pe.transpose(ps[:, X_BANKS[n][b], (k % 2) * SEQ + c * P:(k % 2) * SEQ + (c + 1) * P],
                                                h[:, c, k * P:(k + 1) * P], ident[:, :])
                    last.then_inc(x_tr[n], 1)

            def tokens_out(k, hh, banks, width=512):
                for c in range(TC):
                    for n in range(2):
                        w = slice(n * 512, (n + 1) * 512)
                        last = mm3(ps[:, banks[c][n], :], xhi[:, k, c * P:(c + 1) * P], xlo[:, k, c * P:(c + 1) * P],
                                   w_hi(hh)[:, w], w_lo(hh)[:, w], k == 0, k == KD - 1)
                last.then_inc(used, 1)

            def features_out(k, hh, bank0):
                for hd in range(HEADS):
                    w = slice(hd * P, (hd + 1) * P)
                    last = mm3(ps[:, bank0 + hd // 2, (hd % 2) * SEQ:(hd % 2 + 1) * SEQ], w_hi(hh)[:, w], w_lo(hh)[:, w],
                               xhi[:, k, :], xlo[:, k, :], k == 0 and hd % 2 == 0, k == KD - 1)
                last.then_inc(used, 1)

            pe.wait_ge(ident_ready, 1)
            transpose_x(0, (x_in[0], 16), (x_in[1], 16))
            pe.wait_ge(gain0_in, 16)
            pe.transpose(ps[:, 7, 0:KD], grow[0:KD, :], ident[0:KD, 0:KD]).then_inc(g_tr, 1)
            pe.wait_ge(g_ready, 1)
            for k in range(KD):
                pe.wait_ge(xlo_ready[0], k + 1)
                if k == 2:
                    pe.wait_ge(small_in, 16 * 6)
                    pe.transpose(ps[:, 0, 0:G_ALL], grow[0:G_ALL, :], ident[0:G_ALL, 0:G_ALL]).then_inc(g_tr, 1)
                pe.wait_ge(lo_made, H_DOWN + k + 1)
                for c in range(TC):
                    for n, (a, b) in enumerate(((0, Q_LORA), (Q_LORA, DOWN))):
                        last = mm3(ps[:, 4 + 2 * c + n, 0:b - a], xhi[:, k, c * P:(c + 1) * P], xlo[:, k, c * P:(c + 1) * P],
                                   w_hi(H_DOWN + k)[:, a:b], w_lo(H_DOWN + k)[:, a:b], k == 0, k == KD - 1)
                last.then_inc(used, 1)
            pe.wait_ge(g_ready, 2)
            pe.wait_ge(cq_ready, 2)
            for j in range(CC):
                if j == 3:
                    pe.wait_ge(ckv_ready, 2)
                for c in range(TC):
                    o = (j % 2) * SEQ + c * P
                    last = pe.transpose(ps[:, j // 2, o:o + P], cn[:, c, j * P:(j + 1) * P], ident[:, :])
                if j % 2 or j == CC - 1:
                    last.then_inc(c_tr, 1)

            def query_features(g):
                for hd in range(4 * g, 4 * g + 4):
                    for k in range(3):
                        hh = H_UQ + 3 * g + k
                        w = slice((hd % 4) * QH, (hd % 4) * QH + P)
                        last = mm3(ps[:, hd // 2, (hd % 2) * SEQ:(hd % 2 + 1) * SEQ], w_hi(hh)[:, w], w_lo(hh)[:, w],
                                   chi[:, k, :], clo[:, k, :], k == 0 and hd % 2 == 0, k == 2)
                    if hd % 2 and hd < HEADS - 1:
                        last.then_inc(qn_done, 1)
                return last

            def query_rotary(g):
                for c in range(TC):
                    for k in range(3):
                        hh = H_UQ + 3 * g + k
                        r_hi, r_lo = (f(hh)[:, 0:4 * QH].rearrange("p (a r) -> p a r", r=QH)[:, :, P:QH] for f in (w_hi, w_lo))
                        last = mm3(ps[:, 4 + g, c * SEQ:(c + 1) * SEQ].rearrange("p (a r) -> p a r", r=ROPE),
                                   chi[:, k, c * P:(c + 1) * P], clo[:, k, c * P:(c + 1) * P], r_hi, r_lo,
                                   k == 0 and c == 0, k == 2)
                last.then_inc(rot_done, 1)

            pe.wait_ge(clo_ready, 2)
            pe.wait_ge(lo_made, H_UQ + 3)
            query_rotary(0)
            query_features(0)
            pe.wait_ge(kr_ready, 1)
            pe.transpose(ps[:, 7, 0:P], kr[:, 0, :], ident[:, :]).then_inc(used, 3)
            pe.transpose(ps[:, 7, P:2 * P], kr[:, 1, :], ident[:, :]).then_inc(kr_tr, 1)
            pe.wait_ge(clo_ready, 3)
            pe.wait_ge(lo_made, H_UQ + 6)
            query_rotary(1)
            query_features(1).then_inc(used, 3)
            pe.wait_ge(rb_diag, 2)
            for c in range(TC):
                last = mm(ps[:, 6, c * P:(c + 1) * P], ones[:, :], diag[:, c, :], c == 0, c == TC - 1)
            last.then_inc(rb_mm, 1)
            for hd in range(HEADS):
                if hd % 4 == 0:
                    pe.wait_ge(lo_made, H_UKV + hd // 2 + 2)
                if hd % 2 == 0:
                    pe.wait_ge(qT_ready, hd // 2 + 1)
                for k in range(2):
                    hh = H_UKV + 2 * (hd // 4) + k
                    w = slice((hd % 4) * 2 * P, (hd % 4) * 2 * P + P)
                    last = mm3(ps[:, hd // 2, (hd % 2) * SEQ:(hd % 2 + 1) * SEQ], w_hi(hh)[:, w], w_lo(hh)[:, w],
                               chi[:, 3 + k, :], clo[:, 3 + k, :], k == 0 and hd % 2 == 0, k == 1)
                if hd % 2:
                    last.then_inc(kn_done, 1)
            pe.wait_ge(rot_ready, 4)
            pe.wait_ge(rb_ready, 1)
            pe.wait_ge(krT_ready, 1)
            for b in range(2):
                for pair in (2 * b, 2 * b + 1):
                    for c in range(TC):
                        last = pe.transpose(ps[:, 6 + b, (pair % 2) * SEQ + c * P:(pair % 2) * SEQ + (c + 1) * P],
                                            rot[:, c, 2 * pair:2 * pair + 2, :].rearrange("p a r -> p (a r)"), ident[:, :])
                last.then_inc(rot_tr, 1)
            for g in range(2):
                if g == 1:
                    pe.wait_ge(qrT_ready, 2)
                for c in range(TC):
                    for k in range(2):
                        hh = H_UKV + 2 * g + k
                        v_hi, v_lo = (f(hh).rearrange("p (a r) -> p a r", r=2 * P)[:, :, P:2 * P] for f in (w_hi, w_lo))
                        last = mm3(ps[:, 4 + c + 2 * g, :].rearrange("p (a r) -> p a r", r=P),
                                   chi[:, 3 + k, c * P:(c + 1) * P], clo[:, 3 + k, c * P:(c + 1) * P], v_hi, v_lo,
                                   k == 0, k == 1)
                last.then_inc(used, 2)

            def scores(hd):
                b = hd % 3
                if hd >= 3:
                    pe.wait_ge(o_lo, hd - 2)
                lo = (hd % 2) * ROPE
                for c, (a, e) in enumerate(((0, 128), (128, 384))):
                    mm(ps[:, b, a:e], qT[:, hd, c * P:(c + 1) * P], kT[:, hd, 0:e - a], c == 0, False)
                for c, (a, e) in enumerate(((0, 128), (128, 384))):
                    mm(ps[:, b, a:e], qrT[lo:lo + ROPE, hd // 2, c * P:(c + 1) * P], krT[lo:lo + ROPE, 0:e - a], False, False)
                for a in (CHUNK, 128 + 192):
                    last = mm(ps[:, b, a:a + CHUNK], half_mask[0:1, 0:P], half_mask[0:1, P:P + CHUNK], False, True)
                last.then_inc(s_done, 1)

            def outputs(hd):
                pe.wait_ge(probT_ready, hd + 1)
                o = ps[:, hd % 3, :]
                mm(o[:, 0:SEQ], v[:, 0, hd * P:(hd + 1) * P], probT[:, hd % 2, 0:SEQ], True, False)
                mm(o[:, P:SEQ], v[:, 1, hd * P:(hd + 1) * P], probT[:, hd % 2, SEQ:384], False, True).then_inc(o_done, 1)

            pe.wait_ge(qrT_ready, 2)
            pe.wait_ge(kT_ready, 4)
            scores(0)
            scores(1)
            for c in range(TC):
                pe.wait_ge(v_ready[c], 2)
            for hd in range(HEADS):
                pe.wait_ge(pn_ready, 2 * hd + 2)
                if hd >= 1:
                    pe.wait_ge(probT_ready, hd)
                for n in range(3):
                    last = pe.transpose(ps[:, 3, n * P:(n + 1) * P], prob[:, hd % 2, n * P:(n + 1) * P], ident[:, :])
                last.then_inc(pt_done, 1)
                if hd + 2 < HEADS:
                    scores(hd + 2)
                outputs(hd)
                if hd >= 1:
                    pe.wait_ge(o_lo, hd)
                    pe.wait_ge(lo_made, H_WO + hd)
                    tokens_out(hd - 1, H_WO + hd - 1, ((4, 5), (6, 7)))
            pe.wait_ge(o_lo, HEADS)
            pe.wait_ge(lo_made, H_WO + HEADS)
            tokens_out(HEADS - 1, H_WO + HEADS - 1, ((4, 5), (6, 7)))

            def products(x, j, i=0):
                n, nt, base = FFN[x]
                if j >= 2:
                    pe.wait_ge(gated[x], (i * n + j - 1) * nt)
                for m in range(4):
                    hh = base + 4 * j + m
                    pe.wait_ge(lo_made, i * FH + hh + 1)
                    if j == 0:
                        if x == 0:
                            pe.wait_ge(xlo_ready[1], 2 * m + 2)
                        elif x == 2:
                            pe.wait_ge(xe_lo, i * KD + 2 * m + 2)
                    for c in range(nt):
                        for kk in range(2):
                            k = 2 * m + kk
                            w = slice(kk * 512, (kk + 1) * 512)
                            last = mm3(ps[:, bank_gu(x, c, parity(x, j)), :],
                                       xhi[:, k, c * P:(c + 1) * P], xlo[:, k, c * P:(c + 1) * P],
                                       w_hi(hh)[:, w], w_lo(hh)[:, w], k == 0, k == KD - 1)
                    last.then_inc(used, 1)

            def ffn(x, i=0):
                n, nt, base = FFN[x]

                def transposes(j):
                    pe.wait_ge(gated[x], (i * n + j + 1) * nt)
                    if j >= 2:
                        pe.wait_ge(h_lo[x], i * n + j - 1)
                    for b in range(2):
                        for c in range(nt):
                            o = (b * nt + c) * P
                            last = pe.transpose(ps[:, bank_tr(x, j % 2), o:o + P], gu[:, j % 2, c, b * P:(b + 1) * P], ident[:, :])
                    last.then_inc(gu_tr[x], 1)

                for j in range(first_group(x), n):
                    if x == 1 and j == 1:
                        pe.wait_ge(h_ready[2], 4)
                    products(x, j, i)
                    if j == 1 and x == 2:
                        pe.wait_ge(h_ready[4], i * 4 + 4)
                    if j >= 1:
                        transposes(j - 1)
                hi, lo = (ehi, elo) if nt == 1 else (hhi, hlo)
                for f in range(2 * n):
                    hh = base + 4 * n + f
                    pe.wait_ge(lo_made, i * FH + hh + 1)
                    if f % 2 == 0:
                        pe.wait_ge(h_lo[x], i * n + f // 2 + 1)
                    for c in range(nt):
                        for m in range(2):
                            w = slice(m * 512, (m + 1) * 512)
                            last = mm3(ps[:, bank_out(x, c, m), :], hi[:, f, c * P:(c + 1) * P], lo[:, f, c * P:(c + 1) * P],
                                       w_hi(hh)[:, w], w_lo(hh)[:, w], f == 0, f == 2 * n - 1)
                    last.then_inc(used, 1)
                    if f == LAST_TR:
                        transposes(n - 1)
                    if f == 11 and x == 2:
                        gather(i + 1)

            def gather(item):
                pe.wait_ge(sel_ready, item * 2 + 2)
                if not isinstance(item, int):
                    pe.wait_ge(selT_ready, item)
                for k in range(KD):
                    o = ps[:, 6 + k // 4, (k % 4) * P:(k % 4 + 1) * P]
                    for c in range(TC):
                        last = mm(o, xm[:, c, k * P:(k + 1) * P], sel[:, c, :], c == 0 and k % 4 == 0, c == TC - 1)
                    if k % 4 == 3:
                        last.then_inc(gathered, 1)

            def transpose_sel(item):
                pe.wait_ge(xe_lo, item * KD + KD)
                for c in range(TC):
                    last = pe.transpose(ps[:, 6, c * P:(c + 1) * P], sel[:, c, :], ident[:, :])
                last.then_inc(sel_tr, 1)

            transpose_x(1, (h_ready[1], 2), (h_ready[1], 4))
            ffn(0)
            ffn(1)

            def logits(g):
                for hd in range(4 * g, 4 * g + 4):
                    z = ps[:, hd, :]
                    mm(z[:, 0:SEQ], skT[:, hd, 0:P], sqT[:, hd, :], True, False)
                    mm(z[:, SEQ:384], skT[:, hd, P:SEQ], sqT[:, hd, P:SEQ], False, False)
                    mm(z[:, 0:P], ident_r[:, :], hide_r[:, :], False, False)
                    mm(z[:, SEQ:384], ident_r[:, :], hide_r[:, :], False, True).then_inc(z_done, 1)

            def suffix_sums(g):
                pe.wait_ge(sp_ready, g + 1)
                for hd in range(4 * g, 4 * g + 4):
                    z, s = ps[:, hd, :], sp[:, hd, :]
                    mm(z[:, 0:SEQ], neg_from[:, :], s[:, 0:SEQ], False, False)
                    mm(z[:, SEQ:384], neg_from[:, :], s[:, SEQ:384], False, False)
                    mm(z[:, P:SEQ], neg_ones[:, :], s[:, SEQ:384], False, True).then_inc(c_done, 1)

            def sb_outputs(g):
                for hd in range(4 * g, 4 * g + 4):
                    pe.wait_ge(a_ready, hd + 1)
                    o = ps[:, hd, :]
                    mm(o[:, 0:SEQ], sv[:, 0, hd * P:(hd + 1) * P], sp[:, hd, 0:SEQ], True, False)
                    mm(o[:, P:SEQ], sv[:, 1, hd * P:(hd + 1) * P], sp[:, hd, SEQ:384], False, True).then_inc(so_done, 1)

            transpose_x(2, (h_ready[2], 6), (h_ready[2], 8))
            for k in range(KD):
                pe.wait_ge(xlo_ready[2], k + 1)
                if k == 5:
                    pe.wait_ge(rb_diag, 4)
                    for c in range(TC):
                        last = mm(ps[:, 0, c * P:(c + 1) * P], ones[:, :], sp[:, c, 0:P], c == 0, c == TC - 1)
                    last.then_inc(rb_mm, 1)
                pe.wait_ge(lo_made, H_SBK + k + 1)
                features_out(k, H_SBK + k, 4)
            pe.wait_ge(rb_ready, 2)
            for k in range(KD):
                pe.wait_ge(lo_made, H_SBQ + k + 1)
                features_out(k, H_SBQ + k, 0)
            pe.wait_ge(skT_ready, 4)
            for k in range(KD):
                if k == 2:
                    pe.wait_ge(sqT_ready, 4)
                    logits(0)
                if k == 7:
                    suffix_sums(0)
                pe.wait_ge(lo_made, H_SBV + k + 1)
                tokens_out(k, H_SBV + k, ((4, 5), (6, 7)))
            pe.wait_ge(sv_ready[0], 2)
            pe.wait_ge(sv_ready[1], 2)
            logits(1)
            sb_outputs(0)
            for g in range(2):
                pe.wait_ge(so_lo, 4 * g + 4)
                for k in range(4 * g, 4 * g + 4):
                    pe.wait_ge(lo_made, H_SBO + k + 1)
                    tokens_out(k, H_SBO + k, ((0, 1), (2, 3)))
                if g == 0:
                    suffix_sums(1)
                    sb_outputs(1)

            transpose_x(3, (h_ready[3], 2), (h_ready[3], 4))
            for k in range(KD):
                if k < 6:
                    pe.wait_ge(xhi_ready[3], k // 2 + 1)
                else:
                    pe.wait_ge(xlo_ready[3], 1)
                for c in range(TC):
                    last = mm(ps[:, 5, c * N_EXP:(c + 1) * N_EXP], xr[:, k, c * P:(c + 1) * P], router[:, k, :],
                              k == 0 and c == 0, k == KD - 1)
            last.then_inc(lg_done, 1)
            pe.wait_ge(msk_ready, 1)
            mm(ps[:, 5, 16:24], before[:, :], msk[:, 0, :], False, True)
            mm(ps[:, 5, 24:32], ones[:, :], msk[:, 0, :], False, False)
            mm(ps[:, 5, 24:32], before[:, :], msk[:, 1, :], False, True)
            mm(ps[:, 5, 32:40], ones[:, :], msk[:, 0, :], False, False)
            mm(ps[:, 5, 32:40], ones[:, :], msk[:, 1, :], False, True).then_inc(pos_done, 1)

            pe.wait_ge(xm_ready, 2)
            gather(0)
            products(2, 0)
            transpose_sel(0)
            pe.wait_ge(items_ready, 2)
            n_items = pe.value_load(n_items_i[0:1, 0:1], min_val=N_EXP, max_val=ITEMS - 1)
            with pe.Fori(0, n_items) as i:
                ffn(2, i)
                products(2, 0, i + 1)
                pe.wait_ge(y_lo, i * 2 + 2)
                pe.wait_ge(selT_ready, i + 1)
                for c in range(TC):
                    for n in range(2):
                        o = ps[:, 2 + 2 * c + n, :].rearrange("p (a s) -> p a s", a=4)
                        w = selT[:, c * P:(c + 1) * P]
                        mm(o, w, xhi[:, 4 * n:4 * n + 4, P:SEQ], True, False)
                        mm(o, w, xlo[:, 4 * n:4 * n + 4, P:SEQ], False, True).then_inc(scattered, 1)
                transpose_sel(i + 1)


INPUTS = ["x", "positions", "attn_norm_0", "mla_w_down_0", "mla_q_norm_0", "mla_w_uq_0", "mla_kv_norm_0",
          "mla_w_ukv_0", "mla_w_o_0", "ffn_norm_0", "ffn_w_gate_up_0", "ffn_w_down_0", "attn_norm_1",
          "ffn_norm_1", "moe_router_1", "moe_w_gate_up_1", "moe_w_down_1", "kv_shared_norm", "kv_shared_w",
          "sb_w_q_2", "sb_w_o_2", "final_norm"]


def kernel(**inputs):
    import concourse.bacc as bacc
    from concourse.bass_utils import run_bass_kernel_spmd as run

    nc = bacc.Bacc("TRN2", target_bir_lowering=False, num_devices=1)
    arrays, t = {}, {}
    for name in INPUTS:
        a = np.ascontiguousarray(inputs[name])
        arrays[f"{name}_dram"] = a
        t[name] = nc.dram_tensor(f"{name}_dram", a.shape, mybir.dt.from_np(a.dtype), kind="ExternalInput").ap()
    out = nc.dram_tensor("out_dram", (1, SEQ, D), F32, kind="ExternalOutput").ap()
    build(nc, t, out)
    r = run(nc, [arrays], core_ids=[0])
    return r.results[0]["out_dram"]
```
